# Optimizing a Trainium2 kernel written in Bass

```python
import math
import jax, jax.numpy as jnp
from jax import lax
import numpy as np

D_MODEL = 1024
BATCH = 1
SEQ = 512
DEPTH = 2

PLE_DIM = 256
RET_HEADS = 4
RET_DK = 128
RET_DV = 128
RET_CHUNK = 128
POOL_WINDOWS = (2, 4, 8, 16)
POOL_GROUP = 128
POOL_WIDTH = len(POOL_WINDOWS) * POOL_GROUP
AB_IN = RET_HEADS * (2 * RET_DK + 2 * RET_DV) + POOL_WIDTH
AB_MIX = RET_HEADS * RET_DV + POOL_WIDTH
C_HEADS = 16
C_HEAD_DIM = 64
C_Q_RANK = 256
C_KV_RANK = 256
IDX_HEADS = 8
IDX_DIM = 64
IDX_TOPK_MAX = 256
Q_BLOCK = 128
C_IN = C_Q_RANK + C_KV_RANK + IDX_HEADS * IDX_DIM + IDX_DIM + IDX_HEADS
N_GROUPS = 4
EXPERTS_PER_GROUP = 8
N_EXPERTS = N_GROUPS * EXPERTS_PER_GROUP
TOPK_IN_GROUP = 2
EXPERT_FF = 512
MOE_BLOCK = 128
ALPHA = (2.0 * DEPTH) ** 0.25
BETA = (8.0 * DEPTH) ** -0.25
LN_EPS = 1e-5
N_EVEN = (DEPTH + 1) // 2
N_ODD = DEPTH // 2

kernel_name = "hybrid_retention_pool_dsa_hmoe"

def layer_norm(x, g, b):
    xf = x.astype(jnp.float32)
    mu = xf.mean(-1, keepdims=True)
    var = jnp.square(xf - mu).mean(-1, keepdims=True)
    return ((xf - mu) * lax.rsqrt(var + LN_EPS) * g + b).astype(x.dtype)

def rms_norm(x, g):
    xf = x.astype(jnp.float32)
    return (xf * lax.rsqrt(jnp.mean(xf * xf, -1, keepdims=True) + 1e-6) * g).astype(x.dtype)

def retention_chunkwise(q, k, v):
    B, T, H, dk = q.shape
    dv = v.shape[-1]
    C = RET_CHUNK
    N = T // C
    log_g = jnp.log1p(-jnp.exp2(-5.0 - jnp.arange(H, dtype=jnp.float32)))
    i = jnp.arange(C, dtype=jnp.float32)
    diff = i[:, None] - i[None, :]
    inner_decay = jnp.where(diff >= 0, jnp.exp(log_g[:, None, None] * jnp.maximum(diff, 0.0)), 0.0)
    q_decay = jnp.exp(log_g[:, None] * (i + 1.0))
    k_decay = jnp.exp(log_g[:, None] * (C - 1.0 - i))
    chunk_decay = jnp.exp(log_g * C)

    def to_chunks(a):
        return a.astype(jnp.float32).reshape(B, N, C, H, a.shape[-1]).transpose(1, 0, 3, 2, 4)

    def step(R, inp):
        qi, ki, vi = inp
        s = jnp.einsum('bhqd,bhkd->bhqk', qi, ki) * inner_decay
        o = jnp.einsum('bhqk,bhkv->bhqv', s, vi) + jnp.einsum('bhqd,bhdv->bhqv', qi * q_decay[..., None], R)
        R = R * chunk_decay[:, None, None] + jnp.einsum('bhkd,bhkv->bhdv', ki * k_decay[..., None], vi)
        return R, o

    R0 = jnp.zeros((B, H, dk, dv), jnp.float32)
    _, o = lax.scan(step, R0, (to_chunks(q), to_chunks(k), to_chunks(v)))
    return o.transpose(1, 0, 3, 2, 4).reshape(B, T, H, dv)

def causal_multiscale_pool(u, w_group, scale):
    B, T, _ = u.shape
    nG = len(POOL_WINDOWS)
    uf = u.astype(jnp.float32).reshape(B, T, nG, POOL_GROUP)
    c = jnp.concatenate([jnp.zeros((B, 1, nG, POOL_GROUP), jnp.float32), jnp.cumsum(uf, axis=1)], axis=1)
    t = jnp.arange(T)
    means = []
    for gi, w in enumerate(POOL_WINDOWS):
        cg = c[:, :, gi]
        lo = jnp.maximum(t + 1 - w, 0)
        cnt = jnp.minimum(t + 1, w).astype(jnp.float32)
        means.append((cg[:, 1:] - cg[:, lo]) / cnt[None, :, None])
    d = jnp.stack(means, axis=2) - uf
    y = jnp.einsum('btgc,gcd->btgd', d, w_group.astype(jnp.float32)) * scale.reshape(nG, POOL_GROUP)
    return y.reshape(B, T, nG * POOL_GROUP)

def mixer_ab(x, w_in, gn_g, pool_w, pool_scale, w_out):
    B, T, _ = x.shape
    nq = RET_HEADS * RET_DK
    nv = RET_HEADS * RET_DV
    z = x @ w_in
    q, k, v, g, u = jnp.split(z, [nq, 2 * nq, 2 * nq + nv, 2 * nq + 2 * nv], axis=-1)
    q = q.reshape(B, T, RET_HEADS, RET_DK)
    k = k.reshape(B, T, RET_HEADS, RET_DK) * (RET_DK ** -0.5)
    v = v.reshape(B, T, RET_HEADS, RET_DV)
    o = retention_chunkwise(q, k, v)
    mu = o.mean(-1, keepdims=True)
    var = jnp.square(o - mu).mean(-1, keepdims=True)
    o = ((o - mu) * lax.rsqrt(var + LN_EPS)).reshape(B, T, nv) * gn_g
    ret = jax.nn.silu(g.astype(jnp.float32)) * o
    pool = causal_multiscale_pool(u, pool_w, pool_scale)
    mixed = jnp.concatenate([ret, pool], axis=-1).astype(x.dtype)
    return mixed @ w_out

def alibi_slopes(n):
    return jnp.exp2(-8.0 * jnp.arange(1, n + 1, dtype=jnp.float32) / n)

def mixer_c(x, w_in, q_norm, kv_norm, w_uq, w_uk, w_uv, w_out):
    B, T, _ = x.shape
    topk = min(IDX_TOPK_MAX, T // 4)
    z = x @ w_in
    s1 = C_Q_RANK
    s2 = s1 + C_KV_RANK
    s3 = s2 + IDX_HEADS * IDX_DIM
    s4 = s3 + IDX_DIM
    c_q, c_kv, q_idx, k_idx, w_idx = jnp.split(z, [s1, s2, s3, s4], axis=-1)
    c_q = rms_norm(c_q, q_norm)
    c_kv = rms_norm(c_kv, kv_norm)
    q_idx = q_idx.reshape(B, T, IDX_HEADS, IDX_DIM)
    slopes = alibi_slopes(C_HEADS)
    scale = C_HEAD_DIM ** -0.5
    pos = jnp.arange(T)

    def block(bi):
        start = bi * Q_BLOCK
        tq = start + jnp.arange(Q_BLOCK)
        qb = lax.dynamic_slice_in_dim(q_idx, start, Q_BLOCK, axis=1)
        wb = lax.dynamic_slice_in_dim(w_idx, start, Q_BLOCK, axis=1)
        cqb = lax.dynamic_slice_in_dim(c_q, start, Q_BLOCK, axis=1)
        sc = jax.nn.relu(jnp.einsum('bqhd,bsd->bqhs', qb, k_idx))
        I = jnp.einsum('bqh,bqhs->bqs', wb, sc).astype(jnp.float32)
        I = jnp.where((pos[None, :] <= tq[:, None])[None], I, -jnp.inf)
        _, idx = lax.top_k(I, topk)
        valid = idx <= tq[None, :, None]
        c_sel = jax.vmap(lambda c, i: c[i])(c_kv, idx)
        qh = (cqb @ w_uq).reshape(B, Q_BLOCK, C_HEADS, C_HEAD_DIM)
        q_abs = jnp.einsum('bqhd,chd->bqhc', qh, w_uk)
        logits = jnp.einsum('bqhc,bqkc->bqhk', q_abs, c_sel).astype(jnp.float32) * scale
        dist = (tq[None, :, None] - idx).astype(jnp.float32)
        logits = logits - slopes[None, None, :, None] * dist[:, :, None, :]
        logits = jnp.where(valid[:, :, None, :], logits, -jnp.inf)
        prob = jax.nn.softmax(logits, axis=-1).astype(c_sel.dtype)
        o_lat = jnp.einsum('bqhk,bqkc->bqhc', prob, c_sel)
        o = jnp.einsum('bqhc,chd->bqhd', o_lat, w_uv)
        return o.reshape(B, Q_BLOCK, C_HEADS * C_HEAD_DIM)

    o = lax.map(block, jnp.arange(T // Q_BLOCK))
    o = o.transpose(1, 0, 2, 3).reshape(B, T, C_HEADS * C_HEAD_DIM)
    return o @ w_out

def hierarchical_moe(x, w_group, b_group, w_expert, b_expert, w_gu, w_down):
    B, T, D = x.shape
    N = B * T
    xt = x.reshape(N, D)
    ar = jnp.arange(N)
    g_logits = (xt @ w_group).astype(jnp.float32) + b_group
    g_prob = jax.nn.softmax(g_logits, axis=-1)
    _, grp = lax.top_k(g_logits, 1)
    grp = grp[:, 0]
    g_w = g_prob[ar, grp]
    e_logits = ((xt @ w_expert).astype(jnp.float32) + b_expert).reshape(N, N_GROUPS, EXPERTS_PER_GROUP)
    e_logits = e_logits[ar, grp]
    top_v, top_i = lax.top_k(e_logits, TOPK_IN_GROUP)
    gate = g_w[:, None] * jax.nn.softmax(top_v, axis=-1)
    expert = grp[:, None] * EXPERTS_PER_GROUP + top_i
    M = N * TOPK_IN_GROUP
    flat_e = expert.reshape(M)
    flat_tok = jnp.repeat(ar, TOPK_IN_GROUP)
    flat_gate = gate.reshape(M)
    order = jnp.argsort(flat_e)
    e_sorted = flat_e[order]
    counts = jnp.bincount(flat_e, length=N_EXPERTS)
    start = jnp.cumsum(counts) - counts
    padded = ((counts + MOE_BLOCK - 1) // MOE_BLOCK) * MOE_BLOCK
    pend = jnp.cumsum(padded)
    pstart = pend - padded
    dest = pstart[e_sorted] + (jnp.arange(M) - start[e_sorted])
    n_blocks = -(-(M + N_EXPERTS * (MOE_BLOCK - 1)) // MOE_BLOCK)
    R = n_blocks * MOE_BLOCK
    row_tok = jnp.zeros((R,), jnp.int32).at[dest].set(flat_tok[order].astype(jnp.int32))
    row_gate = jnp.zeros((R,), jnp.float32).at[dest].set(flat_gate[order])
    blk_e = jnp.minimum(jnp.searchsorted(pend, jnp.arange(n_blocks) * MOE_BLOCK, side='right'), N_EXPERTS - 1)

    def run(args):
        tok, e = args
        h = xt[tok] @ w_gu[e]
        a, b = jnp.split(h, 2, axis=-1)
        return (jax.nn.silu(a) * b) @ w_down[e]

    ys = lax.map(run, (row_tok.reshape(n_blocks, MOE_BLOCK), blk_e)).reshape(R, D)
    y = jnp.zeros((N, D), jnp.float32).at[row_tok].add(ys.astype(jnp.float32) * row_gate[:, None])
    return y.astype(x.dtype).reshape(B, T, D)

def setup_inputs(seed: int = 0) -> dict:
    key = jax.random.key(seed)
    ks = iter(jax.random.split(key, 40))
    f32 = jnp.float32

    def nrm(shape, s):
        return jax.random.normal(next(ks), shape, f32) * s

    def gain(shape):
        return 1.0 + 0.02 * jax.random.normal(next(ks), shape, f32)

    nq = RET_HEADS * RET_DK
    nv = RET_HEADS * RET_DV
    ab_col_scale = jnp.ones((AB_IN,), f32).at[2 * nq:2 * nq + nv].set(BETA)
    return {
        "x": nrm((BATCH, SEQ, D_MODEL), 1.0),
        "p": nrm((DEPTH, BATCH, SEQ, PLE_DIM), 1.0),
        "ab_w_in": nrm((N_EVEN, D_MODEL, AB_IN), D_MODEL ** -0.5) * ab_col_scale,
        "ret_gn_g": gain((N_EVEN, nv)),
        "pool_w": nrm((N_EVEN, len(POOL_WINDOWS), POOL_GROUP, POOL_GROUP), POOL_GROUP ** -0.5 * BETA),
        "pool_scale": gain((N_EVEN, POOL_WIDTH)),
        "ab_w_out": nrm((N_EVEN, AB_MIX, D_MODEL), AB_MIX ** -0.5 * BETA),
        "c_w_in": nrm((N_ODD, D_MODEL, C_IN), D_MODEL ** -0.5),
        "c_q_norm": gain((N_ODD, C_Q_RANK)),
        "c_kv_norm": gain((N_ODD, C_KV_RANK)),
        "c_w_uq": nrm((N_ODD, C_Q_RANK, C_HEADS * C_HEAD_DIM), C_Q_RANK ** -0.5),
        "c_w_uk": nrm((N_ODD, C_KV_RANK, C_HEADS, C_HEAD_DIM), C_KV_RANK ** -0.5),
        "c_w_uv": nrm((N_ODD, C_KV_RANK, C_HEADS, C_HEAD_DIM), C_KV_RANK ** -0.5 * BETA),
        "c_w_out": nrm((N_ODD, C_HEADS * C_HEAD_DIM, D_MODEL), (C_HEADS * C_HEAD_DIM) ** -0.5 * BETA),
        "ln1_g": gain((DEPTH, D_MODEL)),
        "ln1_b": nrm((DEPTH, D_MODEL), 0.02),
        "ln2_g": gain((DEPTH, D_MODEL)),
        "ln2_b": nrm((DEPTH, D_MODEL), 0.02),
        "moe_w_group": nrm((DEPTH, D_MODEL, N_GROUPS), D_MODEL ** -0.5),
        "moe_b_group": nrm((DEPTH, N_GROUPS), 0.01),
        "moe_w_expert": nrm((DEPTH, D_MODEL, N_EXPERTS), D_MODEL ** -0.5),
        "moe_b_expert": nrm((DEPTH, N_EXPERTS), 0.01),
        "moe_w_gu": nrm((DEPTH, N_EXPERTS, D_MODEL, 2 * EXPERT_FF), D_MODEL ** -0.5),
        "moe_w_down": nrm((DEPTH, N_EXPERTS, EXPERT_FF, D_MODEL), EXPERT_FF ** -0.5 * BETA),
        "ple_w_gate": nrm((DEPTH, D_MODEL, D_MODEL), D_MODEL ** -0.5),
        "ple_w_proj": nrm((DEPTH, PLE_DIM, D_MODEL), PLE_DIM ** -0.5),
    }

def reference(x, p, ab_w_in, ret_gn_g, pool_w, pool_scale, ab_w_out,
              c_w_in, c_q_norm, c_kv_norm, c_w_uq, c_w_uk, c_w_uv, c_w_out,
              ln1_g, ln1_b, ln2_g, ln2_b,
              moe_w_group, moe_b_group, moe_w_expert, moe_b_expert, moe_w_gu, moe_w_down,
              ple_w_gate, ple_w_proj):
    for i in range(DEPTH):
        j = i // 2
        if i % 2 == 0:
            h = mixer_ab(x, ab_w_in[j], ret_gn_g[j], pool_w[j], pool_scale[j], ab_w_out[j])
        else:
            h = mixer_c(x, c_w_in[j], c_q_norm[j], c_kv_norm[j], c_w_uq[j], c_w_uk[j], c_w_uv[j], c_w_out[j])
        x = layer_norm(ALPHA * x + h.astype(x.dtype), ln1_g[i], ln1_b[i])
        m = hierarchical_moe(x, moe_w_group[i], moe_b_group[i], moe_w_expert[i], moe_b_expert[i],
                             moe_w_gu[i], moe_w_down[i])
        x = layer_norm(ALPHA * x + m, ln2_g[i], ln2_b[i])
        x = x + jax.nn.sigmoid(x @ ple_w_gate[i]) * (p[i] @ ple_w_proj[i])
    return x


_drawn_inputs = setup_inputs


def setup_inputs(seed=0):
    import zlib

    import numpy as np

    out = dict(_drawn_inputs(seed))
    spreads = {}
    factors = {'ret_gn_g': 8.0,
     'pool_scale': 8.0,
     'c_q_norm': 8.0,
     'c_kv_norm': 8.0,
     'moe_b_group': 8.0,
     'moe_b_expert': 8.0}
    for name, (base, spread) in spreads.items():
        noise = np.random.default_rng([zlib.crc32(name.encode()), seed]).standard_normal(out[name].shape)
        drawn = base * np.exp(spread * noise) if base else spread * noise
        out[name] = __import__('jax').numpy.asarray(drawn.astype(out[name].dtype))
    for name, factor in factors.items():
        out[name] = (out[name] * factor).astype(out[name].dtype)
    return out
```

```python
from contextlib import ExitStack

import concourse.bass as bass
from concourse import mybir

F32 = mybir.dt.float32
BF16 = mybir.dt.bfloat16
U32 = mybir.dt.uint32
I32 = mybir.dt.int32
ALU = mybir.AluOpType
ACT = mybir.ActivationFunctionType
AX = mybir.AxisListType

P = 128
SEQ = 512
D = 1024
T = SEQ // P
KD = D // P
NB = 512
PLE = 256
RH = 4
WINDOWS = (2, 4, 8, 16)
WMAX = WINDOWS[-1]
AH, HD = 16, 64
RANK = 256
IH = 8
TOPK = min(256, SEQ // 4)
NG, EPG = 4, 8
NE = NG * EPG
FF = 512
SLOTS = 64
TABLE = SEQ
MORE = (2 * SEQ) // (SLOTS + 1)
NOWHERE = 4 * SEQ
ALPHA = 4.0 ** 0.25
LN_EPS = 1e-5
RMS_EPS = 1e-6
BIG = 1e30
LOWEST = -3.0e38


def build(nc, A, out):
    ctx = ExitStack()
    ctx.enter_context(nc.allow_non_contiguous_dma(reason="small vectors to one feature per partition"))
    with ctx:
        def sb(name, shape, dt=F32):
            return ctx.enter_context(nc.sbuf_tensor(name, shape, dt))

        def lasting(name):
            return ctx.enter_context(nc.semaphore(name))

        class Stages:

            now, cleared = [], []

            @staticmethod
            def new(name):
                s = nc.alloc_semaphore(name)
                Stages.now.append(s)
                return s

            @staticmethod
            def end():
                for s in Stages.cleared:
                    nc.release_semaphore(s)
                for s in Stages.now:
                    nc.gpsimd.sem_clear(s)
                Stages.now, Stages.cleared = [], Stages.now

        sem = Stages.new

        def dram(name, shape):
            return nc.dram_tensor(name, shape, F32, kind="Internal").ap()

        def three(ap, b):
            return ap.rearrange("p (a b) -> p a b", b=b)

        wide = [sb("wide0", [P, KD * D]), sb("wide1", [P, KD * D])]
        slim = [sb("slim0", [P, T * D]), sb("slim1", [P, T * D])]
        X = sb("X", [P, T, D])
        XT = sb("XT", [P, KD, SEQ])
        w1 = sb("w1", [P, 4096])
        w2 = sb("w2", [P, 4096])
        w3 = sb("w3", [P, 4096])
        w4 = sb("w4", [P, 4096])
        ln_g = sb("ln_g", [P, D])
        ln_b = sb("ln_b", [P, D])
        ident = sb("ident", [P, P])
        tri = sb("tri", [P, P], BF16)
        ones = sb("ones", [P, P], BF16)
        eps = sb("eps", [P, 2])
        iota = sb("iota", [P, NE])
        half_col = sb("half_col", [P, 1])
        tok_col = sb("tok_col", [P, T])
        gains = sb("gains", [P, 16])
        stats = sb("stats", [P, 16, 6])
        mv = sb("mv", [P, 16, 2])
        rstd = sb("rstd", [P, 16])
        PS = ctx.enter_context(nc.psum_tensor("PS", [P, 8, NB], F32))

        x_rows = dram("x_rows", [SEQ, D])
        y_rows = dram("y_rows", [2 * SEQ * 2, NB])
        table = dram("table", [NE * TABLE, 4])

        class Jobs:

            def __init__(self, name, owners):
                self.owners = owners
                self.full = sem(f"{name}_full")
                self.emptied = {o: sem(f"{name}_by_{o}") for o in sorted(set(owners))}

            def wait_full(self, eng, j):
                eng.wait_ge(self.full, j + 1)

            def wait_emptied(self, eng, j):
                o = self.owners[j]
                eng.wait_ge(self.emptied[o], self.owners[:j + 1].count(o))

            def wait_all_emptied(self, eng):
                for o, s in self.emptied.items():
                    eng.wait_ge(s, self.owners.count(o))

            def sem_of(self, j):
                return self.emptied[self.owners[j]]

        class Own:

            def __init__(self, eng, name):
                self.eng, self.sem, self.n = eng, sem(name), 0

            def done(self, ins):
                self.n += 1
                ins.then_inc(self.sem, 1)
                self.eng.wait_ge(self.sem, self.n)

            def mark(self, ins):
                self.n += 1
                ins.then_inc(self.sem, 1)

            def wait(self):
                self.eng.wait_ge(self.sem, self.n)

        class Turn:

            def __init__(self, name, bank):
                self.full, self.by_act, self.by_dve = sem(f"{name}_full"), sem(f"{name}_by_act"), sem(f"{name}_by_dve")
                self.bank = bank

            def pe(self, pe, t):
                for k in range(KD):
                    m = pe.transpose(PS[:, self.bank(t) + k // 4, (k % 4) * P:(k % 4 + 1) * P],
                                     X[:, t, k * P:(k + 1) * P], ident[:, :])
                m.then_inc(self.full, 1)

            def act(self, act, t):
                act.wait_ge(self.full, t + 1)
                act.activation(XT[:, 0:4, t * P:(t + 1) * P], three(PS[:, self.bank(t), :], P), ACT.Copy)\
                   .then_inc(self.by_act, 1)

            def dve(self, dve, t):
                dve.wait_ge(self.full, t + 1)
                dve.tensor_copy(XT[:, 4:8, t * P:(t + 1) * P], three(PS[:, self.bank(t) + 1, :], P))\
                   .then_inc(self.by_dve, 1)

            def wait(self, eng, t):
                eng.wait_ge(self.by_act, t + 1)
                eng.wait_ge(self.by_dve, t + 1)

        def alternate(n):
            return ["act" if j % 2 == 0 else "dve" for j in range(n)]

        class Norm:

            def __init__(self, name):
                self.var, self.std, self.done = sem(f"{name}_var"), sem(f"{name}_std"), sem(f"{name}_done")
                self.name = name

            def dve_tile(self, dve, own, t):
                for c in range(2):
                    own.mark(dve.bn_stats(stats[:, 2 * t + c, :], X[:, t, c * NB:(c + 1) * NB]))
                own.wait()
                dve.bn_aggr(mv[:, t, :], stats[:, 2 * t:2 * t + 2, :]).then_inc(self.var, 1)
                dve.wait_ge(self.std, t + 1)
                own.done(dve.reciprocal(rstd[:, t:t + 1], rstd[:, 8 + t:9 + t]))
                own.done(dve.tensor_scalar(X[:, t, :], X[:, t, :], mv[:, t, 0:1], rstd[:, t:t + 1],
                                           ALU.subtract, ALU.mult))
                own.done(dve.tensor_tensor(X[:, t, :], X[:, t, :], ln_g[:, :], ALU.mult))
                dve.tensor_tensor(X[:, t, :], X[:, t, :], ln_b[:, :], ALU.add).then_inc(self.done, 1)

            def act_tile(self, act, t):
                act.wait_ge(self.var, t + 1)
                act.activation(rstd[:, 8 + t:9 + t], mv[:, t, 1:2], ACT.Sqrt, bias=eps[:, 0:1])\
                   .then_inc(self.std, 1)

        def load_ln(eng, g, b, s):
            eng.dma_start(ln_g[:, :], g.partition_broadcast(P)).then_inc(s, 16)
            eng.dma_start(ln_b[:, :], b.partition_broadcast(P)).then_inc(s, 16)

        def rows(w, n):
            return w.rearrange("(k p) n -> p k n", p=P)

        pair = [[(wide[1], slim[0]), (wide[0], slim[1])],
                [(wide[0], slim[1]), (wide[1], slim[0])]]
        gu_in = [[lasting(f"gu_in{l}{q}") for q in range(2)] for l in range(2)]
        dn_in = [[lasting(f"dn_in{l}{q}") for q in range(2)] for l in range(2)]

        def load_gu(eng, l, q, e):
            src = A["moe_w_gu"][l][bass.ds(e, 1)]
            eng.dma_start(pair[l][q][0][:, :].rearrange("p (e k n) -> p e k n", e=1, k=KD),
                          src.rearrange("e (k p) n -> p e k n", p=P)).then_inc(gu_in[l][q], 16)

        def load_dn(eng, l, q, e):
            src = A["moe_w_down"][l][bass.ds(e, 1)]
            eng.dma_start(pair[l][q][1][:, :].rearrange("p (e k n) -> p e k n", e=1, k=FF // P),
                          src.rearrange("e (k p) n -> p e k n", p=P)).then_inc(dn_in[l][q], 16)


        s_x = [lasting(f"s_x{t}") for t in range(T)]
        s_const = lasting("s_const")
        s_ident = lasting("s_ident")
        s_bf = lasting("s_bf")
        s_w = [lasting(f"s_w_in{c}") for c in range(5)]
        s_wout = [lasting(f"s_wout{c}") for c in range(2)]
        s_ln = lasting("s_ln")
        s_gain = lasting("s_gain")
        s_dec = lasting("s_dec")
        s_pool = lasting("s_pool")

        w_in = [three(a, NB) for a in (wide[0][:, 0:4096], wide[0][:, 4096:8192], wide[1][:, 0:4096],
                                       wide[1][:, 4096:8192], slim[0][:, :])]
        QT, KT = three(w1[:, 0:2048], SEQ), three(w1[:, 2048:4096], SEQ)
        V, SG = three(w2[:, 0:2048], NB), three(w2[:, 2048:4096], NB)
        UT, DEC = three(w3[:, 0:2048], SEQ), three(w3[:, 2048:4096], SEQ)
        tri32 = w4[:, 3000:3128]
        w_out0 = [three(slim[1][:, :], NB), three(wide[0][:, 0:4096], NB)]

        turn_x = Turn("turn_x", lambda t: 2 * t)
        pj_owner = alternate(8) + ["dve"] * 4 + ["act"] * 4 + alternate(4)
        pj = Jobs("proj", pj_owner)
        PROJ = len(pj_owner)

        with nc.Block() as block:
            @block.sync
            def _(sp):
                for t in range(T):
                    sp.dma_start(X[:, t, :], A["x"][0, t * P:(t + 1) * P, :]).then_inc(s_x[t], 16)
                for c in range(5):
                    sp.dma_start(w_in[c], rows(A["ab_w_in"][0, :, c * NB:(c + 1) * NB], NB)).then_inc(s_w[c], 16)
                sp.dma_start(DEC, A["c_decay"].rearrange("h p n -> p h n")).then_inc(s_dec, 16)
                sp.dma_start(w_out0[0], rows(A["ab_w_out"][0, :, 0:NB], NB)).then_inc(s_wout[0], 16)

            @block.gpsimd
            def _(pool):
                pool.memset(ones[:, :], 1.0).then_inc(s_bf, 1)
                pool.wait_ge(s_const, 80)
                pool.tensor_copy(tri[:, :], tri32).then_inc(s_bf, 1)
                pool.wait_ge(s_bf, 2)

            @block.scalar
            def _(act):
                act.dma_start(ident[:, :], A["c_ident"]).then_inc(s_ident, 16)
                act.dma_start(tri32, A["c_tri"]).then_inc(s_const, 16)
                act.dma_start(iota[:, :], A["c_iota"]).then_inc(s_const, 16)
                act.dma_start(half_col[:, :], A["c_half"]).then_inc(s_const, 16)
                act.dma_start(tok_col[:, :], A["c_tok"]).then_inc(s_const, 16)
                act.dma_start(eps[:, :], A["c_eps"]).then_inc(s_const, 16)
                load_ln(act, A["ln1_g"][0], A["ln1_b"][0], s_ln)
                act.dma_start(gains[:, 0:4], A["ret_gn_g"][0].rearrange("(k p) -> p k", p=P)).then_inc(s_gain, 16)
                act.dma_start(gains[:, 4:8], A["pool_scale"][0].rearrange("(k p) -> p k", p=P)).then_inc(s_gain, 16)
                for t in range(T):
                    turn_x.act(act, t)
                for j in range(PROJ):
                    if pj_owner[j] != "act":
                        continue
                    pj.wait_full(act, j)
                    dst = (QT, KT, V, SG, UT)[j // 4][:, j % 4, :]
                    act.activation(dst, PS[:, j % 8, :], ACT.Silu if j // 4 == 3 else ACT.Copy)\
                       .then_inc(pj.sem_of(j), 1)

            @block.vector
            def _(dve):
                for t in range(T):
                    turn_x.dve(dve, t)
                for j in range(PROJ):
                    if pj_owner[j] != "dve":
                        continue
                    pj.wait_full(dve, j)
                    dst = (QT, KT, V, SG, UT)[j // 4][:, j % 4, :]
                    dve.tensor_copy(dst, PS[:, j % 8, :]).then_inc(pj.sem_of(j), 1)

            @block.tensor
            def _(pe):
                pe.wait_ge(s_ident, 16)
                for t in range(T):
                    pe.wait_ge(s_x[t], 16)
                    turn_x.pe(pe, t)
                turn_x.wait(pe, T - 1)
                for j in range(PROJ):
                    c, i = j // 4, j % 4
                    if i == 0:
                        pe.wait_ge(s_w[c], 16)
                    if j >= 8:
                        pj.wait_emptied(pe, j - 8)
                    for k in range(KD):
                        if c in (2, 3):
                            lhsT, rhs = XT[:, k, i * P:(i + 1) * P], w_in[c][:, k, :]
                        else:
                            lhsT, rhs = w_in[c][:, k, i * P:(i + 1) * P], XT[:, k, :]
                        m = pe.matmul(PS[:, j % 8, :], lhsT, rhs, start=(k == 0), stop=(k == KD - 1))
                    m.then_inc(pj.full, 1)
        Stages.end()

        ST = [[w4[:, b * 1280 + o:b * 1280 + o + n] for o, n in ((0, 512), (512, 384), (896, 256), (1152, 128))]
              for b in range(2)]
        RN = three(wide[0][:, 4096:6144], NB)
        PW = three(wide[0][:, 6144:6656], P)
        EDGE = three(w4[:, 2560:2624], WMAX)
        DT = three(w1[:, 0:2048], SEQ)
        TMP = [w3[:, 2048:2560], w3[:, 2560:3072]]
        MT = XT

        s_score = sem("s_score")
        s_st = sem("s_st")
        s_o = sem("s_o")
        s_gvar = sem("s_gvar")
        s_gstd = sem("s_gstd")
        s_rn = sem("s_rn")
        s_dt = sem("s_dt")
        s_edge = lasting("s_edge")
        mt = Jobs("mixed", ["act"] * 8)

        with nc.Block() as block:
            @block.sync
            def _(sp):
                sp.dma_start(PW, A["pool_w"][0].rearrange("g c d -> c g d")).then_inc(s_pool, 16)
                sp.dma_start(w4[:, 2560:2624], A["c_edge"].rearrange("g n -> (g n)").partition_broadcast(P))\
                  .then_inc(s_edge, 16)
                sp.dma_start(w_out0[1], rows(A["ab_w_out"][0, :, NB:D], NB)).then_inc(s_wout[1], 16)
                load_gu(sp, 0, 0, 0)
                load_dn(sp, 0, 0, 0)

            @block.tensor
            def _(pe):
                for h in range(RH):
                    for kb in range(T):
                        if h >= 1:
                            pe.wait_ge(s_st, 4 * (h - 1) + kb + 1)
                        pe.matmul(PS[:, 4 + kb, 0:SEQ - kb * P], KT[:, h, kb * P:(kb + 1) * P],
                                  QT[:, h, kb * P:SEQ], start=True, stop=True).then_inc(s_score, 1)
                    pe.wait_ge(s_st, 4 * h + 4)
                    for t in range(T):
                        for kb in range(t + 1):
                            m = pe.matmul(PS[:, t, h * P:(h + 1) * P], ST[h % 2][kb][:, (t - kb) * P:(t - kb + 1) * P],
                                          V[:, kb, h * P:(h + 1) * P], start=(kb == 0), stop=(kb == t))
                    m.then_inc(s_o, 1)
                pe.wait_ge(s_pool, 16)
                for g in range(4):
                    pe.wait_ge(s_dt, g + 1)
                    pe.matmul(PS[:, 4 + g, :], PW[:, g, :], DT[:, g, :], start=True, stop=True)\
                      .then_inc(mt.full, 1)
                pe.wait_ge(s_rn, T)
                for h in range(RH):
                    for t in range(T):
                        m = pe.transpose(PS[:, h, t * P:(t + 1) * P], RN[:, t, h * P:(h + 1) * P], ident[:, :])
                    m.then_inc(mt.full, 1)

            @block.vector
            def _(dve):
                own = Own(dve, "own_ret")
                dve.wait_ge(s_dec, 16)
                for h in range(RH):
                    for kb in range(T):
                        dve.wait_ge(s_score, 4 * h + kb + 1)
                        if h >= 2 and kb == 0:
                            dve.wait_ge(s_o, h - 1)
                        n = SEQ - kb * P
                        dve.tensor_tensor(ST[h % 2][kb], PS[:, 4 + kb, 0:n], DEC[:, h, 0:n], ALU.mult)\
                           .then_inc(s_st, 1)
                dve.wait_ge(s_st, 4 * RH)
                dve.wait_ge(s_o, RH)
                dve.wait_ge(s_edge, 16)
                for g, w in enumerate(WINDOWS):
                    src, n, b = UT[:, g, :], 1, 0
                    while n < w:
                        dst = TMP[b]
                        own.mark(dve.tensor_copy(dst[:, 0:n], src[:, 0:n]))
                        own.done(dve.tensor_tensor(dst[:, n:SEQ], src[:, n:SEQ], src[:, 0:SEQ - n], ALU.add))
                        src, n, b = dst, 2 * n, 1 - b
                    own.done(dve.tensor_tensor(src[:, 0:WMAX], src[:, 0:WMAX], EDGE[:, g, :], ALU.mult))
                    dve.scalar_tensor_tensor(DT[:, g, :], src, 1.0 / w, UT[:, g, :], ALU.mult, ALU.subtract)\
                       .then_inc(s_dt, 1)
                    dve.wait_ge(s_dt, g + 1)
                for i in range(T * RH):
                    own.mark(dve.bn_stats(stats[:, i, :], PS[:, i // RH, (i % RH) * P:(i % RH + 1) * P]))
                own.wait()
                for i in range(T * RH):
                    m = dve.bn_aggr(mv[:, i, :], stats[:, i, :])
                m.then_inc(s_gvar, 1)
                dve.wait_ge(s_gstd, 1)
                own.done(dve.reciprocal(rstd[:, :], rstd[:, :]))
                for t in range(T):
                    for h in range(RH):
                        i = t * RH + h
                        own.mark(dve.tensor_scalar(RN[:, t, h * P:(h + 1) * P], PS[:, t, h * P:(h + 1) * P],
                                                   mv[:, i, 0:1], rstd[:, i:i + 1], ALU.subtract, ALU.mult))
                    own.wait()
                    dve.tensor_tensor(RN[:, t, :], RN[:, t, :], SG[:, t, :], ALU.mult).then_inc(s_rn, 1)

            @block.scalar
            def _(act):
                act.wait_ge(s_const, 80)
                act.wait_ge(s_gain, 32)
                for g in range(4):
                    mt.wait_full(act, g)
                    act.activation(MT[:, 4 + g, :], PS[:, 4 + g, :], ACT.Copy, scale=gains[:, 4 + g:5 + g])\
                       .then_inc(mt.sem_of(g), 1)
                act.wait_ge(s_gvar, 1)
                act.activation(rstd[:, :], mv[:, :, 1], ACT.Sqrt, bias=eps[:, 0:1]).then_inc(s_gstd, 1)
                for h in range(RH):
                    mt.wait_full(act, 4 + h)
                    act.activation(MT[:, h, :], PS[:, h, :], ACT.Copy, scale=gains[:, h:h + 1])\
                       .then_inc(mt.sem_of(4 + h), 1)
        Stages.end()

        def route_views():
            at, views = [0], {}

            def take(name, *shape, rows=P, dt=F32):
                n = 1
                for s in shape:
                    n *= s
                words = n if dt != BF16 else n // 2
                ap = w1[0:rows, at[0]:at[0] + words]
                at[0] += words
                if dt != F32:
                    ap = ap.bitcast(dt)
                views[name] = three(ap, shape[1]) if len(shape) == 2 else ap
                return ap

            take("WR", KD, NG + NE)
            take("LT", SEQ, rows=NG + NE)
            take("L", T, NG + NE)
            for name in ("G8", "gtop", "etop", "es", "gexp"):
                take(name, T, EPG)
            take("gidx", T, EPG, dt=U32)
            take("eidx", T, EPG, dt=U32)
            take("ohg", T, NG)
            for name in ("gf", "gsum", "ngmax", "gw", "diff", "ex", "ex1"):
                take(name, T)
            for name in ("ef", "pos", "gate"):
                take(name, 2, T)
            take("place_f", 2 * T)
            take("place", 2 * T, dt=U32)
            take("entry", 2 * T, 4)
            take("oh0", T, NE)
            take("oh1", T, NE)
            take("junk", NE)
            take("M", T, NE, dt=BF16)
            take("bias", 1, rows=NG + NE)
            take("meta", NE, 4)
            take("taken", NE, dt=U32)
            take("put", NE, dt=U32)
            take("gate_of", NE)
            take("empty", NB)
            for name in ("cnt",):
                take(name, NE, rows=1)
            for name in ("more_key", "more_min", "flags", "keys"):
                take(name, NE * 7, rows=1)
            take("top", 16, rows=1)
            take("start_i", 16, rows=1, dt=I32)
            take("expert_i", 16, rows=1, dt=I32)
            take("n_more", 1, rows=1)
            take("n_more_i", 1, rows=1, dt=I32)
            assert at[0] <= 4096
            return views

        R = route_views()

        def out_projection(l, w_halves, w_sems, then_load):
            n = f"out{l}"
            sums = Jobs(f"{n}_sum", ["dve"] * 8)
            norm = Norm(f"{n}_norm")
            turn = Turn(f"{n}_turn", lambda t: 2 * t)
            s_rows = sem(f"{n}_rows")
            s_wr, s_more, s_empty = sem(f"{n}_router_w"), sem(f"{n}_more"), sem(f"{n}_empty")
            with nc.Block() as block:
                @block.tensor
                def _(pe):
                    for s in w_sems:
                        pe.wait_ge(s, 16)
                    for t in range(T + 2):
                        if t < T:
                            for c in range(2):
                                for k in range(KD):
                                    m = pe.matmul(PS[:, 2 * t + c, :], MT[:, k, t * P:(t + 1) * P],
                                                  w_halves[c][:, k, :], start=(k == 0), stop=(k == KD - 1))
                                m.then_inc(sums.full, 1)
                        if t >= 2:
                            pe.wait_ge(norm.done, t - 1)
                            turn.pe(pe, t - 2)

                @block.vector
                def _(dve):
                    own = Own(dve, f"{n}_own")
                    dve.wait_ge(s_ln, 64 * l + 32)
                    for t in range(T + 1):
                        if t < T:
                            for c in range(2):
                                sums.wait_full(dve, 2 * t + c)
                                xs = X[:, t, c * NB:(c + 1) * NB]
                                dve.scalar_tensor_tensor(xs, xs, ALPHA, PS[:, 2 * t + c, :], ALU.mult, ALU.add)\
                                   .then_inc(sums.sem_of(0), 1)
                            sums.wait_emptied(dve, 2 * t + 1)
                            norm.dve_tile(dve, own, t)
                        if t >= 1:
                            turn.dve(dve, t - 1)

                @block.scalar
                def _(act):
                    for t in range(T + 1):
                        if t < T:
                            norm.act_tile(act, t)
                        if t >= 1:
                            turn.act(act, t - 1)

                @block.sync
                def _(sp):
                    sp.dma_start(R["WR"][:, :, 0:NG], rows(A["moe_w_group"][l], NG)).then_inc(s_wr, 16)
                    sp.dma_start(R["WR"][:, :, NG:NG + NE], rows(A["moe_w_expert"][l], NE)).then_inc(s_wr, 16)
                    sp.dma_start(R["bias"][0:NG, :], A["moe_b_group"][l].rearrange("(n a) -> n a", a=1))\
                      .then_inc(s_wr, 16)
                    sp.dma_start(R["bias"][NG:NG + NE, :], A["moe_b_expert"][l].rearrange("(n a) -> n a", a=1))\
                      .then_inc(s_wr, 16)
                    sp.dma_start(R["more_key"], A["c_more"][0:1, :]).then_inc(s_more, 16)
                    sp.dma_start(R["more_min"], A["c_more"][1:2, :]).then_inc(s_more, 16)
                    sp.dma_start(R["empty"], A["c_empty"]).then_inc(s_empty, 16)
                    sp.wait_ge(s_empty, 16)
                    sp.dma_start(table.rearrange("(p s) c -> p (s c)", p=P), R["empty"]).then_inc(s_empty, 16)
                    for t in range(T):
                        sp.wait_ge(norm.done, t + 1)
                        sp.dma_start(x_rows[t * P:(t + 1) * P, :], X[:, t, :]).then_inc(s_rows, 16)
                    load_ln(sp, A["ln2_g"][l], A["ln2_b"][l], s_ln)
                    then_load(sp, sums)
                    sp.wait_ge(s_rows, 16 * T)
                    sp.wait_ge(s_wr, 64)
                    sp.wait_ge(s_more, 32)
                    sp.wait_ge(s_empty, 32)
            Stages.end()

        LP = three(PS[:, 1, 0:T * (NG + NE)], NG + NE)
        RK = three(PS[:, 2, 0:T * NE], NE)
        CP = PS[0:1, 3, 0:NE]

        def route(l):
            n = f"route{l}"
            s_lt, s_lts, s_l = sem(f"{n}_lt"), sem(f"{n}_lts"), sem(f"{n}_l")
            s_gmax, s_gexp, s_diff, s_ex = sem(f"{n}_gmax"), sem(f"{n}_gexp"), sem(f"{n}_diff"), sem(f"{n}_ex")
            s_member, s_rank, s_entry = sem(f"{n}_member"), sem(f"{n}_rank"), sem(f"{n}_entry")
            s_tab, s_meta = lasting(f"{n}_tab"), sem(f"{n}_meta")
            OH = (R["oh0"], R["oh1"])
            with nc.Block() as block:
                @block.tensor
                def _(pe):
                    for k in range(KD):
                        m = pe.matmul(PS[0:NG + NE, 0, :], R["WR"][:, k, :], XT[:, k, :],
                                      start=(k == 0), stop=(k == KD - 1))
                    m.then_inc(s_lt, 1)
                    pe.wait_ge(s_lts, 1)
                    for t in range(T):
                        m = pe.transpose(LP[:, t, :], R["LT"][:, t * P:(t + 1) * P], ident[0:NG + NE, 0:NG + NE])
                    m.then_inc(s_l, 1)
                    pe.wait_ge(s_member, 1)
                    for t in range(T):
                        for u in range(t):
                            pe.matmul(RK[:, t, :], ones[:, :], R["M"][:, u, :], start=(u == 0), stop=False)
                        pe.matmul(RK[:, t, :], tri[:, :], R["M"][:, t, :], start=(t == 0), stop=True)
                    for t in range(T):
                        m = pe.matmul(CP, ones[:, 0:1], R["M"][:, t, :], start=(t == 0), stop=(t == T - 1))
                    m.then_inc(s_rank, 1)

                @block.scalar
                def _(act):
                    act.wait_ge(s_lt, 1)
                    act.activation(R["LT"], PS[0:NG + NE, 0, :], ACT.Identity, bias=R["bias"]).then_inc(s_lts, 1)
                    act.wait_ge(s_gmax, 1)
                    for t in range(T):
                        m = act.activation(R["gexp"][:, t, :], R["G8"][:, t, :], ACT.Exp,
                                           bias=R["ngmax"][:, t:t + 1], accum_out=R["gsum"][:, t:t + 1])
                        m.then_inc(s_gexp, 1)
                    act.wait_ge(s_diff, 1)
                    act.activation(R["ex"], R["diff"], ACT.Exp).then_inc(s_ex, 1)

                @block.vector
                def _(dve):
                    own = Own(dve, f"{n}_own")
                    L, G8, es, ef, gf = R["L"], R["G8"], R["es"], R["ef"], R["gf"]
                    entry = R["entry"]
                    own.mark(dve.memset(G8, -BIG))
                    own.mark(dve.memset(entry, 0.0))
                    own.mark(dve.memset(es, 0.0))
                    own.wait()
                    dve.wait_ge(s_l, 1)
                    own.mark(dve.tensor_copy(L, LP))
                    own.done(dve.tensor_copy(G8[:, :, 0:NG], LP[:, :, 0:NG]))
                    for t in range(T):
                        own.mark(dve.max(R["gtop"][:, t, :], G8[:, t, :]))
                    own.wait()
                    dve.tensor_scalar(R["ngmax"], R["gtop"][:, :, 0], -1.0, None, ALU.mult).then_inc(s_gmax, 1)
                    for t in range(T):
                        own.mark(dve.max_index(R["gidx"][:, t, :], R["gtop"][:, t, :], G8[:, t, :]))
                    own.wait()
                    own.done(dve.tensor_copy(gf, R["gidx"][:, :, 0]))
                    for t in range(T):
                        own.mark(dve.tensor_scalar(R["ohg"][:, t, :], iota[:, 0:NG], gf[:, t:t + 1], None,
                                                   ALU.is_equal))
                    for g in range(NG):
                        own.wait()
                        for t in range(T):
                            c = NG + g * EPG
                            own.mark(dve.scalar_tensor_tensor(es[:, t, :], L[:, t, c:c + EPG],
                                                              R["ohg"][:, t, g:g + 1], es[:, t, :],
                                                              ALU.mult, ALU.add))
                    own.wait()
                    for t in range(T):
                        own.mark(dve.max(R["etop"][:, t, :], es[:, t, :]))
                    own.wait()
                    dve.tensor_tensor(R["diff"], R["etop"][:, :, 1], R["etop"][:, :, 0], ALU.subtract)\
                       .then_inc(s_diff, 1)
                    for t in range(T):
                        own.mark(dve.max_index(R["eidx"][:, t, :], R["etop"][:, t, :], es[:, t, :]))
                    own.wait()
                    for j in range(2):
                        own.mark(dve.tensor_copy(ef[:, j, :], R["eidx"][:, :, j]))
                    own.wait()
                    for j in range(2):
                        own.mark(dve.scalar_tensor_tensor(ef[:, j, :], gf, float(EPG), ef[:, j, :],
                                                          ALU.mult, ALU.add))
                    own.wait()
                    for j in range(2):
                        for t in range(T):
                            own.mark(dve.tensor_scalar(OH[j][:, t, :], iota[:, :], ef[:, j, t:t + 1], None,
                                                       ALU.is_equal))
                    own.wait()
                    dve.tensor_tensor(R["M"], OH[0], OH[1], ALU.add).then_inc(s_member, 1)
                    dve.wait_ge(s_gexp, T)
                    own.mark(dve.reciprocal(R["gw"], R["gsum"]))
                    dve.wait_ge(s_ex, 1)
                    own.done(dve.tensor_scalar(R["ex1"], R["ex"], 1.0, None, ALU.add))
                    own.done(dve.reciprocal(R["ex1"], R["ex1"]))
                    own.done(dve.tensor_tensor(R["gate"][:, 0, :], R["ex1"], R["gw"], ALU.mult))
                    own.done(dve.tensor_tensor(R["gate"][:, 1, :], R["ex"], R["gate"][:, 0, :], ALU.mult))
                    for j in range(2):
                        js = slice(j * T, (j + 1) * T)
                        own.mark(dve.tensor_copy(entry[:, js, 0], tok_col[:, :]))
                        own.mark(dve.tensor_scalar(entry[:, js, 1], tok_col[:, :], float(j * SEQ), None, ALU.add))
                        own.mark(dve.tensor_copy(entry[:, js, 2], R["gate"][:, j, :]))
                    dve.wait_ge(s_rank, 1)
                    for j in range(2):
                        for t in range(T):
                            own.done(dve.tensor_tensor_reduce(R["junk"], OH[j][:, t, :], RK[:, t, :], 1.0, 0.0,
                                                              ALU.mult, ALU.add, R["pos"][:, j, t:t + 1]))
                    own.done(dve.scalar_tensor_tensor(three(R["place_f"], T), ef, float(TABLE), R["pos"],
                                                      ALU.mult, ALU.add))
                    dve.tensor_copy(R["place"], R["place_f"]).then_inc(s_entry, 1)
                    own.done(dve.tensor_copy(R["cnt"], CP))
                    own.done(dve.tensor_tensor(three(R["flags"], 7),
                                               R["cnt"].rearrange("p (e b) -> p e b", b=1).broadcast_to([1, NE, 7]),
                                               three(R["more_min"], 7), ALU.is_gt))
                    own.done(dve.tensor_reduce(R["n_more"], R["flags"], AX.X, ALU.add))
                    own.mark(dve.tensor_copy(R["n_more_i"], R["n_more"]))
                    own.done(dve.tensor_tensor(R["keys"], R["flags"], R["more_key"], ALU.mult))
                    own.done(dve.max(R["top"][:, 0:8], R["keys"]))
                    own.done(dve.match_replace(R["keys"], R["top"][:, 0:8], R["keys"], 0.0))
                    own.done(dve.max(R["top"][:, 8:16], R["keys"]))
                    own.done(dve.tensor_scalar(R["top"], R["top"], -1.0, float(NE * TABLE), ALU.mult, ALU.add))
                    own.done(dve.tensor_copy(R["start_i"], R["top"]))
                    own.done(dve.tensor_scalar(R["expert_i"], R["start_i"], 9, None, ALU.arith_shift_right))
                    dve.wait_ge(s_meta, 32)
                    half = half_col[:, 0:1].broadcast_to([P, NE])
                    own.mark(dve.scalar_tensor_tensor(R["taken"], R["meta"][:, :, 0], 2.0, half, ALU.mult, ALU.add))
                    own.mark(dve.scalar_tensor_tensor(R["put"], R["meta"][:, :, 1], 2.0, half, ALU.mult, ALU.add))
                    own.done(dve.tensor_copy(R["gate_of"], R["meta"][:, :, 2]))

                @block.gpsimd
                def _(pool):
                    pool.wait_ge(s_entry, 1)
                    for c in range(2 * T):
                        pool.indirect_dma_start(
                            out=table, out_offset=bass.IndirectOffsetOnAxis(ap=R["place"][:, c:c + 1], axis=0),
                            in_=R["entry"][:, c, :], in_offset=None).then_inc(s_tab, 16)

                @block.sync
                def _(sp):
                    sp.wait_ge(s_tab, 16 * 2 * T)
                    view = table.rearrange("(e s) c -> s e c", e=NE)[0:SLOTS]
                    sp.dma_start(R["meta"][0:SLOTS], view).then_inc(s_meta, 16)
                    sp.dma_start(R["meta"][SLOTS:P], view).then_inc(s_meta, 16)
            Stages.end()

        x_half = x_rows.rearrange("t (u c) -> (t u) c", u=2)
        xg = [w2[:, 0:512], w2[:, 512:1024]]
        xeT = [three(w2[:, 1024:1536], SLOTS), three(w2[:, 1536:2048], SLOTS)]
        sa, ga = w2[:, 2048:2304], w2[:, 2304:2560]
        gT = three(w2[:, 2560:2816], SLOTS)
        take1 = [w2[:, 2816 + q:2817 + q].bitcast(U32) for q in range(2)]
        put1 = [w2[:, 2820 + q:2821 + q].bitcast(U32) for q in range(2)]
        meta1 = w2[:, 2824:2828]
        ys = [w2[:, 3072:3584], w2[:, 3584:4096]]

        def wait_alone(eng, semaphore, value, tick):
            eng.wait_ge(semaphore, value)
            eng.sem_inc(tick, 1)

        def gather(pool, q, index, s):
            pool.indirect_dma_start(out=xg[q], out_offset=None, in_=x_half,
                                    in_offset=bass.IndirectOffsetOnAxis(ap=index, axis=0)).then_inc(s, 16)

        def scatter(pool, q, index, s):
            pool.indirect_dma_start(out=y_rows, out_offset=bass.IndirectOffsetOnAxis(ap=index, axis=0),
                                    in_=ys[q], in_offset=None, bounds_check=4 * SEQ - 1, oob_is_err=False)\
                .then_inc(s, 16)

        def turn_gathered(pe, q):
            for c in range(4):
                m = pe.transpose(PS[:, q, c * P:(c + 1) * P], xg[q][:, c * P:(c + 1) * P], ident[:, :])
            return m

        def gate_up(pe, q, gu):
            for k in range(KD):
                for u in range(2):
                    m = pe.matmul(PS[u * SLOTS:(u + 1) * SLOTS, 2 + q, :], xeT[q][:, k, :],
                                  gu[:, k, :].rearrange("p (a u c) -> p a u c", a=2, u=2)[:, :, u, :],
                                  start=(k == 0), stop=(k == KD - 1))
            return m

        def turn_gated(pe, q):
            for c in range(2):
                m = pe.transpose(PS[:, 4 + q, c * P:(c + 1) * P], ga[:, c * P:(c + 1) * P], ident[:, :])
            return m

        def down(pe, q, dn):
            for k in range(FF // P):
                for u in range(2):
                    m = pe.matmul(PS[u * SLOTS:(u + 1) * SLOTS, 6 + q, :], gT[:, k, :],
                                  dn[:, k, u * NB:(u + 1) * NB], start=(k == 0), stop=(k == FF // P - 1))
            return m

        def copy_gathered(act, q):
            return act.activation(xeT[q].rearrange("p (u c) s -> p c u s", u=2),
                                  PS[:, q, :].rearrange("p (c u s) -> p c u s", c=4, u=2), ACT.Copy)

        def silu(act, q):
            return act.activation(sa, PS[:, 2 + q, 0:FF // 2], ACT.Silu)

        def times_up(dve, q):
            return dve.tensor_tensor(ga, sa, PS[:, 2 + q, FF // 2:FF], ALU.mult)

        def copy_gated(dve, q):
            return dve.tensor_copy(gT.rearrange("p (u c) s -> p c u s", u=2),
                                   PS[:, 4 + q, 0:2 * P].rearrange("p (c u s) -> p c u s", c=2, u=2))

        def experts(l, then_load):
            n = f"moe{l}"
            PAIRS = NE // 2

            def both(name, new=sem):
                return [new(f"{n}_{name}{q}") for q in range(2)]

            s_take, s_gath, s_turn, s_xe = both("take"), both("gath", lasting), both("turn"), both("xe")
            s_gu, s_silu, s_gated, s_gturn = both("gu"), both("silu"), both("gated"), both("gturn")
            sp_tick, pool_tick = sem(f"{n}_sp_tick"), sem(f"{n}_pool_tick")
            s_gt, s_dn, s_y, s_put, s_scat = both("gt"), both("dn"), both("y"), both("put"), both("scat", lasting)
            with nc.Block() as block:
                @block.sync
                def _(sp):
                    with sp.Fori(1, PAIRS) as i:
                        for q in range(2):
                            wait_alone(sp, s_gu[q], i, sp_tick)
                            load_gu(sp, l, q, 2 * i + q)
                            wait_alone(sp, s_dn[q], i, sp_tick)
                            load_dn(sp, l, q, 2 * i + q)
                    sp.wait_ge(s_gu[0], PAIRS)
                    sp.wait_ge(s_dn[0], PAIRS)
                    then_load(sp)

                @block.gpsimd
                def _(pool):
                    def take_rows(q, i):
                        pool.tensor_copy(take1[q], R["taken"][:, bass.ds(2 * i + q, 1)]).then_inc(s_take[q], 1)
                        wait_alone(pool, s_take[q], i + 1, pool_tick)
                        gather(pool, q, take1[q], s_gath[q])

                    def put_rows(q, i, done):
                        wait_alone(pool, s_y[q], done, pool_tick)
                        pool.tensor_copy(put1[q], R["put"][:, bass.ds(2 * i + q, 1)]).then_inc(s_put[q], 1)
                        wait_alone(pool, s_put[q], done, pool_tick)
                        scatter(pool, q, put1[q], s_scat[q])

                    take_rows(0, 0)
                    take_rows(1, 0)
                    with pool.Fori(1, PAIRS) as i:
                        for q in range(2):
                            put_rows(q, i - 1, i)
                            take_rows(q, i)
                    for q in range(2):
                        put_rows(q, PAIRS - 1, PAIRS)
                    for q in range(2):
                        pool.wait_ge(s_scat[q], 16 * PAIRS)

                @block.tensor
                def _(pe):
                    def one(q, i, first):
                        pe.wait_ge(s_gath[q], 16 * i + 16)
                        turn_gathered(pe, q).then_inc(s_turn[q], 1)
                        pe.wait_ge(s_xe[q], i + 1)
                        pe.wait_ge(gu_in[l][q], 16 * i + 16)
                        gate_up(pe, q, three(pair[l][q][0][:, :], D)).then_inc(s_gu[q], 1)
                        pe.wait_ge(s_gated[q], i + 1)
                        turn_gated(pe, q).then_inc(s_gturn[q], 1)
                        pe.wait_ge(s_gt[q], i + 1)
                        pe.wait_ge(dn_in[l][q], 16 * i + 16)
                        if not first:
                            pe.wait_ge(s_y[q], i)
                        down(pe, q, three(pair[l][q][1][:, :], D)).then_inc(s_dn[q], 1)

                    one(0, 0, True)
                    one(1, 0, True)
                    with pe.Fori(1, PAIRS) as i:
                        one(0, i, False)
                        one(1, i, False)

                @block.scalar
                def _(act):
                    def one(q, i, first):
                        act.wait_ge(s_turn[q], i + 1)
                        copy_gathered(act, q).then_inc(s_xe[q], 1)
                        act.wait_ge(s_gu[q], i + 1)
                        if q == 1:
                            act.wait_ge(s_gated[0], i + 1)
                        elif not first:
                            act.wait_ge(s_gated[1], i)
                        silu(act, q).then_inc(s_silu[q], 1)
                        act.wait_ge(s_dn[q], i + 1)
                        if not first:
                            act.wait_ge(s_scat[q], 16 * i)
                        act.activation(ys[q], PS[:, 6 + q, :], ACT.Copy,
                                       scale=R["gate_of"][:, bass.ds(2 * i + q, 1)]).then_inc(s_y[q], 1)

                    one(0, 0, True)
                    one(1, 0, True)
                    with act.Fori(1, PAIRS) as i:
                        one(0, i, False)
                        one(1, i, False)

                @block.vector
                def _(dve):
                    def one(q, i, first):
                        dve.wait_ge(s_silu[q], i + 1)
                        times_up(dve, q).then_inc(s_gated[q], 1)
                        dve.wait_ge(s_gturn[q], i + 1)
                        if q == 1:
                            dve.wait_ge(s_dn[0], i + 1)
                        elif not first:
                            dve.wait_ge(s_dn[1], i)
                        copy_gated(dve, q).then_inc(s_gt[q], 1)

                    one(0, 0, True)
                    one(1, 0, True)
                    with dve.Fori(1, PAIRS) as i:
                        one(0, i, False)
                        one(1, i, False)
            Stages.end()

        def further_passes(l):
            n = f"more{l}"
            names = ("meta", "idx", "gath", "turn", "xe", "gu_in", "dn_in", "gu", "silu", "gated", "gturn", "gt",
                     "dn", "y", "scat", "sp", "dve", "pool", "pool_end", "pe", "act")
            s = {k: (lasting if k in ("gath", "scat") else sem)(f"{n}_{k}") for k in names}
            gu, dn = pair[l][1]

            def run(eng, body, tick):
                count = eng.value_load(R["n_more_i"], min_val=0, max_val=MORE)
                with eng.If(count > 0):
                    with eng.Fori(0, count) as i:
                        body(i)
                        wait_alone(eng, s["scat"], 16 * i + 16, tick)

            with nc.Block() as block:
                @block.sync
                def _(sp):
                    def body(i):
                        e = sp.value_load(R["expert_i"][:, bass.ds(i, 1)], min_val=0, max_val=NE - 1)
                        row = sp.value_load(R["start_i"][:, bass.ds(i, 1)], min_val=0, max_val=NE * TABLE - SLOTS)
                        for u in range(2):
                            sp.dma_start(meta1[u * SLOTS:(u + 1) * SLOTS, :], table[bass.ds(row, SLOTS), :])\
                              .then_inc(s["meta"], 16)
                        sp.dma_start(gu[:, :].rearrange("p (e k n) -> p e k n", e=1, k=KD),
                                     A["moe_w_gu"][l][bass.ds(e, 1)].rearrange("e (k p) n -> p e k n", p=P))\
                          .then_inc(s["gu_in"], 16)
                        sp.dma_start(dn[:, :].rearrange("p (e k n) -> p e k n", e=1, k=FF // P),
                                     A["moe_w_down"][l][bass.ds(e, 1)].rearrange("e (k p) n -> p e k n", p=P))\
                          .then_inc(s["dn_in"], 16)
                    run(sp, body, s["sp"])

                @block.vector
                def _(dve):
                    def body(i):
                        dve.wait_ge(s["meta"], 32 * i + 32)
                        dve.scalar_tensor_tensor(take1[1], meta1[:, 0:1], 2.0, half_col[:, :], ALU.mult, ALU.add)\
                           .then_inc(s["idx"], 1)
                        dve.scalar_tensor_tensor(put1[1], meta1[:, 1:2], 2.0, half_col[:, :], ALU.mult, ALU.add)\
                           .then_inc(s["idx"], 1)
                        dve.wait_ge(s["silu"], i + 1)
                        times_up(dve, 1).then_inc(s["gated"], 1)
                        dve.wait_ge(s["gturn"], i + 1)
                        copy_gated(dve, 1).then_inc(s["gt"], 1)
                    run(dve, body, s["dve"])

                @block.gpsimd
                def _(pool):
                    def body(i):
                        wait_alone(pool, s["idx"], 2 * i + 2, s["pool"])
                        gather(pool, 1, take1[1], s["gath"])
                        wait_alone(pool, s["y"], i + 1, s["pool"])
                        scatter(pool, 1, put1[1], s["scat"])
                    run(pool, body, s["pool_end"])

                @block.tensor
                def _(pe):
                    def body(i):
                        pe.wait_ge(s["gath"], 16 * i + 16)
                        turn_gathered(pe, 1).then_inc(s["turn"], 1)
                        pe.wait_ge(s["xe"], i + 1)
                        pe.wait_ge(s["gu_in"], 16 * i + 16)
                        gate_up(pe, 1, three(gu[:, :], D)).then_inc(s["gu"], 1)
                        pe.wait_ge(s["gated"], i + 1)
                        turn_gated(pe, 1).then_inc(s["gturn"], 1)
                        pe.wait_ge(s["gt"], i + 1)
                        pe.wait_ge(s["dn_in"], 16 * i + 16)
                        down(pe, 1, three(dn[:, :], D)).then_inc(s["dn"], 1)
                    run(pe, body, s["pe"])

                @block.scalar
                def _(act):
                    def body(i):
                        act.wait_ge(s["turn"], i + 1)
                        copy_gathered(act, 1).then_inc(s["xe"], 1)
                        act.wait_ge(s["gu"], i + 1)
                        silu(act, 1).then_inc(s["silu"], 1)
                        act.wait_ge(s["dn"], i + 1)
                        act.wait_ge(s["meta"], 32 * i + 32)
                        act.activation(ys[1], PS[:, 7, :], ACT.Copy, scale=meta1[:, 2:3]).then_inc(s["y"], 1)
                    run(act, body, s["act"])
            Stages.end()

        Y0, Y1 = three(w3[:, :], D), three(w4[:, :], D)
        PTOK = three(w1[:, 0:T * PLE], PLE)
        PTR = three(w1[:, 1024:2048], SEQ)
        sig = [w2[:, b * NB:(b + 1) * NB] for b in range(3)]

        def load_injection(eng, l, s_wg, s_wp):
            eng.dma_start(three(pair[l][0][0][:, :], D), rows(A["ple_w_gate"][l], D)).then_inc(s_wg, 16)
            eng.dma_start(three(pair[l][0][1][:, 0:2 * D], D), rows(A["ple_w_proj"][l], D)).then_inc(s_wp, 16)

        def injection(l, s_wg, s_wp, loads, after_tile, turn_after):
            n = f"inj{l}"
            wg, wp = three(pair[l][0][0][:, :], D), three(pair[l][0][1][:, 0:2 * D], D)
            s_y = [sem(f"{n}_y{t}") for t in range(T)]
            s_p, s_pt, s_ptc = sem(f"{n}_p"), sem(f"{n}_pt"), sem(f"{n}_ptc")
            s_sum, s_unit, s_sig, s_done = sem(f"{n}_sum"), sem(f"{n}_unit"), sem(f"{n}_sig"), sem(f"{n}_done")
            norm = Norm(f"{n}_norm")
            turn = Turn(f"{n}_turn", lambda t: 0)
            turn2 = Turn(f"{n}_turn2", lambda t: 0) if turn_after else None
            y_tok = y_rows.rearrange("(j t u) c -> j t (u c)", j=2, u=2)
            U = 2 * T
            with nc.Block() as block:
                @block.sync
                def _(sp):
                    sp.dma_start(PTOK, A["p"][l, 0].rearrange("(t p) c -> p t c", p=P)).then_inc(s_p, 16)
                    for t in range(T):
                        for j, Y in enumerate((Y0, Y1)):
                            sp.dma_start(Y[:, t, :], y_tok[j, t * P:(t + 1) * P, :]).then_inc(s_y[t], 16)
                    loads(sp, norm)
                    after_tile(sp, s_done)

                @block.tensor
                def _(pe):
                    pe.wait_ge(s_p, 16)
                    for k in range(2):
                        for t in range(T):
                            m = pe.transpose(PS[:, 2 + k, t * P:(t + 1) * P], PTOK[:, t, k * P:(k + 1) * P],
                                             ident[:, :])
                    m.then_inc(s_pt, 1)
                    for t in range(T + 2):
                        if t < T:
                            pe.wait_ge(norm.done, t + 1)
                            if t >= 1:
                                turn.wait(pe, t - 1)
                            if t >= 3 and turn2:
                                turn2.wait(pe, t - 3)
                            turn.pe(pe, t)
                            turn.wait(pe, t)
                        if t >= 2 and turn2:
                            pe.wait_ge(s_done, 2 * (t - 1))
                            if t >= 3:
                                turn2.wait(pe, t - 3)
                            turn2.pe(pe, t - 2)
                        if t >= T:
                            continue
                        if t == 0:
                            pe.wait_ge(s_wg, 16)
                            pe.wait_ge(s_wp, 16)
                            pe.wait_ge(s_ptc, 2)
                        for c in range(2):
                            u = 2 * t + c
                            b = 2 + 2 * (u % 3)
                            if u >= 3:
                                pe.wait_ge(s_done, u - 2)
                            for k in range(KD):
                                pe.matmul(PS[:, b, :], XT[:, k, t * P:(t + 1) * P],
                                          wg[:, k, c * NB:(c + 1) * NB], start=(k == 0), stop=(k == KD - 1))
                            for k in range(2):
                                m = pe.matmul(PS[:, b + 1, :], PTR[:, k, t * P:(t + 1) * P],
                                              wp[:, k, c * NB:(c + 1) * NB], start=(k == 0), stop=(k == 1))
                            m.then_inc(s_unit, 1)

                @block.scalar
                def _(act):
                    act.wait_ge(s_pt, 1)
                    act.activation(PTR[:, 0, :], PS[:, 2, :], ACT.Copy).then_inc(s_ptc, 1)
                    for t in range(T + 2):
                        if t < T:
                            norm.act_tile(act, t)
                            turn.act(act, t)
                        if t >= 2 and turn2:
                            turn2.act(act, t - 2)
                        if 1 <= t <= T:
                            for c in range(2):
                                u = 2 * (t - 1) + c
                                act.wait_ge(s_unit, u + 1)
                                if u >= 3:
                                    act.wait_ge(s_done, u - 2)
                                act.activation(sig[u % 3], PS[:, 2 + 2 * (u % 3), :], ACT.Sigmoid).then_inc(s_sig, 1)

                @block.vector
                def _(dve):
                    own = Own(dve, f"{n}_own")
                    dve.wait_ge(s_pt, 1)
                    dve.tensor_copy(PTR[:, 1, :], PS[:, 3, :]).then_inc(s_ptc, 1)
                    dve.wait_ge(s_ln, 64 * l + 64)
                    for t in range(T + 2):
                        if t < T:
                            dve.wait_ge(s_y[t], 32)
                            own.done(dve.scalar_tensor_tensor(X[:, t, :], X[:, t, :], ALPHA, Y0[:, t, :],
                                                              ALU.mult, ALU.add))
                            own.done(dve.tensor_tensor(X[:, t, :], X[:, t, :], Y1[:, t, :], ALU.add))
                            norm.dve_tile(dve, own, t)
                            turn.dve(dve, t)
                        if t >= 2 and turn2:
                            turn2.dve(dve, t - 2)
                        if 1 <= t <= T:
                            for c in range(2):
                                u = 2 * (t - 1) + c
                                dve.wait_ge(s_sig, u + 1)
                                own.done(dve.tensor_tensor(sig[u % 3], sig[u % 3], PS[:, 3 + 2 * (u % 3), :],
                                                           ALU.mult))
                                xs = X[:, t - 1, c * NB:(c + 1) * NB]
                                dve.tensor_tensor(xs, xs, sig[u % 3], ALU.add).then_inc(s_done, 1)
            Stages.end()

        CW = three(wide[0][:, :], D)
        WKI = three(w4[:, 0:1024], P)
        WWI = three(w4[:, 1024:1088], IH)
        UQ, UK = three(slim[1][:, 0:2048], D), three(slim[1][:, 2048:4096], D)
        UV = three(slim[0][:, 2048:4096], D)
        CQ = three(w1[:, 0:2048], NB)
        CT = three(w1[:, 2048:4096], SEQ)
        QI = three(w2[:, 0:2048], SEQ)
        KI = w2[:, 2048:2560]
        WIT = w2[0:IH, 2560:3072]
        WI = three(w2[:, 3072:3104], IH)
        QH, KH = three(w3[:, :], SEQ), three(w4[:, :], SEQ)
        VH = three(XT[:, :, :].rearrange("p k s -> p (k s)"), D)
        squares = w2[:, 3104:3616]
        sq = w2[:, 3616:3632]
        s_cw, s_ki, s_up = lasting("s_cw"), lasting("s_ki"), lasting("s_up")
        s_uv, s_cwout = lasting("s_uv"), lasting("s_cwout")
        s_cgain = lasting("s_cgain")

        def load_latent_weights(sp):
            sp.dma_start(CW, rows(A["c_w_in"][0, :, 0:D], D)).then_inc(s_cw, 16)
            sp.dma_start(UQ, rows(A["c_w_uq"][0], D)).then_inc(s_up, 16)
            sp.dma_start(UK, rows(A["c_w_uk"][0].rearrange("c h d -> c (h d)"), D)).then_inc(s_up, 16)
            sp.dma_start(UV, rows(A["c_w_uv"][0].rearrange("c h d -> c (h d)"), D)).then_inc(s_uv, 16)

        def latents():
            n = "lat"
            s_full, s_sq, s_rms, s_cq = sem(f"{n}_full"), sem(f"{n}_sq"), sem(f"{n}_rms"), sem(f"{n}_cq")
            s_ft, s_fc = sem(f"{n}_ft"), sem(f"{n}_fc")
            s_ct, s_ctc = sem(f"{n}_ct"), sem(f"{n}_ctc")
            s_wi, s_wic = sem(f"{n}_wi"), sem(f"{n}_wic")
            with nc.Block() as block:
                @block.sync
                def _(sp):
                    base = D
                    for u in range(2):
                        sp.dma_start(WKI[:, :, u * HD:(u + 1) * HD], rows(A["c_w_in"][0, :, base:base + HD], HD))\
                          .then_inc(s_ki, 16)
                    sp.dma_start(WWI, rows(A["c_w_in"][0, :, base + HD:base + HD + IH], IH)).then_inc(s_ki, 16)
                    sp.dma_start(gains[:, 8:10], A["c_q_norm"][0].rearrange("(k p) -> p k", p=P)).then_inc(s_cgain, 16)
                    sp.dma_start(gains[:, 10:12], A["c_kv_norm"][0].rearrange("(k p) -> p k", p=P))\
                      .then_inc(s_cgain, 16)
                    sp.dma_start(three(wide[1][:, :], D), rows(A["c_w_out"][0], D)).then_inc(s_cwout, 16)

                @block.tensor
                def _(pe):
                    pe.wait_ge(s_cw, 16)
                    for t in range(T):
                        for k in range(KD):
                            m = pe.matmul(PS[:, t, :], XT[:, k, t * P:(t + 1) * P], CW[:, k, 0:NB],
                                          start=(k == 0), stop=(k == KD - 1))
                        m.then_inc(s_full, 1)
                    for c in range(4):
                        for k in range(KD):
                            m = pe.matmul(PS[:, 4 + c, :], CW[:, k, NB + c * P:NB + (c + 1) * P], XT[:, k, :],
                                          start=(k == 0), stop=(k == KD - 1))
                        m.then_inc(s_ft, 1)
                    pe.wait_ge(s_ki, 48)
                    pe.wait_ge(s_fc, 1)
                    for k in range(KD):
                        m = pe.matmul(PS[:, 4, :], WKI[:, k, :], XT[:, k, :], start=(k == 0), stop=(k == KD - 1))
                    m.then_inc(s_ft, 1)
                    pe.wait_ge(s_fc, 2)
                    for k in range(KD):
                        m = pe.matmul(PS[0:IH, 5, :], WWI[:, k, :], XT[:, k, :], start=(k == 0), stop=(k == KD - 1))
                    m.then_inc(s_ft, 1)
                    pe.wait_ge(s_cq, 2 * T)
                    for c in range(4):
                        for t in range(T):
                            m = pe.transpose(PS[:, c, t * P:(t + 1) * P], CQ[:, t, c * P:(c + 1) * P], ident[:, :])
                        m.then_inc(s_ct, 1)
                    pe.wait_ge(s_fc, 6)
                    for t in range(T):
                        m = pe.transpose(PS[:, 6, t * IH:(t + 1) * IH], WIT[:, t * P:(t + 1) * P], ident[0:IH, 0:IH])
                    m.then_inc(s_wi, 1)

                @block.scalar
                def _(act):
                    for t in range(T):
                        act.wait_ge(s_full, t + 1)
                        for u in range(2):
                            i = 2 * t + u
                            if i >= 1:
                                act.wait_ge(s_sq, i)
                            act.activation(squares[:, 0:RANK], PS[:, t, u * RANK:(u + 1) * RANK], ACT.Square,
                                           accum_out=sq[:, i:i + 1]).then_inc(s_sq, 1)
                    act.wait_ge(s_sq, 2 * T)
                    act.activation(sq[:, 8:16], sq[:, 0:8], ACT.Sqrt, bias=eps[:, 1:2], scale=1.0 / RANK)\
                       .then_inc(s_rms, 1)
                    for c, dst in enumerate([QI[:, 0, :], QI[:, 1, :], QI[:, 2, :], QI[:, 3, :], KI, WIT]):
                        act.wait_ge(s_ft, c + 1)
                        rows_of = IH if c == 5 else P
                        act.activation(dst, PS[0:rows_of, (4, 5, 6, 7, 4, 5)[c], :], ACT.Copy).then_inc(s_fc, 1)
                    act.wait_ge(s_cgain, 32)
                    for c in range(4):
                        act.wait_ge(s_ct, c + 1)
                        act.activation(CT[:, c, :], PS[:, c, :], ACT.Copy, scale=gains[:, 8 + c:9 + c])\
                           .then_inc(s_ctc, 1)
                    act.wait_ge(s_wi, 1)
                    act.activation(WI, three(PS[:, 6, 0:T * IH], IH), ACT.Copy).then_inc(s_wic, 1)

                @block.vector
                def _(dve):
                    own = Own(dve, f"{n}_own")
                    dve.wait_ge(s_rms, 1)
                    own.done(dve.reciprocal(sq[:, 8:16], sq[:, 8:16]))
                    for t in range(T):
                        for u in range(2):
                            dve.tensor_scalar(CQ[:, t, u * RANK:(u + 1) * RANK], PS[:, t, u * RANK:(u + 1) * RANK],
                                              sq[:, 8 + 2 * t + u:9 + 2 * t + u], None, ALU.mult).then_inc(s_cq, 1)
            Stages.end()

        SEL = list(range(1, T))
        width = [(t + 1) * P for t in range(T)]
        at = {1: 0, 2: 256, 3: 640}
        IS = {t: w1[:, at[t]:at[t] + width[t]] for t in SEL}
        WK = {t: slim[0][:, at[t]:at[t] + width[t]] for t in SEL}
        relu = [slim[0][:, 1152:1664], w2[:, 3584:4096]]
        m8 = [w2[:, 3200:3208], w2[:, 3208:3216]]
        DIST = w1[:, 1152:1664]
        s_dist = lasting("s_dist")

        def selection():
            n = "sel"
            job_owner = ["act"] * 24
            up = Jobs(f"{n}_up", job_owner)
            s_is, s_relu, s_acc, s_mask = sem(f"{n}_is"), sem(f"{n}_relu"), sem(f"{n}_acc"), sem(f"{n}_mask")
            units = [(t, h) for t in SEL for h in range(IH)]
            with nc.Block() as block:
                @block.sync
                def _(sp):
                    sp.dma_start(DIST, A["c_dist"]).then_inc(s_dist, 16)

                @block.tensor
                def _(pe):
                    for i, (t, h) in enumerate(units):
                        if i >= 2:
                            pe.wait_ge(s_relu, i - 1)
                        a = (h % 2) * HD
                        pe.matmul(PS[:, i % 2, 0:width[t]], QI[a:a + HD, h // 2, t * P:(t + 1) * P],
                                  KI[a:a + HD, 0:width[t]], start=True, stop=True).then_inc(s_is, 1)
                    pe.wait_ge(s_up, 32)
                    for j in range(24):
                        b = 2 + j % 6
                        if j >= 6:
                            up.wait_emptied(pe, j - 6)
                        if j == 16:
                            pe.wait_ge(s_uv, 16)
                        for k in range(2):
                            if j < 8:
                                lhsT, rhs = UQ[:, k, j * P:(j + 1) * P], CT[:, k, :]
                            elif j < 16:
                                lhsT, rhs = UK[:, k, (j - 8) * P:(j - 7) * P], CT[:, 2 + k, :]
                            else:
                                t, c = (j - 16) // 2, j % 2
                                lhsT, rhs = CT[:, 2 + k, t * P:(t + 1) * P], UV[:, k, c * NB:(c + 1) * NB]
                            m = pe.matmul(PS[:, b, :], lhsT, rhs, start=(k == 0), stop=(k == 1))
                        m.then_inc(up.full, 1)

                @block.scalar
                def _(act):
                    for i, (t, h) in enumerate(units):
                        act.wait_ge(s_is, i + 1)
                        if i >= 2:
                            act.wait_ge(s_acc, i - 1)
                        act.activation(relu[i % 2][:, 0:width[t]], PS[:, i % 2, 0:width[t]], ACT.Relu)\
                           .then_inc(s_relu, 1)
                    for j in range(24):
                        up.wait_full(act, j)
                        src = PS[:, 2 + j % 6, :]
                        if j < 8:
                            act.activation(QH[:, j, :], src, ACT.Copy, scale=HD ** -0.5).then_inc(up.sem_of(0), 1)
                        elif j < 16:
                            act.activation(KH[:, j - 8, :], src, ACT.Copy).then_inc(up.sem_of(0), 1)
                        else:
                            t, c = (j - 16) // 2, j % 2
                            act.activation(VH[:, t, c * NB:(c + 1) * NB], src, ACT.Copy).then_inc(up.sem_of(0), 1)

                @block.vector
                def _(dve):
                    own = Own(dve, f"{n}_own")
                    for i, (t, h) in enumerate(units):
                        dve.wait_ge(s_relu, i + 1)
                        r, w = relu[i % 2][:, 0:width[t]], WI[:, t, h:h + 1]
                        if h == 0:
                            dve.tensor_scalar(IS[t], r, w, None, ALU.mult).then_inc(s_acc, 1)
                        else:
                            dve.wait_ge(s_acc, i)
                            dve.scalar_tensor_tensor(IS[t], r, w, IS[t], ALU.mult, ALU.add).then_inc(s_acc, 1)
                    dve.wait_ge(s_dist, 16)
                    for t in SEL:
                        dve.wait_ge(s_mask, SEL.index(t) + 1)
                        for r in range(TOPK // 8):
                            cur = IS[t] if r == 0 else WK[t]
                            own.done(dve.max(m8[0], cur))
                            own.done(dve.match_replace(WK[t], m8[0], cur, LOWEST))
                        own.done(dve.tensor_tensor(IS[t], IS[t], WK[t], ALU.is_equal))
                        own.done(dve.scalar_tensor_tensor(IS[t], IS[t], BIG, DIST[:, SEQ - width[t]:SEQ],
                                                          ALU.mult, ALU.add))

                @block.gpsimd
                def _(pool):
                    for n_, t in enumerate(SEL):
                        pool.wait_ge(s_acc, IH * (n_ + 1))
                        d = IS[t][:, t * P:(t + 1) * P]
                        pool.affine_select(out=d, in_=d, compare_op=ALU.is_ge, fill=LOWEST, base=0,
                                           pattern=[[-1, P]], channel_multiplier=1).then_inc(s_mask, 1)
            Stages.end()

        DMASK = {t: IS[t] for t in SEL}
        DMASK[0] = DIST[:, SEQ - P:SEQ]
        LG = [w2[:, b * NB:(b + 1) * NB] for b in range(4)]
        PTS = [w2[:, 2048 + b * NB:2560 + b * NB] for b in range(2)]
        nmax = w2[:, 3072:3136]
        rsum = w2[:, 3136:3200]
        rden = w2[:, 3200:3264]
        OH_all = three(slim[0][:, :], D)

        def attention():
            n = "att"
            units = [(t, h) for t in range(T) for h in range(AH)]
            N = len(units)
            s_s, s_l, s_max, s_p = sem(f"{n}_s"), sem(f"{n}_l"), sem(f"{n}_max"), sem(f"{n}_p")
            s_pt, s_ptc, s_pv, s_o = sem(f"{n}_pt"), sem(f"{n}_ptc"), sem(f"{n}_pv"), sem(f"{n}_o")
            s_ot = sem(f"{n}_ot")
            mo = Jobs(f"{n}_mt", alternate(8))
            slope = [2.0 ** (-8.0 * (h + 1) / AH) for h in range(AH)]
            with nc.Block() as block:
                @block.tensor
                def _(pe):
                    for i in range(N + 2):
                        if i < N:
                            t, h = units[i]
                            a = (h % 2) * HD
                            if i >= 2:
                                pe.wait_ge(s_l, i - 1)
                            pe.matmul(PS[:, i % 2, 0:width[t]], QH[a:a + HD, h // 2, t * P:(t + 1) * P],
                                      KH[a:a + HD, h // 2, 0:width[t]], start=True, stop=True).then_inc(s_s, 1)
                        if 1 <= i <= N:
                            t, h = units[i - 1]
                            pe.wait_ge(s_p, i)
                            if i - 1 >= 2:
                                pe.wait_ge(s_ptc, i - 2)
                            for kb in range(t + 1):
                                m = pe.transpose(PS[:, 2 + (i - 1) % 2, kb * P:(kb + 1) * P],
                                                 LG[(i - 1) % 4][:, kb * P:(kb + 1) * P], ident[:, :])
                            m.then_inc(s_pt, 1)
                        if i >= 2:
                            t, h = units[i - 2]
                            pe.wait_ge(s_ptc, i - 1)
                            if t >= 2 and h == 0:
                                pe.wait_ge(s_o, t - 1)
                            for kb in range(t + 1):
                                m = pe.matmul(PS[:, 4 + 2 * (t % 2) + h // 8, (h % 8) * HD:(h % 8 + 1) * HD],
                                              PTS[(i - 2) % 2][:, kb * P:(kb + 1) * P],
                                              VH[:, kb, h * HD:(h + 1) * HD], start=(kb == 0), stop=(kb == t))
                            m.then_inc(s_pv, 1)
                    pe.wait_ge(s_o, T)
                    for k in range(KD):
                        for t in range(T):
                            m = pe.transpose(PS[:, k, t * P:(t + 1) * P], OH_all[:, t, k * P:(k + 1) * P],
                                             ident[:, :])
                        m.then_inc(mo.full, 1)

                @block.vector
                def _(dve):
                    def finish(t):
                        dve.wait_ge(s_pv, AH * (t + 1))
                        dve.wait_ge(s_p, AH * (t + 1))
                        own.done(dve.reciprocal(rden[:, AH * t:AH * t + AH], rsum[:, AH * t:AH * t + AH]))
                        b = 4 + 2 * (t % 2)
                        dve.tensor_tensor(OH_all[:, t, :].rearrange("p (h d) -> p h d", d=HD),
                                          PS[:, b:b + 2, :].rearrange("p b (h d) -> p (b h) d", d=HD),
                                          rden[:, AH * t:AH * t + AH].rearrange("p (h d) -> p h d", d=1)
                                          .broadcast_to([P, AH, HD]), ALU.mult).then_inc(s_o, 1)

                    own = Own(dve, f"{n}_own")
                    for i, (t, h) in enumerate(units):
                        dve.wait_ge(s_s, i + 1)
                        if i >= 4:
                            dve.wait_ge(s_pt, i - 3)
                        g = LG[i % 4][:, 0:width[t]]
                        dve.scalar_tensor_tensor(g, DMASK[t], -slope[h], PS[:, i % 2, 0:width[t]],
                                                 ALU.mult, ALU.add).then_inc(s_l, 1)
                        dve.wait_ge(s_l, i + 1)
                        dve.tensor_reduce(nmax[:, i:i + 1], g, AX.X, ALU.max, negate=True).then_inc(s_max, 1)
                        if h == 4 and t >= 1:
                            finish(t - 1)
                    finish(T - 1)
                    for j in range(8):
                        if mo.owners[j] == "dve":
                            mo.wait_full(dve, j)
                            dve.tensor_copy(MT[:, j, :], PS[:, j, :]).then_inc(mo.sem_of(j), 1)

                @block.scalar
                def _(act):
                    for i in range(N + 1):
                        if i < N:
                            t, h = units[i]
                            act.wait_ge(s_max, i + 1)
                            g = LG[i % 4][:, 0:width[t]]
                            act.activation(g, g, ACT.Exp, bias=nmax[:, i:i + 1],
                                           accum_out=rsum[:, i:i + 1]).then_inc(s_p, 1)
                        if i >= 1:
                            t, h = units[i - 1]
                            act.wait_ge(s_pt, i)
                            if i - 1 >= 2:
                                act.wait_ge(s_pv, i - 2)
                            act.activation(PTS[(i - 1) % 2][:, 0:width[t]], PS[:, 2 + (i - 1) % 2, 0:width[t]],
                                           ACT.Copy).then_inc(s_ptc, 1)
                    for j in range(8):
                        if mo.owners[j] == "act":
                            mo.wait_full(act, j)
                            act.activation(MT[:, j, :], PS[:, j, :], ACT.Copy).then_inc(mo.sem_of(j), 1)

                @block.sync
                def _(sp):
                    load_gu(sp, 1, 0, 0)
                    load_dn(sp, 1, 0, 0)
            Stages.end()

        s_wg = [lasting(f"s_wg{l}") for l in range(2)]
        s_wp = [lasting(f"s_wp{l}") for l in range(2)]
        s_out = lasting("s_out")

        def after_out(l):
            def then_load(sp, sums):
                sums.wait_full(sp, 7)
                load_gu(sp, l, 1, 1)
                load_dn(sp, l, 1, 1)
            return then_load

        def layer_end(l, loads, after_tile, turn_after):
            route(l)
            experts(l, lambda sp: load_injection(sp, l, s_wg[l], s_wp[l]))
            further_passes(l)
            injection(l, s_wg[l], s_wp[l], loads, after_tile, turn_after)

        def next_layer_loads(sp, norm):
            load_latent_weights(sp)
            norm_done = norm.done
            sp.wait_ge(norm_done, T)
            load_ln(sp, A["ln1_g"][1], A["ln1_b"][1], s_ln)

        def store_tiles(sp, s_done):
            for t in range(T):
                sp.wait_ge(s_done, 2 * t + 2)
                sp.dma_start(out[0, t * P:(t + 1) * P, :], X[:, t, :]).then_inc(s_out, 16)
            sp.wait_ge(s_out, 16 * T)

        out_projection(0, w_out0, s_wout, after_out(0))
        layer_end(0, next_layer_loads, lambda sp, s_done: None, True)
        latents()
        selection()
        attention()
        WO = three(wide[1][:, :], D)
        out_projection(1, [WO[:, :, 0:NB], WO[:, :, NB:D]], [s_cwout], after_out(1))
        layer_end(1, lambda sp, norm: None, store_tiles, False)


_INS = ['x', 'p', 'ab_w_in', 'ret_gn_g', 'pool_w', 'pool_scale', 'ab_w_out', 'c_w_in', 'c_q_norm', 'c_kv_norm',
        'c_w_uq', 'c_w_uk', 'c_w_uv', 'c_w_out', 'ln1_g', 'ln1_b', 'ln2_g', 'ln2_b', 'moe_w_group', 'moe_b_group',
        'moe_w_expert', 'moe_b_expert', 'moe_w_gu', 'moe_w_down', 'ple_w_gate', 'ple_w_proj']


def constants(np):
    f = np.float32
    p = np.arange(P)
    j = np.arange(SEQ)
    c = {"c_ident": np.eye(P), "c_tri": (p[:, None] < p[None, :]), "c_iota": np.tile(np.arange(NE), (P, 1)),
         "c_half": (p // SLOTS)[:, None], "c_tok": np.arange(T)[None, :] * P + p[:, None],
         "c_eps": np.tile([LN_EPS, RMS_EPS], (P, 1))}
    diff = j[None, :] - p[:, None]
    gamma = 1.0 - 2.0 ** (-5.0 - np.arange(RH))
    c["c_decay"] = np.where(diff[None] >= 0, gamma[:, None, None] ** np.maximum(diff, 0)[None] * P ** -0.5, 0.0)
    c["c_edge"] = np.array([[w / min(t + 1, w) for t in range(WMAX)] for w in WINDOWS])
    c["c_empty"] = np.tile([0.0, NOWHERE, 0.0, 0.0], (P, NB // 4))
    e, b = np.meshgrid(np.arange(NE), np.arange(1, 8), indexing="ij")
    c["c_more"] = np.stack([(NE * TABLE - (TABLE * e + SLOTS * b)).ravel(), (SLOTS * b).ravel()])
    dist = (SEQ - P) + p[:, None] - j[None, :]
    c["c_dist"] = np.where(dist >= 0, dist, BIG)
    return {k: np.ascontiguousarray(v.astype(f)) for k, v in c.items()}


def kernel(**inputs):
    import numpy as _np
    import concourse.bacc as _bacc
    from concourse import mybir as _mybir
    from concourse.bass_utils import run_bass_kernel_spmd as _run

    nc = _bacc.Bacc("TRN2", target_bir_lowering=False, num_devices=1)
    arrays, args = {}, {}
    given = {name: _np.ascontiguousarray(inputs[name]) for name in _INS}
    given.update(constants(_np))
    for name, a in given.items():
        arrays[f"in_{name}"] = a
        args[name] = nc.dram_tensor(f"in_{name}", a.shape, _mybir.dt.from_np(a.dtype), kind="ExternalInput").ap()
    out = nc.dram_tensor("out", (1, SEQ, D), _mybir.dt.float32, kind="ExternalOutput").ap()
    build(nc, args, out)
    r = _run(nc, [arrays], core_ids=[0])
    return r.results[0]["out"]
```

```python
from contextlib import ExitStack

import concourse.bass as bass
from concourse import mybir

F32 = mybir.dt.float32
BF16 = mybir.dt.bfloat16
U32 = mybir.dt.uint32
I32 = mybir.dt.int32
ALU = mybir.AluOpType
ACT = mybir.ActivationFunctionType
AX = mybir.AxisListType

P = 128
SEQ = 512
D = 1024
T = SEQ // P
KD = D // P
NB = 512
PLE = 256
RH = 4
WINDOWS = (2, 4, 8, 16)
WMAX = WINDOWS[-1]
AH, HD = 16, 64
RANK = 256
IH = 8
TOPK = min(256, SEQ // 4)
NG, EPG = 4, 8
NE = NG * EPG
FF = 512
SLOTS = 64
TABLE = SEQ
MORE = (2 * SEQ) // (SLOTS + 1)
NOWHERE = 4 * SEQ
ALPHA = 4.0 ** 0.25
LN_EPS = 1e-5
RMS_EPS = 1e-6
BIG = 1e30
LOWEST = -3.0e38


def build(nc, A, out):
    ctx = ExitStack()
    ctx.enter_context(nc.allow_non_contiguous_dma(reason="small vectors to one feature per partition"))
    with ctx:
        def sb(name, shape, dt=F32):
            return ctx.enter_context(nc.sbuf_tensor(name, shape, dt))

        def lasting(name):
            return ctx.enter_context(nc.semaphore(name))

        class Stages:

            now, cleared = [], []

            @staticmethod
            def new(name):
                s = nc.alloc_semaphore(name)
                Stages.now.append(s)
                return s

            @staticmethod
            def end():
                for s in Stages.cleared:
                    nc.release_semaphore(s)
                for s in Stages.now:
                    nc.gpsimd.sem_clear(s)
                Stages.now, Stages.cleared = [], Stages.now

        sem = Stages.new

        def dram(name, shape):
            return nc.dram_tensor(name, shape, F32, kind="Internal").ap()

        def three(ap, b):
            return ap.rearrange("p (a b) -> p a b", b=b)

        wide = [sb("wide0", [P, KD * D]), sb("wide1", [P, KD * D])]
        slim = [sb("slim0", [P, T * D]), sb("slim1", [P, T * D])]
        X = sb("X", [P, T, D])
        XT = sb("XT", [P, KD, SEQ])
        w1 = sb("w1", [P, 4096])
        w2 = sb("w2", [P, 4096])
        w3 = sb("w3", [P, 4096])
        w4 = sb("w4", [P, 4096])
        ln_g = sb("ln_g", [P, D])
        ln_b = sb("ln_b", [P, D])
        ident = sb("ident", [P, P])
        tri = sb("tri", [P, P], BF16)
        ones = sb("ones", [P, P], BF16)
        eps = sb("eps", [P, 2])
        iota = sb("iota", [P, NE])
        half_col = sb("half_col", [P, 1])
        tok_col = sb("tok_col", [P, T])
        gains = sb("gains", [P, 16])
        dist = sb("dist", [P, SEQ])
        stats = sb("stats", [P, 16, 6])
        mv = sb("mv", [P, 16, 2])
        rstd = sb("rstd", [P, 16])
        PS = ctx.enter_context(nc.psum_tensor("PS", [P, 8, NB], F32))

        x_rows = dram("x_rows", [SEQ, D])
        y_rows = dram("y_rows", [2 * SEQ * 2, NB])
        table = dram("table", [NE * TABLE, 4])

        class Jobs:

            def __init__(self, name, owners):
                self.owners = owners
                self.full = sem(f"{name}_full")
                self.emptied = {o: sem(f"{name}_by_{o}") for o in sorted(set(owners))}

            def wait_full(self, eng, j):
                eng.wait_ge(self.full, j + 1)

            def wait_emptied(self, eng, j):
                o = self.owners[j]
                eng.wait_ge(self.emptied[o], self.owners[:j + 1].count(o))

            def wait_all_emptied(self, eng):
                for o, s in self.emptied.items():
                    eng.wait_ge(s, self.owners.count(o))

            def sem_of(self, j):
                return self.emptied[self.owners[j]]

        class Own:

            def __init__(self, eng, name):
                self.eng, self.sem, self.n = eng, sem(name), 0

            def done(self, ins):
                self.n += 1
                ins.then_inc(self.sem, 1)
                self.eng.wait_ge(self.sem, self.n)

            def mark(self, ins):
                self.n += 1
                ins.then_inc(self.sem, 1)

            def wait(self):
                self.eng.wait_ge(self.sem, self.n)

        class Turn:

            def __init__(self, name, bank):
                self.full, self.by_act, self.by_dve = sem(f"{name}_full"), sem(f"{name}_by_act"), sem(f"{name}_by_dve")
                self.bank = bank

            def pe(self, pe, t):
                for k in range(KD):
                    m = pe.transpose(PS[:, self.bank(t) + k // 4, (k % 4) * P:(k % 4 + 1) * P],
                                     X[:, t, k * P:(k + 1) * P], ident[:, :])
                m.then_inc(self.full, 1)

            def act(self, act, t):
                act.wait_ge(self.full, t + 1)
                act.activation(XT[:, 0:4, t * P:(t + 1) * P], three(PS[:, self.bank(t), :], P), ACT.Copy)\
                   .then_inc(self.by_act, 1)

            def dve(self, dve, t):
                dve.wait_ge(self.full, t + 1)
                dve.tensor_copy(XT[:, 4:8, t * P:(t + 1) * P], three(PS[:, self.bank(t) + 1, :], P))\
                   .then_inc(self.by_dve, 1)

            def wait(self, eng, t):
                eng.wait_ge(self.by_act, t + 1)
                eng.wait_ge(self.by_dve, t + 1)

        def alternate(n):
            return ["act" if j % 2 == 0 else "dve" for j in range(n)]

        class Norm:

            def __init__(self, name):
                self.var, self.std, self.done = sem(f"{name}_var"), sem(f"{name}_std"), sem(f"{name}_done")
                self.name = name

            def dve_tile(self, dve, own, t):
                for c in range(2):
                    own.mark(dve.bn_stats(stats[:, 2 * t + c, :], X[:, t, c * NB:(c + 1) * NB]))
                own.wait()
                dve.bn_aggr(mv[:, t, :], stats[:, 2 * t:2 * t + 2, :]).then_inc(self.var, 1)
                dve.wait_ge(self.std, t + 1)
                own.done(dve.reciprocal(rstd[:, t:t + 1], rstd[:, 8 + t:9 + t]))
                own.done(dve.tensor_scalar(X[:, t, :], X[:, t, :], mv[:, t, 0:1], rstd[:, t:t + 1],
                                           ALU.subtract, ALU.mult))
                own.done(dve.tensor_tensor(X[:, t, :], X[:, t, :], ln_g[:, :], ALU.mult))
                dve.tensor_tensor(X[:, t, :], X[:, t, :], ln_b[:, :], ALU.add).then_inc(self.done, 1)

            def act_tile(self, act, t):
                act.wait_ge(self.var, t + 1)
                act.activation(rstd[:, 8 + t:9 + t], mv[:, t, 1:2], ACT.Sqrt, bias=eps[:, 0:1])\
                   .then_inc(self.std, 1)

        def load_ln(eng, g, b, s):
            eng.dma_start(ln_g[:, :], g.partition_broadcast(P)).then_inc(s, 16)
            eng.dma_start(ln_b[:, :], b.partition_broadcast(P)).then_inc(s, 16)

        def rows(w, n):
            return w.rearrange("(k p) n -> p k n", p=P)

        pair = [[(wide[1], slim[0]), (wide[0], slim[1])],
                [(wide[0], slim[1]), (wide[1], slim[0])]]
        gu_in = [[lasting(f"gu_in{l}{q}") for q in range(2)] for l in range(2)]
        dn_in = [[lasting(f"dn_in{l}{q}") for q in range(2)] for l in range(2)]

        def load_gu(eng, l, q, e):
            src = A["moe_w_gu"][l][bass.ds(e, 1)]
            eng.dma_start(pair[l][q][0][:, :].rearrange("p (e k n) -> p e k n", e=1, k=KD),
                          src.rearrange("e (k p) n -> p e k n", p=P)).then_inc(gu_in[l][q], 16)

        def load_dn(eng, l, q, e):
            src = A["moe_w_down"][l][bass.ds(e, 1)]
            eng.dma_start(pair[l][q][1][:, :].rearrange("p (e k n) -> p e k n", e=1, k=FF // P),
                          src.rearrange("e (k p) n -> p e k n", p=P)).then_inc(dn_in[l][q], 16)


        s_x = [lasting(f"s_x{t}") for t in range(T)]
        s_const = lasting("s_const")
        s_ident = lasting("s_ident")
        s_bf = lasting("s_bf")
        s_w = [lasting(f"s_w_in{c}") for c in range(5)]
        s_wout = [lasting(f"s_wout{c}") for c in range(2)]
        s_ln = lasting("s_ln")
        s_gain = lasting("s_gain")
        s_dec = lasting("s_dec")
        s_pool = lasting("s_pool")

        w_in = [three(a, NB) for a in (wide[0][:, 0:4096], wide[0][:, 4096:8192], wide[1][:, 0:4096],
                                       wide[1][:, 4096:8192], slim[0][:, :])]
        QT, KT = three(w1[:, 0:2048], SEQ), three(w1[:, 2048:4096], SEQ)
        V, SG = three(w2[:, 0:2048], NB), three(w2[:, 2048:4096], NB)
        UT, DEC = three(w3[:, 0:2048], SEQ), three(w3[:, 2048:4096], SEQ)
        tri32 = w4[:, 3000:3128]
        w_out0 = [three(slim[1][:, :], NB), three(wide[0][:, 0:4096], NB)]

        turn_x = Turn("turn_x", lambda t: 2 * t)
        pj_owner = alternate(8) + ["dve"] * 4 + ["act"] * 4 + alternate(4)
        pj = Jobs("proj", pj_owner)
        PROJ = len(pj_owner)

        with nc.Block() as block:
            @block.sync
            def _(sp):
                for t in range(T):
                    sp.dma_start(X[:, t, :], A["x"][0, t * P:(t + 1) * P, :]).then_inc(s_x[t], 16)
                for c in range(5):
                    sp.dma_start(w_in[c], rows(A["ab_w_in"][0, :, c * NB:(c + 1) * NB], NB)).then_inc(s_w[c], 16)
                sp.dma_start(DEC, A["c_decay"].rearrange("h p n -> p h n")).then_inc(s_dec, 16)
                sp.dma_start(w_out0[0], rows(A["ab_w_out"][0, :, 0:NB], NB)).then_inc(s_wout[0], 16)

            @block.gpsimd
            def _(pool):
                pool.memset(ones[:, :], 1.0).then_inc(s_bf, 1)
                pool.wait_ge(s_const, 80)
                pool.tensor_copy(tri[:, :], tri32).then_inc(s_bf, 1)
                pool.wait_ge(s_bf, 2)

            @block.scalar
            def _(act):
                act.dma_start(ident[:, :], A["c_ident"]).then_inc(s_ident, 16)
                act.dma_start(tri32, A["c_tri"]).then_inc(s_const, 16)
                act.dma_start(iota[:, :], A["c_iota"]).then_inc(s_const, 16)
                act.dma_start(half_col[:, :], A["c_half"]).then_inc(s_const, 16)
                act.dma_start(tok_col[:, :], A["c_tok"]).then_inc(s_const, 16)
                act.dma_start(eps[:, :], A["c_eps"]).then_inc(s_const, 16)
                load_ln(act, A["ln1_g"][0], A["ln1_b"][0], s_ln)
                act.dma_start(gains[:, 0:4], A["ret_gn_g"][0].rearrange("(k p) -> p k", p=P)).then_inc(s_gain, 16)
                act.dma_start(gains[:, 4:8], A["pool_scale"][0].rearrange("(k p) -> p k", p=P)).then_inc(s_gain, 16)
                for t in range(T):
                    turn_x.act(act, t)
                for j in range(PROJ):
                    if pj_owner[j] != "act":
                        continue
                    pj.wait_full(act, j)
                    dst = (QT, KT, V, SG, UT)[j // 4][:, j % 4, :]
                    act.activation(dst, PS[:, j % 8, :], ACT.Silu if j // 4 == 3 else ACT.Copy)\
                       .then_inc(pj.sem_of(j), 1)

            @block.vector
            def _(dve):
                for t in range(T):
                    turn_x.dve(dve, t)
                for j in range(PROJ):
                    if pj_owner[j] != "dve":
                        continue
                    pj.wait_full(dve, j)
                    dst = (QT, KT, V, SG, UT)[j // 4][:, j % 4, :]
                    dve.tensor_copy(dst, PS[:, j % 8, :]).then_inc(pj.sem_of(j), 1)

            @block.tensor
            def _(pe):
                pe.wait_ge(s_ident, 16)
                for t in range(T):
                    pe.wait_ge(s_x[t], 16)
                    turn_x.pe(pe, t)
                turn_x.wait(pe, T - 1)
                for j in range(PROJ):
                    c, i = j // 4, j % 4
                    if i == 0:
                        pe.wait_ge(s_w[c], 16)
                    if j >= 8:
                        pj.wait_emptied(pe, j - 8)
                    for k in range(KD):
                        if c in (2, 3):
                            lhsT, rhs = XT[:, k, i * P:(i + 1) * P], w_in[c][:, k, :]
                        else:
                            lhsT, rhs = w_in[c][:, k, i * P:(i + 1) * P], XT[:, k, :]
                        m = pe.matmul(PS[:, j % 8, :], lhsT, rhs, start=(k == 0), stop=(k == KD - 1))
                    m.then_inc(pj.full, 1)
        Stages.end()

        ST = [[w4[:, b * 1280 + o:b * 1280 + o + n] for o, n in ((0, 512), (512, 384), (896, 256), (1152, 128))]
              for b in range(2)]
        RN = three(wide[0][:, 4096:6144], NB)
        PW = three(wide[0][:, 6144:6656], P)
        EDGE = three(w4[:, 2560:2624], WMAX)
        DT = three(w1[:, 0:2048], SEQ)
        TMP = [w3[:, 2048:2560], w3[:, 2560:3072]]
        MT = XT

        s_score = sem("s_score")
        s_st = sem("s_st")
        s_o = sem("s_o")
        s_gvar = sem("s_gvar")
        s_gstd = sem("s_gstd")
        s_rn = sem("s_rn")
        s_dt = sem("s_dt")
        s_edge = lasting("s_edge")
        mt = Jobs("mixed", ["act"] * 8)

        with nc.Block() as block:
            @block.sync
            def _(sp):
                sp.dma_start(PW, A["pool_w"][0].rearrange("g c d -> c g d")).then_inc(s_pool, 16)
                sp.dma_start(w4[:, 2560:2624], A["c_edge"].rearrange("g n -> (g n)").partition_broadcast(P))\
                  .then_inc(s_edge, 16)
                sp.dma_start(w_out0[1], rows(A["ab_w_out"][0, :, NB:D], NB)).then_inc(s_wout[1], 16)
                load_gu(sp, 0, 0, 0)
                load_dn(sp, 0, 0, 0)

            @block.tensor
            def _(pe):
                for h in range(RH):
                    for kb in range(T):
                        if h >= 1:
                            pe.wait_ge(s_st, 4 * (h - 1) + kb + 1)
                        pe.matmul(PS[:, 4 + kb, 0:SEQ - kb * P], KT[:, h, kb * P:(kb + 1) * P],
                                  QT[:, h, kb * P:SEQ], start=True, stop=True).then_inc(s_score, 1)
                    pe.wait_ge(s_st, 4 * h + 4)
                    for t in range(T):
                        for kb in range(t + 1):
                            m = pe.matmul(PS[:, t, h * P:(h + 1) * P], ST[h % 2][kb][:, (t - kb) * P:(t - kb + 1) * P],
                                          V[:, kb, h * P:(h + 1) * P], start=(kb == 0), stop=(kb == t))
                    m.then_inc(s_o, 1)
                pe.wait_ge(s_pool, 16)
                for g in range(4):
                    pe.wait_ge(s_dt, g + 1)
                    pe.matmul(PS[:, 4 + g, :], PW[:, g, :], DT[:, g, :], start=True, stop=True)\
                      .then_inc(mt.full, 1)
                pe.wait_ge(s_rn, T)
                for h in range(RH):
                    for t in range(T):
                        m = pe.transpose(PS[:, h, t * P:(t + 1) * P], RN[:, t, h * P:(h + 1) * P], ident[:, :])
                    m.then_inc(mt.full, 1)

            @block.vector
            def _(dve):
                own = Own(dve, "own_ret")
                dve.wait_ge(s_dec, 16)
                for h in range(RH):
                    for kb in range(T):
                        dve.wait_ge(s_score, 4 * h + kb + 1)
                        if h >= 2 and kb == 0:
                            dve.wait_ge(s_o, h - 1)
                        n = SEQ - kb * P
                        dve.tensor_tensor(ST[h % 2][kb], PS[:, 4 + kb, 0:n], DEC[:, h, 0:n], ALU.mult)\
                           .then_inc(s_st, 1)
                dve.wait_ge(s_st, 4 * RH)
                dve.wait_ge(s_o, RH)
                dve.wait_ge(s_edge, 16)
                for g, w in enumerate(WINDOWS):
                    src, n, b = UT[:, g, :], 1, 0
                    while n < w:
                        dst = TMP[b]
                        own.mark(dve.tensor_copy(dst[:, 0:n], src[:, 0:n]))
                        own.done(dve.tensor_tensor(dst[:, n:SEQ], src[:, n:SEQ], src[:, 0:SEQ - n], ALU.add))
                        src, n, b = dst, 2 * n, 1 - b
                    own.done(dve.tensor_tensor(src[:, 0:WMAX], src[:, 0:WMAX], EDGE[:, g, :], ALU.mult))
                    dve.scalar_tensor_tensor(DT[:, g, :], src, 1.0 / w, UT[:, g, :], ALU.mult, ALU.subtract)\
                       .then_inc(s_dt, 1)
                    dve.wait_ge(s_dt, g + 1)
                for i in range(T * RH):
                    own.mark(dve.bn_stats(stats[:, i, :], PS[:, i // RH, (i % RH) * P:(i % RH + 1) * P]))
                own.wait()
                for i in range(T * RH):
                    m = dve.bn_aggr(mv[:, i, :], stats[:, i, :])
                m.then_inc(s_gvar, 1)
                dve.wait_ge(s_gstd, 1)
                own.done(dve.reciprocal(rstd[:, :], rstd[:, :]))
                for t in range(T):
                    for h in range(RH):
                        i = t * RH + h
                        own.mark(dve.tensor_scalar(RN[:, t, h * P:(h + 1) * P], PS[:, t, h * P:(h + 1) * P],
                                                   mv[:, i, 0:1], rstd[:, i:i + 1], ALU.subtract, ALU.mult))
                    own.wait()
                    dve.tensor_tensor(RN[:, t, :], RN[:, t, :], SG[:, t, :], ALU.mult).then_inc(s_rn, 1)

            @block.scalar
            def _(act):
                act.wait_ge(s_const, 80)
                act.wait_ge(s_gain, 32)
                for g in range(4):
                    mt.wait_full(act, g)
                    act.activation(MT[:, 4 + g, :], PS[:, 4 + g, :], ACT.Copy, scale=gains[:, 4 + g:5 + g])\
                       .then_inc(mt.sem_of(g), 1)
                act.wait_ge(s_gvar, 1)
                act.activation(rstd[:, :], mv[:, :, 1], ACT.Sqrt, bias=eps[:, 0:1]).then_inc(s_gstd, 1)
                for h in range(RH):
                    mt.wait_full(act, 4 + h)
                    act.activation(MT[:, h, :], PS[:, h, :], ACT.Copy, scale=gains[:, h:h + 1])\
                       .then_inc(mt.sem_of(4 + h), 1)
        Stages.end()

        def route_views():
            at, views = [0], {}

            def take(name, *shape, rows=P, dt=F32):
                n = 1
                for s in shape:
                    n *= s
                words = n if dt != BF16 else n // 2
                ap = w1[0:rows, at[0]:at[0] + words]
                at[0] += words
                if dt != F32:
                    ap = ap.bitcast(dt)
                views[name] = three(ap, shape[1]) if len(shape) == 2 else ap
                return ap

            take("WR", KD, NG + NE)
            take("LT", SEQ, rows=NG + NE)
            take("L", T, NG + NE)
            for name in ("G8", "gtop", "etop", "es", "gexp"):
                take(name, T, EPG)
            take("gidx", T, EPG, dt=U32)
            take("eidx", T, EPG, dt=U32)
            take("ohg", T, NG)
            for name in ("gf", "gsum", "ngmax", "gw", "diff", "ex", "ex1"):
                take(name, T)
            for name in ("ef", "pos", "gate"):
                take(name, 2, T)
            take("place_f", 2 * T)
            take("place", 2 * T, dt=U32)
            take("entry", 2 * T, 4)
            take("oh0", T, NE)
            take("oh1", T, NE)
            take("junk", NE)
            take("M", T, NE, dt=BF16)
            take("bias", 1, rows=NG + NE)
            take("meta", NE, 4)
            take("taken", NE, dt=U32)
            take("put", NE, dt=U32)
            take("gate_of", NE)
            take("empty", NB)
            for name in ("cnt",):
                take(name, NE, rows=1)
            for name in ("more_key", "more_min", "flags", "keys"):
                take(name, NE * 7, rows=1)
            take("top", 16, rows=1)
            take("start_i", 16, rows=1, dt=I32)
            take("expert_i", 16, rows=1, dt=I32)
            take("n_more", 1, rows=1)
            take("n_more_i", 1, rows=1, dt=I32)
            assert at[0] <= 4096
            return views

        R = route_views()

        def out_projection(l, mixed, w_halves, w_sems, load_first, then_load):
            n = f"out{l}"
            sums = Jobs(f"{n}_sum", ["dve"] * 8)
            norm = Norm(f"{n}_norm")
            turn = Turn(f"{n}_turn", lambda t: 2 * t)
            s_rows = sem(f"{n}_rows")
            s_wr, s_more, s_empty = sem(f"{n}_router_w"), sem(f"{n}_more"), sem(f"{n}_empty")
            with nc.Block() as block:
                @block.tensor
                def _(pe):
                    for s in w_sems:
                        pe.wait_ge(s, 16)
                    for t in range(T + 2):
                        if t < T:
                            for c in range(2):
                                for k in range(KD):
                                    m = pe.matmul(PS[:, 2 * t + c, :], mixed[:, k, t * P:(t + 1) * P],
                                                  w_halves[c][:, k, :], start=(k == 0), stop=(k == KD - 1))
                                m.then_inc(sums.full, 1)
                        if t >= 2:
                            pe.wait_ge(norm.done, t - 1)
                            turn.pe(pe, t - 2)

                @block.vector
                def _(dve):
                    own = Own(dve, f"{n}_own")
                    dve.wait_ge(s_ln, 64 * l + 32)
                    for t in range(T + 1):
                        if t < T:
                            for c in range(2):
                                sums.wait_full(dve, 2 * t + c)
                                xs = X[:, t, c * NB:(c + 1) * NB]
                                dve.scalar_tensor_tensor(xs, xs, ALPHA, PS[:, 2 * t + c, :], ALU.mult, ALU.add)\
                                   .then_inc(sums.sem_of(0), 1)
                            sums.wait_emptied(dve, 2 * t + 1)
                            norm.dve_tile(dve, own, t)
                        if t >= 1:
                            turn.dve(dve, t - 1)

                @block.scalar
                def _(act):
                    for t in range(T + 1):
                        if t < T:
                            norm.act_tile(act, t)
                        if t >= 1:
                            turn.act(act, t - 1)

                @block.sync
                def _(sp):
                    load_first(sp)
                    sp.dma_start(R["WR"][:, :, 0:NG], rows(A["moe_w_group"][l], NG)).then_inc(s_wr, 16)
                    sp.dma_start(R["WR"][:, :, NG:NG + NE], rows(A["moe_w_expert"][l], NE)).then_inc(s_wr, 16)
                    sp.dma_start(R["bias"][0:NG, :], A["moe_b_group"][l].rearrange("(n a) -> n a", a=1))\
                      .then_inc(s_wr, 16)
                    sp.dma_start(R["bias"][NG:NG + NE, :], A["moe_b_expert"][l].rearrange("(n a) -> n a", a=1))\
                      .then_inc(s_wr, 16)
                    sp.dma_start(R["more_key"], A["c_more"][0:1, :]).then_inc(s_more, 16)
                    sp.dma_start(R["more_min"], A["c_more"][1:2, :]).then_inc(s_more, 16)
                    sp.dma_start(R["empty"], A["c_empty"]).then_inc(s_empty, 16)
                    sp.wait_ge(s_empty, 16)
                    sp.dma_start(table.rearrange("(p s) c -> p (s c)", p=P), R["empty"]).then_inc(s_empty, 16)
                    for t in range(T):
                        sp.wait_ge(norm.done, t + 1)
                        sp.dma_start(x_rows[t * P:(t + 1) * P, :], X[:, t, :]).then_inc(s_rows, 16)
                    load_ln(sp, A["ln2_g"][l], A["ln2_b"][l], s_ln)
                    then_load(sp, sums)
                    sp.wait_ge(s_rows, 16 * T)
                    sp.wait_ge(s_wr, 64)
                    sp.wait_ge(s_more, 32)
                    sp.wait_ge(s_empty, 32)
            Stages.end()

        LP = three(PS[:, 1, 0:T * (NG + NE)], NG + NE)
        RK = three(PS[:, 2, 0:T * NE], NE)
        CP = PS[0:1, 3, 0:NE]

        def route(l):
            n = f"route{l}"
            s_lt, s_lts, s_l = sem(f"{n}_lt"), sem(f"{n}_lts"), sem(f"{n}_l")
            s_gmax, s_gexp, s_diff, s_ex = sem(f"{n}_gmax"), sem(f"{n}_gexp"), sem(f"{n}_diff"), sem(f"{n}_ex")
            s_member, s_rank, s_entry = sem(f"{n}_member"), sem(f"{n}_rank"), sem(f"{n}_entry")
            s_tab, s_meta, s_zero = lasting(f"{n}_tab"), sem(f"{n}_meta"), sem(f"{n}_zero")
            OH = (R["oh0"], R["oh1"])
            with nc.Block() as block:
                @block.tensor
                def _(pe):
                    for k in range(KD):
                        m = pe.matmul(PS[0:NG + NE, 0, :], R["WR"][:, k, :], XT[:, k, :],
                                      start=(k == 0), stop=(k == KD - 1))
                    m.then_inc(s_lt, 1)
                    pe.wait_ge(s_lts, 1)
                    for t in range(T):
                        m = pe.transpose(LP[:, t, :], R["LT"][:, t * P:(t + 1) * P], ident[0:NG + NE, 0:NG + NE])
                    m.then_inc(s_l, 1)
                    pe.wait_ge(s_member, 1)
                    for t in range(T):
                        for u in range(t):
                            pe.matmul(RK[:, t, :], ones[:, :], R["M"][:, u, :], start=(u == 0), stop=False)
                        pe.matmul(RK[:, t, :], tri[:, :], R["M"][:, t, :], start=(t == 0), stop=True)
                    for t in range(T):
                        m = pe.matmul(CP, ones[:, 0:1], R["M"][:, t, :], start=(t == 0), stop=(t == T - 1))
                    m.then_inc(s_rank, 1)

                @block.scalar
                def _(act):
                    act.wait_ge(s_lt, 1)
                    act.activation(R["LT"], PS[0:NG + NE, 0, :], ACT.Identity, bias=R["bias"]).then_inc(s_lts, 1)
                    act.wait_ge(s_gmax, 1)
                    for t in range(T):
                        m = act.activation(R["gexp"][:, t, :], R["G8"][:, t, :], ACT.Exp,
                                           bias=R["ngmax"][:, t:t + 1], accum_out=R["gsum"][:, t:t + 1])
                        m.then_inc(s_gexp, 1)
                    act.wait_ge(s_diff, 1)
                    act.activation(R["ex"], R["diff"], ACT.Exp).then_inc(s_ex, 1)

                @block.vector
                def _(dve):
                    own = Own(dve, f"{n}_own")
                    L, G8, es, ef, gf = R["L"], R["G8"], R["es"], R["ef"], R["gf"]
                    entry = R["entry"]
                    own.mark(dve.memset(G8, -BIG))
                    own.mark(dve.memset(entry, 0.0))
                    own.mark(dve.memset(es, 0.0))
                    own.wait()
                    dve.wait_ge(s_l, 1)
                    own.mark(dve.tensor_copy(L, LP))
                    own.done(dve.tensor_copy(G8[:, :, 0:NG], LP[:, :, 0:NG]))
                    for t in range(T):
                        own.mark(dve.max(R["gtop"][:, t, :], G8[:, t, :]))
                    own.wait()
                    dve.tensor_scalar(R["ngmax"], R["gtop"][:, :, 0], -1.0, None, ALU.mult).then_inc(s_gmax, 1)
                    for t in range(T):
                        own.mark(dve.max_index(R["gidx"][:, t, :], R["gtop"][:, t, :], G8[:, t, :]))
                    own.wait()
                    own.done(dve.tensor_copy(gf, R["gidx"][:, :, 0]))
                    for t in range(T):
                        own.mark(dve.tensor_scalar(R["ohg"][:, t, :], iota[:, 0:NG], gf[:, t:t + 1], None,
                                                   ALU.is_equal))
                    for g in range(NG):
                        own.wait()
                        for t in range(T):
                            c = NG + g * EPG
                            own.mark(dve.scalar_tensor_tensor(es[:, t, :], L[:, t, c:c + EPG],
                                                              R["ohg"][:, t, g:g + 1], es[:, t, :],
                                                              ALU.mult, ALU.add))
                    own.wait()
                    for t in range(T):
                        own.mark(dve.max(R["etop"][:, t, :], es[:, t, :]))
                    own.wait()
                    dve.tensor_tensor(R["diff"], R["etop"][:, :, 1], R["etop"][:, :, 0], ALU.subtract)\
                       .then_inc(s_diff, 1)
                    for t in range(T):
                        own.mark(dve.max_index(R["eidx"][:, t, :], R["etop"][:, t, :], es[:, t, :]))
                    own.wait()
                    for j in range(2):
                        own.mark(dve.tensor_copy(ef[:, j, :], R["eidx"][:, :, j]))
                    own.wait()
                    for j in range(2):
                        own.mark(dve.scalar_tensor_tensor(ef[:, j, :], gf, float(EPG), ef[:, j, :],
                                                          ALU.mult, ALU.add))
                    own.wait()
                    for j in range(2):
                        for t in range(T):
                            own.mark(dve.tensor_scalar(OH[j][:, t, :], iota[:, :], ef[:, j, t:t + 1], None,
                                                       ALU.is_equal))
                    own.wait()
                    dve.tensor_tensor(R["M"], OH[0], OH[1], ALU.add).then_inc(s_member, 1)
                    dve.wait_ge(s_gexp, T)
                    own.mark(dve.reciprocal(R["gw"], R["gsum"]))
                    dve.wait_ge(s_ex, 1)
                    own.done(dve.tensor_scalar(R["ex1"], R["ex"], 1.0, None, ALU.add))
                    own.done(dve.reciprocal(R["ex1"], R["ex1"]))
                    own.done(dve.tensor_tensor(R["gate"][:, 0, :], R["ex1"], R["gw"], ALU.mult))
                    own.done(dve.tensor_tensor(R["gate"][:, 1, :], R["ex"], R["gate"][:, 0, :], ALU.mult))
                    for j in range(2):
                        js = slice(j * T, (j + 1) * T)
                        own.mark(dve.tensor_copy(entry[:, js, 0], tok_col[:, :]))
                        own.mark(dve.tensor_scalar(entry[:, js, 1], tok_col[:, :], float(j * SEQ), None, ALU.add))
                        own.mark(dve.tensor_copy(entry[:, js, 2], R["gate"][:, j, :]))
                    dve.wait_ge(s_rank, 1)
                    for j in range(2):
                        for t in range(T):
                            own.done(dve.tensor_tensor_reduce(R["junk"], OH[j][:, t, :], RK[:, t, :], 1.0, 0.0,
                                                              ALU.mult, ALU.add, R["pos"][:, j, t:t + 1]))
                    own.done(dve.scalar_tensor_tensor(three(R["place_f"], T), ef, float(TABLE), R["pos"],
                                                      ALU.mult, ALU.add))
                    dve.tensor_copy(R["place"], R["place_f"]).then_inc(s_entry, 1)
                    own.done(dve.tensor_copy(R["cnt"], CP))
                    own.done(dve.tensor_tensor(three(R["flags"], 7),
                                               R["cnt"].rearrange("p (e b) -> p e b", b=1).broadcast_to([1, NE, 7]),
                                               three(R["more_min"], 7), ALU.is_gt))
                    own.done(dve.tensor_reduce(R["n_more"], R["flags"], AX.X, ALU.add))
                    own.mark(dve.tensor_copy(R["n_more_i"], R["n_more"]))
                    own.done(dve.tensor_tensor(R["keys"], R["flags"], R["more_key"], ALU.mult))
                    own.done(dve.max(R["top"][:, 0:8], R["keys"]))
                    own.done(dve.match_replace(R["keys"], R["top"][:, 0:8], R["keys"], 0.0))
                    own.done(dve.max(R["top"][:, 8:16], R["keys"]))
                    own.done(dve.tensor_scalar(R["top"], R["top"], -1.0, float(NE * TABLE), ALU.mult, ALU.add))
                    own.done(dve.tensor_copy(R["start_i"], R["top"]))
                    own.done(dve.tensor_scalar(R["expert_i"], R["start_i"], 9, None, ALU.arith_shift_right))
                    dve.wait_ge(s_meta, 32)
                    half = half_col[:, 0:1].broadcast_to([P, NE])
                    own.mark(dve.scalar_tensor_tensor(R["taken"], R["meta"][:, :, 0], 2.0, half, ALU.mult, ALU.add))
                    own.mark(dve.scalar_tensor_tensor(R["put"], R["meta"][:, :, 1], 2.0, half, ALU.mult, ALU.add))
                    own.done(dve.tensor_copy(R["gate_of"], R["meta"][:, :, 2]))

                @block.gpsimd
                def _(pool):
                    pool.memset(w2[:, 0:1024], 0.0).then_inc(s_zero, 1)
                    pool.wait_ge(s_zero, 1)
                    pool.wait_ge(s_entry, 1)
                    for c in range(2 * T):
                        pool.indirect_dma_start(
                            out=table, out_offset=bass.IndirectOffsetOnAxis(ap=R["place"][:, c:c + 1], axis=0),
                            in_=R["entry"][:, c, :], in_offset=None).then_inc(s_tab, 16)

                @block.sync
                def _(sp):
                    sp.wait_ge(s_tab, 16 * 2 * T)
                    view = table.rearrange("(e s) c -> s e c", e=NE)[0:SLOTS]
                    sp.dma_start(R["meta"][0:SLOTS], view).then_inc(s_meta, 16)
                    sp.dma_start(R["meta"][SLOTS:P], view).then_inc(s_meta, 16)
            Stages.end()

        x_half = x_rows.rearrange("t (u c) -> (t u) c", u=2)
        xg = [w2[:, 0:512], w2[:, 512:1024]]
        xeT = [three(w2[:, 1024:1536], SLOTS), three(w2[:, 1536:2048], SLOTS)]
        sa, ga = w2[:, 2048:2304], w2[:, 2304:2560]
        gT = three(w2[:, 2560:2816], SLOTS)
        take1 = [w2[:, 2816 + q:2817 + q].bitcast(U32) for q in range(2)]
        put1 = [w2[:, 2820 + q:2821 + q].bitcast(U32) for q in range(2)]
        meta1 = w2[:, 2824:2828]
        ys = [w2[:, 3072:3584], w2[:, 3584:4096]]

        def wait_alone(eng, semaphore, value, tick):
            eng.wait_ge(semaphore, value)
            eng.sem_inc(tick, 1)

        def gather(pool, q, index, s):
            pool.indirect_dma_start(out=xg[q], out_offset=None, in_=x_half,
                                    in_offset=bass.IndirectOffsetOnAxis(ap=index, axis=0),
                                    bounds_check=2 * SEQ - 1, oob_is_err=False).then_inc(s, 16)

        def scatter(pool, q, index, s):
            pool.indirect_dma_start(out=y_rows, out_offset=bass.IndirectOffsetOnAxis(ap=index, axis=0),
                                    in_=ys[q], in_offset=None, bounds_check=4 * SEQ - 1, oob_is_err=False)\
                .then_inc(s, 16)

        def turn_gathered(pe, q):
            for c in range(4):
                m = pe.transpose(PS[:, q, c * P:(c + 1) * P], xg[q][:, c * P:(c + 1) * P], ident[:, :])
            return m

        def gate_up(pe, q, gu):
            for k in range(KD):
                for u in range(2):
                    m = pe.matmul(PS[u * SLOTS:(u + 1) * SLOTS, 2 + q, :], xeT[q][:, k, :],
                                  gu[:, k, :].rearrange("p (a u c) -> p a u c", a=2, u=2)[:, :, u, :],
                                  start=(k == 0), stop=(k == KD - 1))
            return m

        def turn_gated(pe, q):
            for c in range(2):
                m = pe.transpose(PS[:, 4 + q, c * P:(c + 1) * P], ga[:, c * P:(c + 1) * P], ident[:, :])
            return m

        def down(pe, q, dn):
            for k in range(FF // P):
                for u in range(2):
                    m = pe.matmul(PS[u * SLOTS:(u + 1) * SLOTS, 6 + q, :], gT[:, k, :],
                                  dn[:, k, u * NB:(u + 1) * NB], start=(k == 0), stop=(k == FF // P - 1))
            return m

        def copy_gathered(act, q):
            return act.activation(xeT[q].rearrange("p (u c) s -> p c u s", u=2),
                                  PS[:, q, :].rearrange("p (c u s) -> p c u s", c=4, u=2), ACT.Copy)

        def silu(act, q):
            return act.activation(sa, PS[:, 2 + q, 0:FF // 2], ACT.Silu)

        def times_up(dve, q):
            return dve.tensor_tensor(ga, sa, PS[:, 2 + q, FF // 2:FF], ALU.mult)

        def copy_gated(dve, q):
            return dve.tensor_copy(gT.rearrange("p (u c) s -> p c u s", u=2),
                                   PS[:, 4 + q, 0:2 * P].rearrange("p (c u s) -> p c u s", c=2, u=2))

        def experts(l, then_load):
            n = f"moe{l}"
            PAIRS = NE // 2

            def both(name, new=sem):
                return [new(f"{n}_{name}{q}") for q in range(2)]

            s_take, s_gath, s_turn, s_xe = both("take"), both("gath", lasting), both("turn"), both("xe")
            s_gu, s_silu, s_gated, s_gturn = both("gu"), both("silu"), both("gated"), both("gturn")
            sp_tick, pool_tick = sem(f"{n}_sp_tick"), sem(f"{n}_pool_tick")
            s_gt, s_dn, s_y, s_put, s_scat = both("gt"), both("dn"), both("y"), both("put"), both("scat", lasting)
            with nc.Block() as block:
                @block.sync
                def _(sp):
                    with sp.Fori(1, PAIRS) as i:
                        for q in range(2):
                            wait_alone(sp, s_gu[q], i, sp_tick)
                            load_gu(sp, l, q, 2 * i + q)
                            wait_alone(sp, s_dn[q], i, sp_tick)
                            load_dn(sp, l, q, 2 * i + q)
                    sp.wait_ge(s_gu[0], PAIRS)
                    sp.wait_ge(s_dn[0], PAIRS)
                    then_load(sp)

                @block.gpsimd
                def _(pool):
                    def take_rows(q, i):
                        pool.tensor_copy(take1[q], R["taken"][:, bass.ds(2 * i + q, 1)]).then_inc(s_take[q], 1)
                        wait_alone(pool, s_take[q], i + 1, pool_tick)
                        gather(pool, q, take1[q], s_gath[q])

                    def put_rows(q, i, done):
                        wait_alone(pool, s_y[q], done, pool_tick)
                        pool.tensor_copy(put1[q], R["put"][:, bass.ds(2 * i + q, 1)]).then_inc(s_put[q], 1)
                        wait_alone(pool, s_put[q], done, pool_tick)
                        scatter(pool, q, put1[q], s_scat[q])

                    take_rows(0, 0)
                    take_rows(1, 0)
                    with pool.Fori(1, PAIRS) as i:
                        for q in range(2):
                            put_rows(q, i - 1, i)
                            take_rows(q, i)
                    for q in range(2):
                        put_rows(q, PAIRS - 1, PAIRS)
                    for q in range(2):
                        pool.wait_ge(s_scat[q], 16 * PAIRS)

                @block.tensor
                def _(pe):
                    def one(q, i, first):
                        pe.wait_ge(s_gath[q], 16 * i + 16)
                        turn_gathered(pe, q).then_inc(s_turn[q], 1)
                        pe.wait_ge(s_xe[q], i + 1)
                        pe.wait_ge(gu_in[l][q], 16 * i + 16)
                        gate_up(pe, q, three(pair[l][q][0][:, :], D)).then_inc(s_gu[q], 1)
                        pe.wait_ge(s_gated[q], i + 1)
                        turn_gated(pe, q).then_inc(s_gturn[q], 1)
                        pe.wait_ge(s_gt[q], i + 1)
                        pe.wait_ge(dn_in[l][q], 16 * i + 16)
                        if not first:
                            pe.wait_ge(s_y[q], i)
                        down(pe, q, three(pair[l][q][1][:, :], D)).then_inc(s_dn[q], 1)

                    one(0, 0, True)
                    one(1, 0, True)
                    with pe.Fori(1, PAIRS) as i:
                        one(0, i, False)
                        one(1, i, False)

                @block.scalar
                def _(act):
                    def one(q, i, first):
                        act.wait_ge(s_turn[q], i + 1)
                        copy_gathered(act, q).then_inc(s_xe[q], 1)
                        act.wait_ge(s_gu[q], i + 1)
                        if q == 1:
                            act.wait_ge(s_gated[0], i + 1)
                        elif not first:
                            act.wait_ge(s_gated[1], i)
                        silu(act, q).then_inc(s_silu[q], 1)
                        act.wait_ge(s_dn[q], i + 1)
                        if not first:
                            act.wait_ge(s_scat[q], 16 * i)
                        act.activation(ys[q], PS[:, 6 + q, :], ACT.Copy,
                                       scale=R["gate_of"][:, bass.ds(2 * i + q, 1)]).then_inc(s_y[q], 1)

                    one(0, 0, True)
                    one(1, 0, True)
                    with act.Fori(1, PAIRS) as i:
                        one(0, i, False)
                        one(1, i, False)

                @block.vector
                def _(dve):
                    def one(q, i, first):
                        dve.wait_ge(s_silu[q], i + 1)
                        times_up(dve, q).then_inc(s_gated[q], 1)
                        dve.wait_ge(s_gturn[q], i + 1)
                        if q == 1:
                            dve.wait_ge(s_dn[0], i + 1)
                        elif not first:
                            dve.wait_ge(s_dn[1], i)
                        copy_gated(dve, q).then_inc(s_gt[q], 1)

                    one(0, 0, True)
                    one(1, 0, True)
                    with dve.Fori(1, PAIRS) as i:
                        one(0, i, False)
                        one(1, i, False)
            Stages.end()

        def further_passes(l):
            n = f"more{l}"
            names = ("meta", "idx", "gath", "turn", "xe", "gu_in", "dn_in", "gu", "silu", "gated", "gturn", "gt",
                     "dn", "y", "scat", "sp", "dve", "pool", "pool_end", "pe", "act")
            s = {k: (lasting if k in ("gath", "scat") else sem)(f"{n}_{k}") for k in names}
            gu, dn = pair[l][1]

            def run(eng, body, tick):
                count = eng.value_load(R["n_more_i"], min_val=0, max_val=MORE)
                with eng.If(count > 0):
                    with eng.Fori(0, count) as i:
                        body(i)
                        wait_alone(eng, s["scat"], 16 * i + 16, tick)

            with nc.Block() as block:
                @block.sync
                def _(sp):
                    def body(i):
                        e = sp.value_load(R["expert_i"][:, bass.ds(i, 1)], min_val=0, max_val=NE - 1)
                        row = sp.value_load(R["start_i"][:, bass.ds(i, 1)], min_val=0, max_val=NE * TABLE - SLOTS)
                        for u in range(2):
                            sp.dma_start(meta1[u * SLOTS:(u + 1) * SLOTS, :], table[bass.ds(row, SLOTS), :])\
                              .then_inc(s["meta"], 16)
                        sp.dma_start(gu[:, :].rearrange("p (e k n) -> p e k n", e=1, k=KD),
                                     A["moe_w_gu"][l][bass.ds(e, 1)].rearrange("e (k p) n -> p e k n", p=P))\
                          .then_inc(s["gu_in"], 16)
                        sp.dma_start(dn[:, :].rearrange("p (e k n) -> p e k n", e=1, k=FF // P),
                                     A["moe_w_down"][l][bass.ds(e, 1)].rearrange("e (k p) n -> p e k n", p=P))\
                          .then_inc(s["dn_in"], 16)
                    run(sp, body, s["sp"])

                @block.vector
                def _(dve):
                    def body(i):
                        dve.wait_ge(s["meta"], 32 * i + 32)
                        dve.scalar_tensor_tensor(take1[1], meta1[:, 0:1], 2.0, half_col[:, :], ALU.mult, ALU.add)\
                           .then_inc(s["idx"], 1)
                        dve.scalar_tensor_tensor(put1[1], meta1[:, 1:2], 2.0, half_col[:, :], ALU.mult, ALU.add)\
                           .then_inc(s["idx"], 1)
                        dve.wait_ge(s["silu"], i + 1)
                        times_up(dve, 1).then_inc(s["gated"], 1)
                        dve.wait_ge(s["gturn"], i + 1)
                        copy_gated(dve, 1).then_inc(s["gt"], 1)
                    run(dve, body, s["dve"])

                @block.gpsimd
                def _(pool):
                    def body(i):
                        wait_alone(pool, s["idx"], 2 * i + 2, s["pool"])
                        gather(pool, 1, take1[1], s["gath"])
                        wait_alone(pool, s["y"], i + 1, s["pool"])
                        scatter(pool, 1, put1[1], s["scat"])
                    run(pool, body, s["pool_end"])

                @block.tensor
                def _(pe):
                    def body(i):
                        pe.wait_ge(s["gath"], 16 * i + 16)
                        turn_gathered(pe, 1).then_inc(s["turn"], 1)
                        pe.wait_ge(s["xe"], i + 1)
                        pe.wait_ge(s["gu_in"], 16 * i + 16)
                        gate_up(pe, 1, three(gu[:, :], D)).then_inc(s["gu"], 1)
                        pe.wait_ge(s["gated"], i + 1)
                        turn_gated(pe, 1).then_inc(s["gturn"], 1)
                        pe.wait_ge(s["gt"], i + 1)
                        pe.wait_ge(s["dn_in"], 16 * i + 16)
                        down(pe, 1, three(dn[:, :], D)).then_inc(s["dn"], 1)
                    run(pe, body, s["pe"])

                @block.scalar
                def _(act):
                    def body(i):
                        act.wait_ge(s["turn"], i + 1)
                        copy_gathered(act, 1).then_inc(s["xe"], 1)
                        act.wait_ge(s["gu"], i + 1)
                        silu(act, 1).then_inc(s["silu"], 1)
                        act.wait_ge(s["dn"], i + 1)
                        act.wait_ge(s["meta"], 32 * i + 32)
                        act.activation(ys[1], PS[:, 7, :], ACT.Copy, scale=meta1[:, 2:3]).then_inc(s["y"], 1)
                    run(act, body, s["act"])
            Stages.end()

        Y0, Y1 = three(w3[:, :], D), three(w4[:, :], D)
        PTOK = three(w1[:, 0:T * PLE], PLE)
        PTR = three(w1[:, 1024:2048], SEQ)
        sig = [w2[:, b * NB:(b + 1) * NB] for b in range(3)]

        def load_injection(eng, l, s_wg, s_wp):
            eng.dma_start(three(pair[l][0][0][:, :], D), rows(A["ple_w_gate"][l], D)).then_inc(s_wg, 16)
            eng.dma_start(three(pair[l][0][1][:, 0:2 * D], D), rows(A["ple_w_proj"][l], D)).then_inc(s_wp, 16)

        def injection(l, s_wg, s_wp, loads, after_tile, turn_after):
            n = f"inj{l}"
            wg, wp = three(pair[l][0][0][:, :], D), three(pair[l][0][1][:, 0:2 * D], D)
            s_y = [sem(f"{n}_y{t}") for t in range(T)]
            s_p, s_pt, s_ptc = sem(f"{n}_p"), sem(f"{n}_pt"), sem(f"{n}_ptc")
            s_sum, s_unit, s_sig, s_done = sem(f"{n}_sum"), sem(f"{n}_unit"), sem(f"{n}_sig"), sem(f"{n}_done")
            norm = Norm(f"{n}_norm")
            turn = Turn(f"{n}_turn", lambda t: 0)
            turn2 = Turn(f"{n}_turn2", lambda t: 0) if turn_after else None
            y_tok = y_rows.rearrange("(j t u) c -> j t (u c)", j=2, u=2)
            U = 2 * T
            with nc.Block() as block:
                @block.sync
                def _(sp):
                    sp.dma_start(PTOK, A["p"][l, 0].rearrange("(t p) c -> p t c", p=P)).then_inc(s_p, 16)
                    for t in range(T):
                        for j, Y in enumerate((Y0, Y1)):
                            sp.dma_start(Y[:, t, :], y_tok[j, t * P:(t + 1) * P, :]).then_inc(s_y[t], 16)
                    loads(sp, norm)
                    after_tile(sp, s_done)

                @block.tensor
                def _(pe):
                    pe.wait_ge(s_p, 16)
                    for k in range(2):
                        for t in range(T):
                            m = pe.transpose(PS[:, 2 + k, t * P:(t + 1) * P], PTOK[:, t, k * P:(k + 1) * P],
                                             ident[:, :])
                    m.then_inc(s_pt, 1)
                    for t in range(T + 2):
                        if t < T:
                            pe.wait_ge(norm.done, t + 1)
                            if t >= 1:
                                turn.wait(pe, t - 1)
                            if t >= 3 and turn2:
                                turn2.wait(pe, t - 3)
                            turn.pe(pe, t)
                            turn.wait(pe, t)
                        if t >= 2 and turn2:
                            pe.wait_ge(s_done, 2 * (t - 1))
                            if t >= 3:
                                turn2.wait(pe, t - 3)
                            turn2.pe(pe, t - 2)
                        if t >= T:
                            continue
                        if t == 0:
                            pe.wait_ge(s_wg, 16)
                            pe.wait_ge(s_wp, 16)
                            pe.wait_ge(s_ptc, 2)
                        for c in range(2):
                            u = 2 * t + c
                            b = 2 + 2 * (u % 3)
                            if u >= 3:
                                pe.wait_ge(s_done, u - 2)
                            for k in range(KD):
                                pe.matmul(PS[:, b, :], XT[:, k, t * P:(t + 1) * P],
                                          wg[:, k, c * NB:(c + 1) * NB], start=(k == 0), stop=(k == KD - 1))
                            for k in range(2):
                                m = pe.matmul(PS[:, b + 1, :], PTR[:, k, t * P:(t + 1) * P],
                                              wp[:, k, c * NB:(c + 1) * NB], start=(k == 0), stop=(k == 1))
                            m.then_inc(s_unit, 1)

                @block.scalar
                def _(act):
                    act.wait_ge(s_pt, 1)
                    act.activation(PTR[:, 0, :], PS[:, 2, :], ACT.Copy).then_inc(s_ptc, 1)
                    for t in range(T + 2):
                        if t < T:
                            norm.act_tile(act, t)
                            turn.act(act, t)
                        if t >= 2 and turn2:
                            turn2.act(act, t - 2)
                        if 1 <= t <= T:
                            for c in range(2):
                                u = 2 * (t - 1) + c
                                act.wait_ge(s_unit, u + 1)
                                if u >= 3:
                                    act.wait_ge(s_done, u - 2)
                                act.activation(sig[u % 3], PS[:, 2 + 2 * (u % 3), :], ACT.Sigmoid).then_inc(s_sig, 1)

                @block.vector
                def _(dve):
                    own = Own(dve, f"{n}_own")
                    dve.wait_ge(s_pt, 1)
                    dve.tensor_copy(PTR[:, 1, :], PS[:, 3, :]).then_inc(s_ptc, 1)
                    dve.wait_ge(s_ln, 64 * l + 64)
                    for t in range(T + 2):
                        if t < T:
                            dve.wait_ge(s_y[t], 32)
                            own.done(dve.scalar_tensor_tensor(X[:, t, :], X[:, t, :], ALPHA, Y0[:, t, :],
                                                              ALU.mult, ALU.add))
                            own.done(dve.tensor_tensor(X[:, t, :], X[:, t, :], Y1[:, t, :], ALU.add))
                            norm.dve_tile(dve, own, t)
                            turn.dve(dve, t)
                        if t >= 2 and turn2:
                            turn2.dve(dve, t - 2)
                        if 1 <= t <= T:
                            for c in range(2):
                                u = 2 * (t - 1) + c
                                dve.wait_ge(s_sig, u + 1)
                                own.done(dve.tensor_tensor(sig[u % 3], sig[u % 3], PS[:, 3 + 2 * (u % 3), :],
                                                           ALU.mult))
                                xs = X[:, t - 1, c * NB:(c + 1) * NB]
                                dve.tensor_tensor(xs, xs, sig[u % 3], ALU.add).then_inc(s_done, 1)
            Stages.end()

        CW = three(wide[0][:, :], D)
        WKI = three(w4[:, 0:1024], P)
        WWI = three(w4[:, 1024:1088], IH)
        WIT = w4[0:IH, 1088:1600]
        UQ, UK = three(slim[1][:, 0:2048], D), three(slim[1][:, 2048:4096], D)
        UV = three(slim[0][:, 2048:4096], D)
        CQ = three(w1[:, 0:2048], NB)
        CT = three(w1[:, 2048:4096], SEQ)
        QI = three(w2[:, 0:2048], SEQ)
        KI = three(w2[:, 2048:3072], SEQ)
        QH = wide[0][:, :].rearrange("p (u c s) -> p u c s", u=2, c=8)
        KH = three(w4[:, :], SEQ)
        VH = three(XT[:, :, :].rearrange("p k s -> p (k s)"), D)
        WI = three(w2[:, 3072:3104], IH)
        squares = w2[:, 3104:3360]
        sq = w2[:, 3360:3376]
        m8 = {1: w2[:, 3376:3384], 2: w2[:, 3384:3392], 3: w2[:, 3392:3400]}
        SEL = list(range(1, T))
        width = [(t + 1) * P for t in range(T)]
        at = {1: 0, 2: 256, 3: 640}
        IS = {t: w3[:, at[t]:at[t] + width[t]] for t in SEL}
        WK = {t: slim[0][:, at[t]:at[t] + width[t]] for t in SEL}
        relu = [slim[0][:, 1152:1664], w2[:, 3584:4096]]
        DIST = dist[:, :]
        s_cw, s_ki, s_up = lasting("s_cw"), lasting("s_ki"), lasting("s_up")
        s_uv, s_cwout = lasting("s_uv"), lasting("s_cwout")
        s_cgain, s_dist = lasting("s_cgain"), lasting("s_dist")

        def load_latent_weights(sp):
            sp.dma_start(CW, rows(A["c_w_in"][0, :, 0:D], D)).then_inc(s_cw, 16)
            sp.dma_start(UQ, rows(A["c_w_uq"][0], D)).then_inc(s_up, 16)
            sp.dma_start(UK, rows(A["c_w_uk"][0].rearrange("c h d -> c (h d)"), D)).then_inc(s_up, 16)
            sp.dma_start(UV, rows(A["c_w_uv"][0].rearrange("c h d -> c (h d)"), D)).then_inc(s_uv, 16)

        def latents():
            n = "lat"
            s_full, s_sq, s_rms, s_cq = sem(f"{n}_full"), sem(f"{n}_sq"), sem(f"{n}_rms"), sem(f"{n}_cq")
            s_key, s_keyc, s_wt, s_wtc = sem(f"{n}_key"), sem(f"{n}_keyc"), sem(f"{n}_wt"), sem(f"{n}_wtc")
            s_qi, s_qic = sem(f"{n}_qi"), sem(f"{n}_qic")
            s_ct, s_ctc = sem(f"{n}_ct"), sem(f"{n}_ctc")
            s_wi, s_wic = sem(f"{n}_wi"), sem(f"{n}_wic")
            s_is, s_relu, s_acc, s_mask = sem(f"{n}_is"), sem(f"{n}_relu"), sem(f"{n}_acc"), sem(f"{n}_mask")
            s_half, s_inv = sem(f"{n}_half"), sem(f"{n}_inv")
            up = Jobs(f"{n}_up", ["act"] * 24)
            units = [(t, h) for h in range(IH) for t in SEL]
            per_chunk = 2 * len(SEL)
            with nc.Block() as block:
                @block.sync
                def _(sp):
                    base = D
                    for u in range(2):
                        sp.dma_start(WKI[:, :, u * HD:(u + 1) * HD], rows(A["c_w_in"][0, :, base:base + HD], HD))\
                          .then_inc(s_ki, 16)
                    sp.dma_start(WWI, rows(A["c_w_in"][0, :, base + HD:base + HD + IH], IH)).then_inc(s_ki, 16)
                    sp.dma_start(gains[:, 8:10], A["c_q_norm"][0].rearrange("(k p) -> p k", p=P)).then_inc(s_cgain, 16)
                    sp.dma_start(gains[:, 10:12], A["c_kv_norm"][0].rearrange("(k p) -> p k", p=P))\
                      .then_inc(s_cgain, 16)
                    sp.dma_start(three(wide[1][:, :], D), rows(A["c_w_out"][0], D)).then_inc(s_cwout, 16)
                    sp.dma_start(DIST, A["c_dist"]).then_inc(s_dist, 16)

                @block.tensor
                def _(pe):
                    def queries(c):
                        for k in range(KD):
                            m = pe.matmul(PS[:, c, :], CW[:, k, NB + c * P:NB + (c + 1) * P], XT[:, k, :],
                                          start=(k == 0), stop=(k == KD - 1))
                        m.then_inc(s_qi, 1)

                    def scores(c):
                        pe.wait_ge(s_qic, c + 1)
                        for i in range(per_chunk * c, per_chunk * (c + 1)):
                            t, h = units[i]
                            if i >= 2:
                                pe.wait_ge(s_relu, i - 1)
                            pe.matmul(PS[:, 6 + i % 2, 0:width[t]], QI[:, h // 2, t * P:(t + 1) * P],
                                      KI[:, h % 2, 0:width[t]], start=True, stop=True).then_inc(s_is, 1)

                    pe.wait_ge(s_ki, 48)
                    for k in range(KD):
                        m = pe.matmul(PS[:, 4, :], WKI[:, k, :], XT[:, k, :], start=(k == 0), stop=(k == KD - 1))
                    m.then_inc(s_key, 1)
                    for k in range(KD):
                        m = pe.matmul(PS[0:IH, 5, :], WWI[:, k, :], XT[:, k, :], start=(k == 0), stop=(k == KD - 1))
                    m.then_inc(s_wt, 1)
                    pe.wait_ge(s_cw, 16)
                    queries(0)
                    pe.wait_ge(s_wtc, 1)
                    for t in range(T):
                        m = pe.transpose(PS[:, 5, t * IH:(t + 1) * IH], WIT[:, t * P:(t + 1) * P], ident[0:IH, 0:IH])
                    m.then_inc(s_wi, 1)
                    queries(1)
                    pe.wait_ge(s_keyc, 2)
                    pe.wait_ge(s_half, 2)
                    scores(0)
                    queries(2)
                    scores(1)
                    queries(3)
                    scores(2)
                    scores(3)
                    for t in range(T):
                        for k in range(KD):
                            m = pe.matmul(PS[:, t, :], XT[:, k, t * P:(t + 1) * P], CW[:, k, 0:NB],
                                          start=(k == 0), stop=(k == KD - 1))
                        m.then_inc(s_full, 1)
                    pe.wait_ge(s_wic, 1)
                    pe.wait_ge(s_relu, len(units))
                    pe.wait_ge(s_cq, 2 * T)
                    for c in range(4):
                        for t in range(T):
                            m = pe.transpose(PS[:, 4 + c, t * P:(t + 1) * P], CQ[:, t, c * P:(c + 1) * P],
                                             ident[:, :])
                        m.then_inc(s_ct, 1)
                    pe.wait_ge(s_ctc, 4)
                    pe.wait_ge(s_up, 32)
                    for j in range(24):
                        if j >= 8:
                            up.wait_emptied(pe, j - 8)
                        if j == 16:
                            pe.wait_ge(s_uv, 16)
                        for k in range(2):
                            if j < 8:
                                lhsT, rhs = UQ[:, k, j * P:(j + 1) * P], CT[:, k, :]
                            elif j < 16:
                                lhsT, rhs = UK[:, k, (j - 8) * P:(j - 7) * P], CT[:, 2 + k, :]
                            else:
                                t, c = (j - 16) // 2, j % 2
                                lhsT, rhs = CT[:, 2 + k, t * P:(t + 1) * P], UV[:, k, c * NB:(c + 1) * NB]
                            m = pe.matmul(PS[:, j % 8, :], lhsT, rhs, start=(k == 0), stop=(k == 1))
                        m.then_inc(up.full, 1)

                @block.scalar
                def _(act):
                    def copy_queries(c):
                        act.wait_ge(s_qi, c + 1)
                        act.activation(QI[:, c, :], PS[:, c, :], ACT.Copy).then_inc(s_qic, 1)

                    def rectify(c):
                        for i in range(per_chunk * c, per_chunk * (c + 1)):
                            t, h = units[i]
                            act.wait_ge(s_is, i + 1)
                            if i >= 2:
                                act.wait_ge(s_acc, i - 1)
                            act.activation(relu[i % 2][:, 0:width[t]], PS[:, 6 + i % 2, 0:width[t]], ACT.Relu)\
                               .then_inc(s_relu, 1)

                    act.wait_ge(s_key, 1)
                    for u in range(2):
                        act.activation(KI[u * HD:(u + 1) * HD, u, :], PS[u * HD:(u + 1) * HD, 4, :], ACT.Copy)\
                           .then_inc(s_keyc, 1)
                    act.wait_ge(s_wt, 1)
                    act.activation(WIT, PS[0:IH, 5, :], ACT.Copy).then_inc(s_wtc, 1)
                    copy_queries(0)
                    act.wait_ge(s_wi, 1)
                    act.activation(WI, three(PS[:, 5, 0:T * IH], IH), ACT.Copy).then_inc(s_wic, 1)
                    copy_queries(1)
                    rectify(0)
                    copy_queries(2)
                    rectify(1)
                    copy_queries(3)
                    rectify(2)
                    rectify(3)
                    for t in range(T):
                        act.wait_ge(s_full, t + 1)
                        for u in range(2):
                            i = 2 * t + u
                            if i >= 1:
                                act.wait_ge(s_sq, i)
                            act.activation(squares, PS[:, t, u * RANK:(u + 1) * RANK], ACT.Square,
                                           accum_out=sq[:, i:i + 1]).then_inc(s_sq, 1)
                    act.wait_ge(s_sq, 2 * T)
                    act.activation(sq[:, 8:16], sq[:, 0:8], ACT.Sqrt, bias=eps[:, 1:2], scale=1.0 / RANK)\
                       .then_inc(s_rms, 1)
                    act.wait_ge(s_inv, 1)
                    for t in range(T):
                        for u in range(2):
                            act.activation(CQ[:, t, u * RANK:(u + 1) * RANK], PS[:, t, u * RANK:(u + 1) * RANK],
                                           ACT.Copy, scale=sq[:, 8 + 2 * t + u:9 + 2 * t + u]).then_inc(s_cq, 1)
                    act.wait_ge(s_cgain, 32)
                    for c in range(4):
                        act.wait_ge(s_ct, c + 1)
                        act.activation(CT[:, c, :], PS[:, 4 + c, :], ACT.Copy, scale=gains[:, 8 + c:9 + c])\
                           .then_inc(s_ctc, 1)
                    for j in range(24):
                        up.wait_full(act, j)
                        src = PS[:, j % 8, :]
                        if j < 8:
                            act.activation(QH[0:HD, 0, j, :], src[0:HD, :], ACT.Copy, scale=HD ** -0.5)
                            act.activation(QH[HD:P, 1, j, :], src[HD:P, :], ACT.Copy, scale=HD ** -0.5)\
                               .then_inc(up.sem_of(0), 1)
                        elif j < 16:
                            act.activation(KH[:, j - 8, :], src, ACT.Copy).then_inc(up.sem_of(0), 1)
                        else:
                            t, c = (j - 16) // 2, j % 2
                            act.activation(VH[:, t, c * NB:(c + 1) * NB], src, ACT.Copy).then_inc(up.sem_of(0), 1)

                @block.vector
                def _(dve):
                    own = Own(dve, f"{n}_own")
                    dve.wait_ge(s_wic, 1)
                    for i, (t, h) in enumerate(units):
                        dve.wait_ge(s_relu, i + 1)
                        r, w = relu[i % 2][:, 0:width[t]], WI[:, t, h:h + 1]
                        if h == 0:
                            dve.tensor_scalar(IS[t], r, w, None, ALU.mult).then_inc(s_acc, 1)
                        else:
                            dve.wait_ge(s_acc, i - len(SEL) + 1)
                            dve.scalar_tensor_tensor(IS[t], r, w, IS[t], ALU.mult, ALU.add).then_inc(s_acc, 1)
                    dve.wait_ge(s_dist, 16)
                    dve.wait_ge(s_mask, len(SEL))
                    last = {}

                    def step(t, ins):
                        own.mark(ins)
                        last[t] = own.n

                    for r in range(TOPK // 8):
                        cur = IS if r == 0 else WK
                        for t in SEL:
                            if r > 0:
                                dve.wait_ge(own.sem, last[t])
                            step(t, dve.max(m8[t], cur[t]))
                        for t in SEL:
                            dve.wait_ge(own.sem, last[t])
                            step(t, dve.match_replace(WK[t], m8[t], cur[t], LOWEST))
                        if r == TOPK // 16:
                            dve.wait_ge(s_rms, 1)
                            dve.reciprocal(sq[:, 8:16], sq[:, 8:16]).then_inc(s_inv, 1)
                    for t in SEL:
                        dve.wait_ge(own.sem, last[t])
                        step(t, dve.tensor_tensor(IS[t], IS[t], WK[t], ALU.is_equal))
                    for t in SEL:
                        dve.wait_ge(own.sem, last[t])
                        own.mark(dve.scalar_tensor_tensor(IS[t], IS[t], BIG, DIST[:, SEQ - width[t]:SEQ],
                                                          ALU.mult, ALU.add))
                    own.wait()

                @block.gpsimd
                def _(pool):
                    pool.memset(KI[HD:P, 0, :], 0.0).then_inc(s_half, 1)
                    pool.wait_ge(s_half, 1)
                    pool.memset(KI[0:HD, 1, :], 0.0).then_inc(s_half, 1)
                    pool.wait_ge(s_half, 2)
                    for n_, t in enumerate(SEL):
                        pool.wait_ge(s_acc, len(units) - len(SEL) + n_ + 1)
                        d = IS[t][:, t * P:(t + 1) * P]
                        pool.affine_select(out=d, in_=d, compare_op=ALU.is_ge, fill=LOWEST, base=0,
                                           pattern=[[-1, P]], channel_multiplier=1).then_inc(s_mask, 1)
                        pool.wait_ge(s_mask, n_ + 1)
                    pool.wait_ge(s_full, T)
                    pool.memset(QH[HD:P, 0, :, :], 0.0).then_inc(s_half, 1)
                    pool.wait_ge(s_half, 3)
                    pool.memset(QH[0:HD, 1, :, :], 0.0).then_inc(s_half, 1)
                    pool.wait_ge(s_half, 4)
            Stages.end()

        DMASK = {t: IS[t] for t in SEL}
        DMASK[0] = DIST[:, SEQ - P:SEQ]
        LGS = 8
        LG = [w3[:, 1536 + b * NB:2048 + b * NB] for b in range(5)] + [w1[:, b * NB:(b + 1) * NB] for b in range(3)]
        PTS = [w2[:, b * NB:(b + 1) * NB] for b in range(4)]
        nmax = w2[:, 2048:2112]
        rsum = w2[:, 2112:2176]
        rden = w2[:, 2176:2240]
        MC = three(slim[0][:, :], SEQ)

        def attention():
            n = "att"
            units = [(t, h) for t in range(T) for h in range(AH)]
            N = len(units)
            LAG_R, LAG_T, LAG_V = 1, 4, 6
            s_s, s_l, s_max, s_p = sem(f"{n}_s"), sem(f"{n}_l"), sem(f"{n}_max"), sem(f"{n}_p")
            s_r, s_n = sem(f"{n}_r"), [sem(f"{n}_n_{e}") for e in ("pool", "dve")]
            s_pt, s_ptc, s_pv = sem(f"{n}_pt"), sem(f"{n}_ptc"), sem(f"{n}_pv")
            s_o = [sem(f"{n}_o_{e}") for e in ("act", "dve")]
            slope = [2.0 ** (-8.0 * (h + 1) / AH) for h in range(AH)]

            def finish(eng, copy, half, t):
                eng.wait_ge(s_pv, AH // 2 * (t + 1))
                copy(MC[:, 4 * half:4 * half + 4, t * P:(t + 1) * P], three(PS[:, 4 + 2 * (t % 2) + half, :], P))\
                    .then_inc(s_o[half], 1)

            with nc.Block() as block:
                @block.tensor
                def _(pe):
                    for i in range(0, N + LAG_V, 2):
                        for j in (i, i + 1):
                            if j < N:
                                t, h = units[j]
                                if j >= 2:
                                    pe.wait_ge(s_l, j - 1)
                                pe.matmul(PS[:, j % 2, 0:width[t]], QH[:, h % 2, h // 2, t * P:(t + 1) * P],
                                          KH[:, h // 2, 0:width[t]], start=True, stop=True).then_inc(s_s, 1)
                            j -= LAG_T
                            if 0 <= j < N:
                                t, h = units[j]
                                pe.wait_ge(s_n[j % 2], j // 2 + 1)
                                if j >= 2:
                                    pe.wait_ge(s_ptc, j - 1)
                                for kb in range(t + 1):
                                    m = pe.transpose(PS[:, 2 + j % 2, kb * P:(kb + 1) * P],
                                                     LG[j % LGS][:, kb * P:(kb + 1) * P], ident[:, :])
                                m.then_inc(s_pt, 1)
                        j = i - LAG_V
                        if j >= 0:
                            t, h = units[j]
                            pe.wait_ge(s_ptc, j + 2)
                            if t >= 2 and h == 0:
                                for s in s_o:
                                    pe.wait_ge(s, t - 1)
                            for kb in range(t + 1):
                                for u in range(2):
                                    m = pe.matmul(PS[u * HD:(u + 1) * HD, 4 + 2 * (t % 2) + h // 8,
                                                     (h // 2 % 4) * P:(h // 2 % 4 + 1) * P],
                                                  VH[:, kb, (h + u) * HD:(h + u + 1) * HD],
                                                  PTS[(j + u) % 4][:, kb * P:(kb + 1) * P],
                                                  start=(kb == 0), stop=(kb == t))
                            m.then_inc(s_pv, 1)

                @block.vector
                def _(dve):
                    def invert(i):
                        dve.wait_ge(s_p, i + 1)
                        dve.reciprocal(rden[:, i:i + 1], rsum[:, i:i + 1]).then_inc(s_r, 1)

                    def divide(i):
                        if i % 2 == 1:
                            dve.wait_ge(s_r, i + 1)
                            g = LG[i % LGS][:, 0:width[units[i][0]]]
                            dve.tensor_scalar(g, g, rden[:, i:i + 1], None, ALU.mult).then_inc(s_n[1], 1)

                    for i, (t, h) in enumerate(units):
                        dve.wait_ge(s_s, i + 1)
                        if i >= LGS:
                            dve.wait_ge(s_pt, i - LGS + 1)
                        g = LG[i % LGS][:, 0:width[t]]
                        dve.scalar_tensor_tensor(g, DMASK[t], -slope[h], PS[:, i % 2, 0:width[t]],
                                                 ALU.mult, ALU.add).then_inc(s_l, 1)
                        dve.wait_ge(s_l, i + 1)
                        dve.tensor_reduce(nmax[:, i:i + 1], g, AX.X, ALU.max, negate=True).then_inc(s_max, 1)
                        if i >= LAG_R:
                            invert(i - LAG_R)
                        if i > LAG_R:
                            divide(i - LAG_R - 1)
                        if h == 10 and t >= 1:
                            finish(dve, dve.tensor_copy, 1, t - 1)
                    for i in range(N - LAG_R, N):
                        divide(i - 1)
                        invert(i)
                    divide(N - 1)
                    finish(dve, dve.tensor_copy, 1, T - 1)

                @block.scalar
                def _(act):
                    for i in range(N + LAG_T):
                        if i < N:
                            t, h = units[i]
                            act.wait_ge(s_max, i + 1)
                            g = LG[i % LGS][:, 0:width[t]]
                            act.activation(g, g, ACT.Exp, bias=nmax[:, i:i + 1],
                                           accum_out=rsum[:, i:i + 1]).then_inc(s_p, 1)
                        j = i - LAG_T
                        if j >= 0:
                            t, h = units[j]
                            act.wait_ge(s_pt, j + 1)
                            if j >= 4:
                                act.wait_ge(s_pv, (j - 4) // 2 + 1)
                            act.activation(PTS[j % 4][:, 0:width[t]], PS[:, 2 + j % 2, 0:width[t]],
                                           ACT.Copy).then_inc(s_ptc, 1)
                            if h == 8 and t >= 1:
                                finish(act, lambda o, a: act.activation(o, a, ACT.Copy), 0, t - 1)
                    finish(act, lambda o, a: act.activation(o, a, ACT.Copy), 0, T - 1)

                @block.gpsimd
                def _(pool):
                    for i in range(0, N, 2):
                        pool.wait_ge(s_r, i + 1)
                        g = LG[i % LGS][:, 0:width[units[i][0]]]
                        pool.tensor_scalar(g, g, rden[:, i:i + 1], None, ALU.mult).then_inc(s_n[0], 1)
                        pool.wait_ge(s_n[0], i // 2 + 1)
            Stages.end()

        s_wg = [lasting(f"s_wg{l}") for l in range(2)]
        s_wp = [lasting(f"s_wp{l}") for l in range(2)]
        s_out = lasting("s_out")

        def before_out(l):
            def load_first(sp):
                if l == 1:
                    load_gu(sp, 1, 0, 0)
                    load_dn(sp, 1, 0, 0)
            return load_first

        def after_out(l):
            def then_load(sp, sums):
                sums.wait_full(sp, 7)
                load_gu(sp, l, 1, 1)
                load_dn(sp, l, 1, 1)
            return then_load

        def layer_end(l, loads, after_tile, turn_after):
            route(l)
            experts(l, lambda sp: load_injection(sp, l, s_wg[l], s_wp[l]))
            further_passes(l)
            injection(l, s_wg[l], s_wp[l], loads, after_tile, turn_after)

        def next_layer_loads(sp, norm):
            load_latent_weights(sp)
            norm_done = norm.done
            sp.wait_ge(norm_done, T)
            load_ln(sp, A["ln1_g"][1], A["ln1_b"][1], s_ln)

        def store_tiles(sp, s_done):
            for t in range(T):
                sp.wait_ge(s_done, 2 * t + 2)
                sp.dma_start(out[0, t * P:(t + 1) * P, :], X[:, t, :]).then_inc(s_out, 16)
            sp.wait_ge(s_out, 16 * T)

        out_projection(0, MT, w_out0, s_wout, before_out(0), after_out(0))
        layer_end(0, next_layer_loads, lambda sp, s_done: None, True)
        latents()
        attention()
        WO = three(wide[1][:, :], D)
        out_projection(1, MC, [WO[:, :, 0:NB], WO[:, :, NB:D]], [s_cwout], before_out(1), after_out(1))
        layer_end(1, lambda sp, norm: None, store_tiles, False)


_INS = ['x', 'p', 'ab_w_in', 'ret_gn_g', 'pool_w', 'pool_scale', 'ab_w_out', 'c_w_in', 'c_q_norm', 'c_kv_norm',
        'c_w_uq', 'c_w_uk', 'c_w_uv', 'c_w_out', 'ln1_g', 'ln1_b', 'ln2_g', 'ln2_b', 'moe_w_group', 'moe_b_group',
        'moe_w_expert', 'moe_b_expert', 'moe_w_gu', 'moe_w_down', 'ple_w_gate', 'ple_w_proj']


def constants(np):
    f = np.float32
    p = np.arange(P)
    j = np.arange(SEQ)
    c = {"c_ident": np.eye(P), "c_tri": (p[:, None] < p[None, :]), "c_iota": np.tile(np.arange(NE), (P, 1)),
         "c_half": (p // SLOTS)[:, None], "c_tok": np.arange(T)[None, :] * P + p[:, None],
         "c_eps": np.tile([LN_EPS, RMS_EPS], (P, 1))}
    diff = j[None, :] - p[:, None]
    gamma = 1.0 - 2.0 ** (-5.0 - np.arange(RH))
    c["c_decay"] = np.where(diff[None] >= 0, gamma[:, None, None] ** np.maximum(diff, 0)[None] * P ** -0.5, 0.0)
    c["c_edge"] = np.array([[w / min(t + 1, w) for t in range(WMAX)] for w in WINDOWS])
    c["c_empty"] = np.tile([NOWHERE, NOWHERE, 0.0, 0.0], (P, NB // 4))
    e, b = np.meshgrid(np.arange(NE), np.arange(1, 8), indexing="ij")
    c["c_more"] = np.stack([(NE * TABLE - (TABLE * e + SLOTS * b)).ravel(), (SLOTS * b).ravel()])
    dist = (SEQ - P) + p[:, None] - j[None, :]
    c["c_dist"] = np.where(dist >= 0, dist, BIG)
    return {k: np.ascontiguousarray(v.astype(f)) for k, v in c.items()}


def kernel(**inputs):
    import numpy as _np
    import concourse.bacc as _bacc
    from concourse import mybir as _mybir
    from concourse.bass_utils import run_bass_kernel_spmd as _run

    nc = _bacc.Bacc("TRN2", target_bir_lowering=False, num_devices=1)
    arrays, args = {}, {}
    given = {name: _np.ascontiguousarray(inputs[name]) for name in _INS}
    given.update(constants(_np))
    for name, a in given.items():
        arrays[f"in_{name}"] = a
        args[name] = nc.dram_tensor(f"in_{name}", a.shape, _mybir.dt.from_np(a.dtype), kind="ExternalInput").ap()
    out = nc.dram_tensor("out", (1, SEQ, D), _mybir.dt.float32, kind="ExternalOutput").ap()
    build(nc, args, out)
    r = _run(nc, [arrays], core_ids=[0])
    return r.results[0]["out"]
```

```python
from contextlib import ExitStack

import concourse.bass as bass
from concourse import mybir

F32 = mybir.dt.float32
F32R = mybir.dt.float32r
BF16 = mybir.dt.bfloat16
U32 = mybir.dt.uint32
I32 = mybir.dt.int32
ALU = mybir.AluOpType
ACT = mybir.ActivationFunctionType
AX = mybir.AxisListType

P = 128
SEQ = 512
D = 1024
T = SEQ // P
KD = D // P
NB = 512
PLE = 256
RH = 4
WINDOWS = (2, 4, 8, 16)
WMAX = WINDOWS[-1]
AH, HD = 16, 64
RANK = 256
IH = 8
TOPK = min(256, SEQ // 4)
NG, EPG = 4, 8
NE = NG * EPG
FF = 512
SLOTS = 64
TABLE = SEQ
MORE = (2 * SEQ) // (SLOTS + 1)
NOWHERE = 4 * SEQ
ALPHA = 4.0 ** 0.25
LN_EPS = 1e-5
RMS_EPS = 1e-6
BIG = 1e30
LOWEST = -3.0e38


def build(nc, A, out):
    ctx = ExitStack()
    ctx.enter_context(nc.allow_non_contiguous_dma(reason="small vectors to one feature per partition"))
    with ctx:
        def sb(name, shape, dt=F32):
            return ctx.enter_context(nc.sbuf_tensor(name, shape, dt))

        def lasting(name):
            return ctx.enter_context(nc.semaphore(name))

        class Stages:

            now, cleared = [], []

            @staticmethod
            def new(name):
                s = nc.alloc_semaphore(name)
                Stages.now.append(s)
                return s

            @staticmethod
            def end():
                for s in Stages.cleared:
                    nc.release_semaphore(s)
                for s in Stages.now:
                    nc.gpsimd.sem_clear(s)
                Stages.now, Stages.cleared = [], Stages.now

        sem = Stages.new

        def dram(name, shape):
            return nc.dram_tensor(name, shape, F32, kind="Internal").ap()

        def three(ap, b):
            return ap.rearrange("p (a b) -> p a b", b=b)

        X = sb("X", [P, T, D])
        w1 = sb("w1", [P, 4096])
        w2 = sb("w2", [P, 4096])
        w3 = sb("w3", [P, 4096])
        w4 = sb("w4", [P, 4096])
        ln_g = sb("ln_g", [P, D])
        ln_b = sb("ln_b", [P, D])
        ident = sb("ident", [P, P])
        tri = sb("tri", [P, P], BF16)
        ones = sb("ones", [P, P], BF16)
        eps = sb("eps", [P, 2])
        iota = sb("iota", [P, NE])
        half_col = sb("half_col", [P, 2])
        tok_col = sb("tok_col", [P, T])
        gains = sb("gains", [P, 16])
        dist = sb("dist", [P, SEQ])
        unread = sb("unread", [P, 1])
        stats = sb("stats", [P, 16, 6])
        mv = sb("mv", [P, 16, 2])
        rstd = sb("rstd", [P, 16])
        PS = ctx.enter_context(nc.psum_tensor("PS", [P, 8, NB], F32))

        x_rows = dram("x_rows", [SEQ, D])
        y_rows = dram("y_rows", [2 * SEQ * 2, NB])
        table = dram("table", [NE * TABLE, 4])

        class Jobs:

            def __init__(self, name, owners):
                self.owners = owners
                self.full = sem(f"{name}_full")
                self.emptied = {o: sem(f"{name}_by_{o}") for o in sorted(set(owners))}

            def wait_full(self, eng, j):
                eng.wait_ge(self.full, j + 1)

            def wait_emptied(self, eng, j):
                o = self.owners[j]
                eng.wait_ge(self.emptied[o], self.owners[:j + 1].count(o))

            def sem_of(self, j):
                return self.emptied[self.owners[j]]

        class Own:

            def __init__(self, eng, name):
                self.eng, self.sem, self.n = eng, sem(name), 0

            def done(self, ins):
                self.n += 1
                ins.then_inc(self.sem, 1)
                self.eng.wait_ge(self.sem, self.n)

            def mark(self, ins):
                self.n += 1
                ins.then_inc(self.sem, 1)

            def wait(self):
                self.eng.wait_ge(self.sem, self.n)

        class Turn:

            def __init__(self, name, bank):
                self.full, self.copied = sem(f"{name}_full"), sem(f"{name}_copied")
                self.bank = bank

            def pe(self, pe, t):
                for k in range(KD):
                    m = pe.transpose(PS[:, self.bank(t) + k // 4, (k % 4) * P:(k % 4 + 1) * P],
                                     X[:, t, k * P:(k + 1) * P], ident[:, :])
                m.then_inc(self.full, 1)

            def act(self, act, t):
                act.wait_ge(self.full, t + 1)
                for u in range(2):
                    act.activation(XT[:, 4 * u:4 * u + 4, t * P:(t + 1) * P], three(PS[:, self.bank(t) + u, :], P),
                                   ACT.Copy).then_inc(self.copied, 1)

            def wait(self, eng, t):
                eng.wait_ge(self.copied, 2 * (t + 1))

        def fetch_sqrt(act):
            act.activation(unread[:, :], eps[:, 0:1], ACT.Sqrt)

        def alternate(n):
            return ["act" if j % 2 == 0 else "dve" for j in range(n)]

        class Norm:

            def __init__(self, name):
                self.var, self.std, self.done = sem(f"{name}_var"), sem(f"{name}_std"), sem(f"{name}_done")
                self.name = name

            def dve_stats(self, dve, own, t, c):
                own.mark(dve.bn_stats(stats[:, 2 * t + c, :], X[:, t, c * NB:(c + 1) * NB]))

            def dve_tile(self, dve, own, t):
                own.wait()
                dve.bn_aggr(mv[:, t, :], stats[:, 2 * t:2 * t + 2, :]).then_inc(self.var, 1)
                dve.wait_ge(self.var, t + 1)
                own.mark(dve.scalar_tensor_tensor(X[:, t, :], X[:, t, :], mv[:, t, 0:1], ln_g[:, :],
                                                  ALU.subtract, ALU.mult))
                dve.wait_ge(self.std, t + 1)
                own.done(dve.reciprocal(rstd[:, t:t + 1], rstd[:, 8 + t:9 + t]))
                dve.scalar_tensor_tensor(X[:, t, :], X[:, t, :], rstd[:, t:t + 1], ln_b[:, :],
                                         ALU.mult, ALU.add).then_inc(self.done, 1)

            def act_tile(self, act, t):
                act.wait_ge(self.var, t + 1)
                act.activation(rstd[:, 8 + t:9 + t], mv[:, t, 1:2], ACT.Sqrt, bias=eps[:, 0:1])\
                   .then_inc(self.std, 1)

        def load_ln(eng, g, b, s):
            eng.dma_start(ln_g[:, :], g.partition_broadcast(P)).then_inc(s, 16)
            eng.dma_start(ln_b[:, :], b.partition_broadcast(P)).then_inc(s, 16)

        def rows(w, n):
            return w.rearrange("(k p) n -> p k n", p=P)


        s_x = [lasting(f"s_x{t}") for t in range(T)]
        s_const = lasting("s_const")
        s_ident = lasting("s_ident")
        s_bf = lasting("s_bf")
        s_w = [lasting(f"s_w_in{c}") for c in range(5)]
        s_w_half = lasting("s_w_half")
        s_wout = [lasting(f"s_wout{c}") for c in range(2)]
        s_ln = lasting("s_ln")
        s_gain = lasting("s_gain")
        s_dec = lasting("s_dec")
        s_pool = lasting("s_pool")

        QT, KT = three(w1[:, 0:2048], SEQ), three(w1[:, 2048:4096], SEQ)
        V, SG = three(w2[:, 0:2048], NB), three(w2[:, 2048:4096], NB)
        UT, DEC = three(w3[:, 0:2048], SEQ), three(w3[:, 2048:4096], SEQ)
        TMP = [w3[:, 2048:2560], w3[:, 2560:3072]]
        EDGE = three(w3[:, 3072:3136], WMAX)
        tri32 = w3[:, 3136:3264]
        s_edge = lasting("s_edge")
        PIECES = [(0, k, k + 2) for k in range(0, KD, 2)] + [(n, k, k + 4) for n in range(1, 5) for k in (0, 4)]
        s_xfull, s_xh, s_xl = sem("x_full"), sem("x_high"), sem("x_low")
        s_wh, s_wl = sem("w_high"), sem("w_low")

        CHUNKS = (4, 0, 1, 2, 3)

        def pieces_of(n):
            return [i for i, piece in enumerate(PIECES) if piece[0] == n]
        pj_owner = alternate(12) + ["dve"] * 4 + ["act"] * 4
        pj = Jobs("proj", pj_owner)
        PROJ = len(pj_owner)

        with ExitStack() as first:
            def early(name, shape, dt=F32):
                return first.enter_context(nc.sbuf_tensor(name, shape, dt))

            w_in = [early("w_in0", [P, KD, NB])[:, :, :], three(w4[:, :], NB)]
            w_high = [early(f"w_high{b}", [P, KD, NB], F32R) for b in range(2)]
            w_low = [early(f"w_low{b}", [P, KD, NB], F32R) for b in range(2)]
            XH, XL = early("x_high", [P, KD, SEQ], F32R), early("x_low", [P, KD, SEQ], F32R)
            with nc.Block() as block:
                @block.sync
                def _(sp):
                    for t in range(T):
                        sp.dma_start(X[:, t, :], A["x"][0, t * P:(t + 1) * P, :]).then_inc(s_x[t], 16)
                    sp.dma_start(w3[:, 3072:3136], A["c_edge"].rearrange("g n -> (g n)").partition_broadcast(P))\
                      .then_inc(s_edge, 16)
                    for n, c in enumerate(CHUNKS):
                        w = rows(A["ab_w_in"][0, :, c * NB:(c + 1) * NB], NB)
                        if n == 0:
                            sp.dma_start(w_in[0][:, 0:KD // 2, :], w[:, 0:KD // 2, :]).then_inc(s_w_half, 16)
                            sp.dma_start(w_in[0][:, KD // 2:KD, :], w[:, KD // 2:KD, :]).then_inc(s_w[c], 16)
                        else:
                            if n >= 2:
                                sp.wait_ge(s_wl, pieces_of(n - 2)[-1] + 1)
                            sp.dma_start(w_in[n % 2], w).then_inc(s_w[c], 16)
                    sp.wait_ge(s_bf, 2)
                    pj.wait_emptied(sp, 12)
                    sp.dma_start(DEC, A["c_decay"].rearrange("h p n -> p h n")).then_inc(s_dec, 16)

                @block.gpsimd
                def _(pool):
                    pool.memset(ones[:, :], 1.0).then_inc(s_bf, 1)
                    pool.wait_ge(s_const, 80)
                    pool.tensor_copy(tri[:, :], tri32).then_inc(s_bf, 1)
                    pool.wait_ge(s_bf, 2)

                @block.scalar
                def _(act):
                    act.dma_start(ident[:, :], A["c_ident"]).then_inc(s_ident, 16)
                    act.dma_start(tri32, A["c_tri"]).then_inc(s_const, 16)
                    act.dma_start(iota[:, :], A["c_iota"]).then_inc(s_const, 16)
                    act.dma_start(half_col[:, :], A["c_half"]).then_inc(s_const, 16)
                    act.dma_start(tok_col[:, :], A["c_tok"]).then_inc(s_const, 16)
                    act.dma_start(eps[:, :], A["c_eps"]).then_inc(s_const, 16)
                    load_ln(act, A["ln1_g"][0], A["ln1_b"][0], s_ln)
                    act.dma_start(gains[:, 0:4], A["ret_gn_g"][0].rearrange("(k p) -> p k", p=P)).then_inc(s_gain, 16)
                    act.dma_start(gains[:, 4:8], A["pool_scale"][0].rearrange("(k p) -> p k", p=P)).then_inc(s_gain, 16)
                    for t in range(T):
                        act.wait_ge(s_xfull, t + 1)
                        for u in range(2):
                            act.activation(XH[:, 4 * u:4 * u + 4, t * P:(t + 1) * P], three(PS[:, 2 * t + u, :], P),
                                           ACT.Copy).then_inc(s_xh, 1)

                    def split(n):
                        if n >= 2:
                            pj.wait_full(act, 4 * (n - 1) - 1)
                        for i in pieces_of(n):
                            _, k0, k1 = PIECES[i]
                            act.wait_ge(s_w_half if n == 0 and k0 < KD // 2 else s_w[CHUNKS[n]], 16)
                            act.activation(w_high[n % 2][:, k0:k1, :], w_in[n % 2][:, k0:k1, :], ACT.Copy)\
                               .then_inc(s_wh, 1)

                    split(0)
                    split(1)
                    for j in range(PROJ):
                        if j % 4 == 0 and 1 <= j // 4 < 4:
                            split(j // 4 + 1)
                        if pj_owner[j] != "act":
                            continue
                        pj.wait_full(act, j)
                        c = CHUNKS[j // 4]
                        dst = (QT, KT, V, SG, UT)[c][:, j % 4, :]
                        act.activation(dst, PS[:, j % 8, :], ACT.Silu if c == 3 else ACT.Copy)\
                           .then_inc(pj.sem_of(j), 1)

                @block.vector
                def _(dve):
                    for i in range(2 * T):
                        t, u = i // 2, i % 2
                        at_tile = (slice(None), slice(4 * u, 4 * u + 4), slice(t * P, (t + 1) * P))
                        dve.wait_ge(s_xh, i + 1)
                        dve.tensor_tensor(XL[at_tile], three(PS[:, i, :], P), XH[at_tile].bitcast(F32), ALU.subtract)\
                           .then_inc(s_xl, 1)

                    def split(n):
                        for i in pieces_of(n):
                            _, k0, k1 = PIECES[i]
                            dve.wait_ge(s_wh, i + 1)
                            dve.tensor_tensor(w_low[n % 2][:, k0:k1, :], w_in[n % 2][:, k0:k1, :],
                                              w_high[n % 2][:, k0:k1, :].bitcast(F32), ALU.subtract).then_inc(s_wl, 1)

                    split(0)
                    split(1)
                    own = Own(dve, "own_pool")

                    def pool_group(g):
                        src, n, b = UT[:, g, :], 1, 0
                        while n < WINDOWS[g]:
                            dst = TMP[b]
                            own.mark(dve.tensor_copy(dst[:, 0:n], src[:, 0:n]))
                            own.done(dve.tensor_tensor(dst[:, n:SEQ], src[:, n:SEQ], src[:, 0:SEQ - n], ALU.add))
                            src, n, b = dst, 2 * n, 1 - b
                        own.done(dve.tensor_tensor(src[:, 0:WMAX], src[:, 0:WMAX], EDGE[:, g, :], ALU.mult))
                        own.done(dve.scalar_tensor_tensor(UT[:, g, :], src, 1.0 / WINDOWS[g], UT[:, g, :],
                                                          ALU.mult, ALU.subtract))

                    for j in range(PROJ):
                        if j % 4 == 0 and 1 <= j // 4 < 4:
                            split(j // 4 + 1)
                        if pj_owner[j] != "dve":
                            continue
                        pj.wait_full(dve, j)
                        dst = (QT, KT, V, SG, UT)[CHUNKS[j // 4]][:, j % 4, :]
                        dve.tensor_copy(dst, PS[:, j % 8, :]).then_inc(pj.sem_of(j), 1)
                        if 4 <= j < 12:
                            if j == 5:
                                dve.wait_ge(s_edge, 16)
                                pj.wait_emptied(dve, 2)
                                pj.wait_emptied(dve, 3)
                            pool_group((j - 4) // 2)

                @block.tensor
                def _(pe):
                    pe.wait_ge(s_ident, 16)
                    for t in range(T):
                        pe.wait_ge(s_x[t], 16)
                        for k in range(KD):
                            m = pe.transpose(PS[:, 2 * t + k // 4, (k % 4) * P:(k % 4 + 1) * P],
                                             X[:, t, k * P:(k + 1) * P], ident[:, :])
                        m.then_inc(s_xfull, 1)
                    pe.wait_ge(s_xl, 2 * T)
                    for j in range(PROJ):
                        n, i = j // 4, j % 4
                        c = CHUNKS[n]
                        if i == 0 and n > 0:
                            pe.wait_ge(s_wl, pieces_of(n)[-1] + 1)
                        if j >= 8:
                            pj.wait_emptied(pe, j - 8)
                        for k in range(KD):
                            if j == 0 and k % 2 == 0:
                                pe.wait_ge(s_wl, k // 2 + 1)
                            wh, wl = w_high[n % 2][:, k, :], w_low[n % 2][:, k, :]
                            xh, xl = XH[:, k, :], XL[:, k, :]
                            tile = slice(i * P, (i + 1) * P)
                            if c in (2, 3):
                                passes = ((xh[:, tile], wh), (xh[:, tile], wl), (xl[:, tile], wh))
                            else:
                                passes = ((wh[:, tile], xh), (wh[:, tile], xl), (wl[:, tile], xh))
                            for r, (lhsT, rhs) in enumerate(passes):
                                m = pe.matmul(PS[:, j % 8, :], lhsT, rhs, start=(k == 0 and r == 0),
                                              stop=(k == KD - 1 and r == 2))
                        m.then_inc(pj.full, 1)
        Stages.end()

        wide = [sb("wide0", [P, KD * D]), sb("wide1", [P, KD * D])]
        slim = [sb("slim0", [P, T * D]), sb("slim1", [P, T * D])]
        XT = sb("XT", [P, KD, SEQ])
        w_out0 = [three(slim[1][:, :], NB), three(wide[0][:, 0:4096], NB)]

        pair = [(wide[1], slim[0]), (wide[0], slim[1])]
        last_in = [lasting(f"last_gu_in{l}") for l in range(2)], [lasting(f"last_dn_in{l}") for l in range(2)]
        gu_in = [[[lasting(f"gu_in{l}{q}{u}") for u in range(2)] for q in range(2)] for l in range(2)]
        dn_in = [[lasting(f"dn_in{l}{q}") for q in range(2)] for l in range(2)]

        def load_gu(eng, l, q, e, halves=(0, 1)):
            for u in halves:
                ks = slice(u * KD // 2, (u + 1) * KD // 2)
                dst = pair[q][0][:, :].rearrange("p (e k n) -> p e k n", e=1, k=KD)[:, :, ks, :]
                src = A["moe_w_gu"][l][bass.ds(e, 1)].rearrange("e (k p) n -> p e k n", p=P)[:, :, ks, :]
                eng.dma_start(dst, src).then_inc(gu_in[l][q][u], 16)

        def load_dn(eng, l, q, e):
            src = A["moe_w_down"][l][bass.ds(e, 1)]
            eng.dma_start(pair[q][1][:, :].rearrange("p (e k n) -> p e k n", e=1, k=FF // P),
                          src.rearrange("e (k p) n -> p e k n", p=P)).then_inc(dn_in[l][q], 16)

        def load_last_gu(eng, l):
            for u, w in enumerate((w3, w4)):
                eng.dma_start(three(w[:, :], D), rows(A["moe_w_gu"][l, NE - 1, u * NB:(u + 1) * NB, :], D))\
                   .then_inc(last_in[0][l], 16)

        def load_last_dn(eng, l):
            eng.dma_start(three(XT[:, :, :].rearrange("p k s -> p (k s)"), D), rows(A["moe_w_down"][l, NE - 1], D))\
               .then_inc(last_in[1][l], 16)

        ST = [[w4[:, b * 1280 + o:b * 1280 + o + n] for o, n in ((0, 512), (512, 384), (896, 256), (1152, 128))]
              for b in range(2)]
        RN = three(wide[0][:, 4096:6144], NB)
        PW = three(wide[0][:, 6144:6656], P)
        MT = XT
        SB = [PS[:, 4 + kb, 0:SEQ - kb * P] for kb in range(3)] + [PS[:, 6, 2 * P:3 * P]]

        s_score = sem("s_score")
        s_st = sem("s_st")
        s_o = sem("s_o")
        s_gvar = sem("s_gvar")
        s_gstd = sem("s_gstd")
        s_rn = sem("s_rn")
        LAST = [("map", 0), ("map", 1), ("turn", 0), ("map", 2), ("turn", 1), ("map", 3), ("turn", 2), ("turn", 3)]
        mt = Jobs("mixed", ["act"] * len(LAST))

        with nc.Block() as block:
            @block.sync
            def _(sp):
                sp.dma_start(PW, A["pool_w"][0].rearrange("g c d -> c g d")).then_inc(s_pool, 16)
                sp.dma_start(w_out0[0], rows(A["ab_w_out"][0, :, 0:NB], NB)).then_inc(s_wout[0], 16)
                sp.dma_start(w_out0[1], rows(A["ab_w_out"][0, :, NB:D], NB)).then_inc(s_wout[1], 16)
                load_gu(sp, 0, 0, 0)
                load_dn(sp, 0, 0, 0)

            @block.tensor
            def _(pe):
                def bank7(kind, i):
                    j = LAST.index((kind, i))
                    if j >= 1:
                        mt.wait_emptied(pe, j - 1)
                    if kind == "map":
                        m = pe.matmul(PS[:, 7, :], PW[:, i, :], UT[:, i, :], start=True, stop=True)
                    else:
                        pe.wait_ge(s_rn, i + 1)
                        for t in range(T):
                            m = pe.transpose(PS[:, 7, t * P:(t + 1) * P], RN[:, t, i * P:(i + 1) * P], ident[:, :])
                    m.then_inc(mt.full, 1)

                for h in range(RH + 2):
                    if h < RH:
                        for kb in range(T):
                            if h >= 1:
                                pe.wait_ge(s_st, 4 * (h - 1) + (kb + 1 if kb < 2 else 4))
                            pe.matmul(SB[kb], KT[:, h, kb * P:(kb + 1) * P],
                                      QT[:, h, kb * P:SEQ], start=True, stop=True).then_inc(s_score, 1)
                    if 1 <= h <= RH:
                        g = h - 1
                        pe.wait_ge(s_st, 4 * g + 4)
                        for t in range(T):
                            for kb in range(t + 1):
                                m = pe.matmul(PS[:, g, t * P:(t + 1) * P],
                                              ST[g % 2][kb][:, (t - kb) * P:(t - kb + 1) * P],
                                              V[:, kb, g * P:(g + 1) * P], start=(kb == 0), stop=(kb == t))
                        m.then_inc(s_o, 1)
                        if g == 0:
                            pe.wait_ge(s_pool, 16)
                        bank7("map", g)
                    if h >= 2:
                        bank7("turn", h - 2)

            @block.vector
            def _(dve):
                own = Own(dve, "own_ret")
                dve.wait_ge(s_dec, 16)
                for h in range(RH + 1):
                    if h < RH:
                        for kb in range(T):
                            dve.wait_ge(s_score, 4 * h + (kb + 1 if kb < 2 else 4))
                            if h >= 2 and kb == 0:
                                dve.wait_ge(s_o, h - 1)
                            dve.tensor_tensor(ST[h % 2][kb], SB[kb], DEC[:, h, 0:SEQ - kb * P], ALU.mult)\
                               .then_inc(s_st, 1)
                    if h >= 1:
                        g = h - 1
                        hs = slice(g * P, (g + 1) * P)
                        dve.wait_ge(s_o, g + 1)
                        for t in range(T):
                            own.mark(dve.bn_stats(stats[:, g * T + t, :], PS[:, g, t * P:(t + 1) * P]))
                        own.wait()
                        for t in range(T):
                            m = dve.bn_aggr(mv[:, g * T + t, :], stats[:, g * T + t, :])
                        m.then_inc(s_gvar, 1)
                        dve.wait_ge(s_gstd, g + 1)
                        own.done(dve.reciprocal(rstd[:, g * T:(g + 1) * T], rstd[:, g * T:(g + 1) * T]))
                        for t in range(T):
                            i = g * T + t
                            own.mark(dve.tensor_scalar(RN[:, t, hs], PS[:, g, t * P:(t + 1) * P], mv[:, i, 0:1],
                                                       rstd[:, i:i + 1], ALU.subtract, ALU.mult))
                        own.wait()
                        dve.tensor_tensor(RN[:, :, hs], RN[:, :, hs], SG[:, :, hs], ALU.mult).then_inc(s_rn, 1)

            @block.scalar
            def _(act):
                act.wait_ge(s_const, 80)
                act.wait_ge(s_gain, 32)
                for j, (kind, i) in enumerate(LAST):
                    mt.wait_full(act, j)
                    k = i if kind == "turn" else 4 + i
                    act.activation(MT[:, k, :], PS[:, 7, :], ACT.Copy, scale=gains[:, k:k + 1])\
                       .then_inc(mt.sem_of(j), 1)
                    if kind == "map":
                        act.wait_ge(s_gvar, i + 1)
                        gs = slice(i * T, (i + 1) * T)
                        act.activation(rstd[:, gs], mv[:, gs, 1], ACT.Sqrt, bias=eps[:, 0:1]).then_inc(s_gstd, 1)
        Stages.end()

        def route_views():
            at, views = [0], {}

            def take(name, *shape, rows=P, dt=F32):
                n = 1
                for s in shape:
                    n *= s
                words = n if dt != BF16 else n // 2
                ap = w1[0:rows, at[0]:at[0] + words]
                at[0] += words
                if dt != F32:
                    ap = ap.bitcast(dt)
                views[name] = three(ap, shape[1]) if len(shape) == 2 else ap
                return ap

            take("WR", KD, NG + NE)
            take("EL", T * NG, EPG)
            take("chosen", T * NG, EPG)
            take("slot", P)
            for name in ("G8", "gtop", "etop", "es", "gexp"):
                take(name, T, EPG)
            take("gidx", T, EPG, dt=U32)
            take("eidx", T, EPG, dt=U32)
            take("ohg", T, NG)
            for name in ("gf", "gsum", "ngmax", "gw", "diff", "ex", "ex1"):
                take(name, T)
            for name in ("ef", "pos", "gate"):
                take(name, 2, T)
            take("place_f", 2 * T)
            take("place", 2 * T, dt=U32)
            take("entry", 2 * T, 4)
            take("OH", 2 * T, NE)
            take("rank", 2 * T, NE)
            take("M", T, NE, dt=BF16)
            take("bias", NG + NE)
            take("rows", 2 * NE, dt=U32)
            views["taken"], views["put"] = views["rows"][:, 0:NE], views["rows"][:, NE:2 * NE]
            take("gate_of", NE)
            take("empty", NB)
            for name in ("cnt",):
                take(name, NE, rows=1)
            for name in ("more_key", "more_min", "flags", "keys"):
                take(name, NE * 7, rows=1)
            take("top", 16, rows=1)
            take("start_i", 16, rows=1, dt=I32)
            take("expert_i", 16, rows=1, dt=I32)
            take("n_more", 1, rows=1)
            take("n_more_i", 1, rows=1, dt=I32)
            assert at[0] <= 4096
            return views

        R = route_views()
        LG_ALL = PS[:, 0:2 * T:2, 0:NG + NE]

        def out_projection(l, mixed, w_halves, w_sems, load_first, then_load):
            n = f"out{l}"
            sums = Jobs(f"{n}_sum", ["dve"] * 8)
            norm = Norm(f"{n}_norm")
            turn = Turn(f"{n}_turn", lambda t: 2 * t)
            s_rows = sem(f"{n}_rows")
            s_wr, s_more, s_empty = sem(f"{n}_router_w"), sem(f"{n}_more"), sem(f"{n}_empty")
            with nc.Block() as block:
                @block.tensor
                def _(pe):
                    for s in w_sems:
                        pe.wait_ge(s, 16)
                    def logits(t):
                        turn.wait(pe, t)
                        for k in range(KD):
                            pe.matmul(LG_ALL[:, t, :], XT[:, k, t * P:(t + 1) * P], R["WR"][:, k, :],
                                      start=(k == 0), stop=(k == KD - 1))

                    for t in range(T):
                        for c in range(2):
                            for k in range(KD):
                                m = pe.matmul(PS[:, 2 * t + c, :], mixed[:, k, t * P:(t + 1) * P],
                                              w_halves[c][:, k, :], start=(k == 0), stop=(k == KD - 1))
                            m.then_inc(sums.full, 1)
                            if t >= 2 and c == 0:
                                if t == 2:
                                    pe.wait_ge(s_wr, 64)
                                logits(t - 2)
                        if t >= 1:
                            pe.wait_ge(norm.done, t)
                            turn.pe(pe, t - 1)
                    logits(T - 2)
                    pe.wait_ge(norm.done, T)
                    turn.pe(pe, T - 1)
                    logits(T - 1)

                @block.vector
                def _(dve):
                    own = Own(dve, f"{n}_own")
                    dve.wait_ge(s_ln, 64 * l + 32)
                    for t in range(T):
                        for c in range(2):
                            sums.wait_full(dve, 2 * t + c)
                            xs = X[:, t, c * NB:(c + 1) * NB]
                            dve.scalar_tensor_tensor(xs, xs, ALPHA, PS[:, 2 * t + c, :], ALU.mult, ALU.add)\
                               .then_inc(sums.sem_of(0), 1)
                            sums.wait_emptied(dve, 2 * t + c)
                            norm.dve_stats(dve, own, t, c)
                        norm.dve_tile(dve, own, t)

                @block.scalar
                def _(act):
                    fetch_sqrt(act)
                    for t in range(T + 1):
                        if t >= 1:
                            turn.act(act, t - 1)
                        if t < T:
                            norm.act_tile(act, t)

                @block.sync
                def _(sp):
                    sp.dma_start(R["WR"][:, :, 0:NG], rows(A["moe_w_group"][l], NG)).then_inc(s_wr, 16)
                    sp.dma_start(R["WR"][:, :, NG:NG + NE], rows(A["moe_w_expert"][l], NE)).then_inc(s_wr, 16)
                    sp.dma_start(R["bias"][:, 0:NG], A["moe_b_group"][l].partition_broadcast(P)).then_inc(s_wr, 16)
                    sp.dma_start(R["bias"][:, NG:NG + NE], A["moe_b_expert"][l].partition_broadcast(P))\
                      .then_inc(s_wr, 16)
                    load_first(sp)
                    sp.dma_start(R["slot"], A["c_slot"]).then_inc(s_more, 16)
                    sp.dma_start(R["more_key"], A["c_more"][0:1, :]).then_inc(s_more, 16)
                    sp.dma_start(R["more_min"], A["c_more"][1:2, :]).then_inc(s_more, 16)
                    sp.dma_start(R["empty"], A["c_empty"]).then_inc(s_empty, 16)
                    sp.wait_ge(s_empty, 16)
                    sp.dma_start(table.rearrange("(p s) c -> p (s c)", p=P), R["empty"]).then_inc(s_empty, 16)
                    for t in range(T):
                        sp.wait_ge(norm.done, t + 1)
                        sp.dma_start(x_rows[t * P:(t + 1) * P, :], X[:, t, :]).then_inc(s_rows, 16)
                    load_ln(sp, A["ln2_g"][l], A["ln2_b"][l], s_ln)
                    then_load(sp, sums)
                    sp.wait_ge(s_rows, 16 * T)
                    sp.wait_ge(s_wr, 64)
                    sp.wait_ge(s_more, 48)
                    sp.wait_ge(s_empty, 32)
            Stages.end()

        RK = three(PS[:, 1, 0:T * NE], NE)
        CP = PS[0:1, 3, 0:NE]
        MP = PS[:, 5, 0:2 * NE]
        GP = PS[:, 7, 0:NE]
        RS = three(w2[:, 1024:1024 + 2 * T * P], P)
        VALUES = three(w2[:, 3072:3072 + 2 * T * 2 * NE], 2 * NE)
        GATES = three(w2[:, 2048:2048 + 2 * T * NE], NE)

        def over_tiles(ap, n):
            return ap.rearrange("p (o e) -> p o e", o=1).broadcast_to([P, n, ap.shape[1]])

        def over_columns(ap, n):
            return ap.rearrange("p (t o) -> p t o", o=1).broadcast_to([P, ap.shape[1], n])

        def route(l):
            n = f"route{l}"
            s_gmax, s_gexp, s_diff, s_ex = sem(f"{n}_gmax"), sem(f"{n}_gexp"), sem(f"{n}_diff"), sem(f"{n}_ex")
            s_member, s_rank = sem(f"{n}_member"), sem(f"{n}_rank")
            s_values, s_slots = sem(f"{n}_values"), sem(f"{n}_slots")
            s_zero = sem(f"{n}_zero")
            with nc.Block() as block:
                @block.tensor
                def _(pe):
                    pe.wait_ge(s_member, 1)
                    for t in range(T):
                        for u in range(t):
                            pe.matmul(RK[:, t, :], ones[:, :], R["M"][:, u, :], start=(u == 0), stop=False)
                        m = pe.matmul(RK[:, t, :], tri[:, :], R["M"][:, t, :], start=(t == 0), stop=True)
                    m.then_inc(s_rank, 1)
                    for t in range(T):
                        m = pe.matmul(CP, ones[:, 0:1], R["M"][:, t, :], start=(t == 0), stop=(t == T - 1))
                    m.then_inc(s_rank, 1)
                    pe.wait_ge(s_values, 1)
                    for u in range(2 * T):
                        m = pe.matmul(MP, RS[:, u, :], VALUES[:, u, :], start=(u == 0), stop=(u == 2 * T - 1))
                    m.then_inc(s_slots, 1)

                @block.scalar
                def _(act):
                    act.wait_ge(s_gmax, 1)
                    for t in range(T):
                        m = act.activation(R["gexp"][:, t, :], R["G8"][:, t, :], ACT.Exp,
                                           bias=R["ngmax"][:, t:t + 1], accum_out=R["gsum"][:, t:t + 1])
                        m.then_inc(s_gexp, 1)
                    act.wait_ge(s_diff, 1)
                    act.activation(R["ex"], R["diff"], ACT.Exp).then_inc(s_ex, 1)

                @block.gpsimd
                def _(pool):
                    pool.memset(w2[:, 0:1024], 0.0).then_inc(s_zero, 1)
                    pool.wait_ge(s_zero, 1)

                @block.vector
                def _(dve):
                    own = Own(dve, f"{n}_own")
                    G8, es, ef, gf, OH = R["G8"], R["es"], R["ef"], R["gf"], R["OH"]
                    entry = R["entry"]
                    own.mark(dve.memset(G8, -BIG))
                    own.mark(dve.memset(entry, 0.0))
                    own.wait()
                    own.done(dve.tensor_tensor(G8[:, :, 0:NG], LG_ALL[:, :, 0:NG], over_tiles(R["bias"][:, 0:NG], T),
                                               ALU.add))
                    own.mark(dve.tensor_tensor(R["EL"].rearrange("p (t g) e -> p t (g e)", t=T),
                                               LG_ALL[:, :, NG:NG + NE], over_tiles(R["bias"][:, NG:NG + NE], T),
                                               ALU.add))
                    for t in range(T):
                        own.mark(dve.max(R["gtop"][:, t, :], G8[:, t, :]))
                    own.wait()
                    dve.tensor_scalar(R["ngmax"], R["gtop"][:, :, 0], -1.0, None, ALU.mult).then_inc(s_gmax, 1)
                    for t in range(T):
                        own.mark(dve.max_index(R["gidx"][:, t, :], R["gtop"][:, t, :], G8[:, t, :]))
                    own.wait()
                    own.done(dve.tensor_copy(gf, R["gidx"][:, :, 0]))
                    own.done(dve.tensor_tensor(R["ohg"], over_tiles(iota[:, 0:NG], T), over_columns(gf, NG),
                                               ALU.is_equal))
                    own.done(dve.tensor_tensor(R["chosen"], R["EL"],
                                               over_columns(R["ohg"].rearrange("p t g -> p (t g)"), EPG), ALU.mult))
                    own.done(dve.tensor_reduce(es, R["chosen"].rearrange("p (t g) e -> p t e g", t=T), AX.X, ALU.add))
                    for t in range(T):
                        own.mark(dve.max(R["etop"][:, t, :], es[:, t, :]))
                    own.wait()
                    dve.tensor_tensor(R["diff"], R["etop"][:, :, 1], R["etop"][:, :, 0], ALU.subtract)\
                       .then_inc(s_diff, 1)
                    for t in range(T):
                        own.mark(dve.max_index(R["eidx"][:, t, :], R["etop"][:, t, :], es[:, t, :]))
                    own.wait()
                    for j in range(2):
                        own.mark(dve.tensor_copy(ef[:, j, :], R["eidx"][:, :, j]))
                    own.wait()
                    for j in range(2):
                        own.mark(dve.scalar_tensor_tensor(ef[:, j, :], gf, float(EPG), ef[:, j, :],
                                                          ALU.mult, ALU.add))
                    own.wait()
                    own.done(dve.tensor_tensor(OH, over_tiles(iota[:, :], 2 * T),
                                               over_columns(ef.rearrange("p j t -> p (j t)"), NE), ALU.is_equal))
                    dve.tensor_tensor(R["M"], OH[:, 0:T, :], OH[:, T:2 * T, :], ALU.add).then_inc(s_member, 1)
                    for j in range(2):
                        js = slice(j * T, (j + 1) * T)
                        own.mark(dve.tensor_copy(entry[:, js, 0], tok_col[:, :]))
                        own.mark(dve.tensor_scalar(entry[:, js, 1], tok_col[:, :], float(j * SEQ), None, ALU.add))
                    own.wait()
                    for k in range(2):
                        own.mark(dve.scalar_tensor_tensor(VALUES[:, :, k * NE:(k + 1) * NE],
                                                          over_columns(entry[:, :, k], NE), float(NOWHERE), OH,
                                                          ALU.subtract, ALU.mult))
                    dve.wait_ge(s_rank, 1)
                    for j in range(2):
                        own.mark(dve.tensor_tensor(R["rank"][:, j * T:(j + 1) * T, :], OH[:, j * T:(j + 1) * T, :], RK,
                                                   ALU.mult))
                    own.wait()
                    pos = R["pos"].rearrange("p j t -> p (j t)")
                    own.done(dve.tensor_reduce(pos, R["rank"], AX.X, ALU.add))
                    dve.tensor_tensor(RS, over_tiles(R["slot"], 2 * T), over_columns(pos, P), ALU.is_equal)\
                       .then_inc(s_values, 1)
                    dve.wait_ge(s_gexp, T)
                    own.mark(dve.reciprocal(R["gw"], R["gsum"]))
                    dve.wait_ge(s_ex, 1)
                    own.done(dve.tensor_scalar(R["ex1"], R["ex"], 1.0, None, ALU.add))
                    own.done(dve.reciprocal(R["ex1"], R["ex1"]))
                    own.done(dve.tensor_tensor(R["gate"][:, 0, :], R["ex1"], R["gw"], ALU.mult))
                    own.done(dve.tensor_tensor(R["gate"][:, 1, :], R["ex"], R["gate"][:, 0, :], ALU.mult))
                    gates = R["gate"].rearrange("p j t -> p (j t)")
                    own.mark(dve.tensor_tensor(GATES, over_columns(gates, NE), OH, ALU.mult))
                    own.mark(dve.tensor_copy(entry[:, :, 2], gates))
                    dve.wait_ge(s_slots, 1)
                    own.mark(dve.scalar_tensor_tensor(R["rows"], MP, 2.0,
                                                      half_col[:, 1:2].broadcast_to([P, 2 * NE]), ALU.mult, ALU.add))
                    own.wait()
            Stages.end()

        x_half = x_rows.rearrange("t (u c) -> (t u) c", u=2)
        xg = [w2[:, 0:512], w2[:, 512:1024]]
        xeT = [three(w2[:, 1024:1536], SLOTS), three(w2[:, 1536:2048], SLOTS)]
        sa, ga = w2[:, 2048:2304], w2[:, 2304:2560]
        gT = three(w2[:, 2560:2816], SLOTS)
        take1 = [w2[:, 2816 + q:2817 + q].bitcast(U32) for q in range(2)]
        put1 = [w2[:, 2820 + q:2821 + q].bitcast(U32) for q in range(2)]
        meta1 = w2[:, 2824:2828]
        ys = [w2[:, 3072:3584], w2[:, 3584:4096]]

        def wait_alone(eng, semaphore, value, tick):
            eng.wait_ge(semaphore, value)
            eng.sem_inc(tick, 1)

        def gather(pool, q, index, s):
            pool.indirect_dma_start(out=xg[q], out_offset=None, in_=x_half,
                                    in_offset=bass.IndirectOffsetOnAxis(ap=index, axis=0),
                                    bounds_check=2 * SEQ - 1, oob_is_err=False).then_inc(s, 16)

        def scatter(pool, q, index, s):
            pool.indirect_dma_start(out=y_rows, out_offset=bass.IndirectOffsetOnAxis(ap=index, axis=0),
                                    in_=ys[q], in_offset=None, bounds_check=4 * SEQ - 1, oob_is_err=False)\
                .then_inc(s, 16)

        def turn_gathered(pe, q):
            for c in range(4):
                m = pe.transpose(PS[:, q, c * P:(c + 1) * P], xg[q][:, c * P:(c + 1) * P], ident[:, :])
            return m

        def chunks(*areas):
            return [three(a[:, :], D)[:, k, :] for a in areas for k in range(a.shape[1] // D)]

        gu_of = [chunks(pair[q][0]) for q in range(2)]
        dn_of = [chunks(pair[q][1]) for q in range(2)]
        last_gu, last_dn = chunks(w3, w4), chunks(XT[:, :, :].rearrange("p k s -> p (k s)"))

        def gate_up(pe, q, gu, half):
            for k in range(half * KD // 2, (half + 1) * KD // 2):
                for u in range(2):
                    m = pe.matmul(PS[u * SLOTS:(u + 1) * SLOTS, 2 + q, :], xeT[q][:, k, :],
                                  gu[k].rearrange("p (a u c) -> p a u c", a=2, u=2)[:, :, u, :],
                                  start=(k == 0), stop=(k == KD - 1))
            return m

        def turn_gated(pe, q):
            for c in range(2):
                m = pe.transpose(PS[:, 4 + q, c * P:(c + 1) * P], ga[:, c * P:(c + 1) * P], ident[:, :])
            return m

        def down(pe, q, dn):
            for k in range(FF // P):
                for u in range(2):
                    m = pe.matmul(PS[u * SLOTS:(u + 1) * SLOTS, 6 + q, :], gT[:, k, :],
                                  dn[k][:, u * NB:(u + 1) * NB], start=(k == 0), stop=(k == FF // P - 1))
            return m

        def copy_gathered(act, q):
            return act.activation(xeT[q].rearrange("p (u c) s -> p c u s", u=2),
                                  PS[:, q, :].rearrange("p (c u s) -> p c u s", c=4, u=2), ACT.Copy)

        def silu(act, q):
            return act.activation(sa, PS[:, 2 + q, 0:FF // 2], ACT.Silu)

        def times_up(dve, q):
            return dve.tensor_tensor(ga, sa, PS[:, 2 + q, FF // 2:FF], ALU.mult)

        def copy_gated(dve, q):
            return dve.tensor_copy(gT.rearrange("p (u c) s -> p c u s", u=2),
                                   PS[:, 4 + q, 0:2 * P].rearrange("p (c u s) -> p c u s", c=2, u=2))

        def list_further(dve, own, s_gates, s_place):
            ef = R["ef"]
            dve.wait_ge(s_gates, 1)
            own.mark(dve.tensor_copy(R["gate_of"], GP))
            own.done(dve.scalar_tensor_tensor(three(R["place_f"], T), ef, float(TABLE), R["pos"],
                                              ALU.mult, ALU.add))
            dve.tensor_copy(R["place"], R["place_f"]).then_inc(s_place, 1)
            own.done(dve.tensor_copy(R["cnt"], CP))
            own.done(dve.tensor_tensor(three(R["flags"], 7),
                                       R["cnt"].rearrange("p (e b) -> p e b", b=1).broadcast_to([1, NE, 7]),
                                       three(R["more_min"], 7), ALU.is_gt))
            own.done(dve.tensor_reduce(R["n_more"], R["flags"], AX.X, ALU.add))
            own.mark(dve.tensor_copy(R["n_more_i"], R["n_more"]))
            own.done(dve.tensor_tensor(R["keys"], R["flags"], R["more_key"], ALU.mult))
            own.done(dve.max(R["top"][:, 0:8], R["keys"]))
            own.done(dve.match_replace(R["keys"], R["top"][:, 0:8], R["keys"], 0.0))
            own.done(dve.max(R["top"][:, 8:16], R["keys"]))
            own.done(dve.tensor_scalar(R["top"], R["top"], -1.0, float(NE * TABLE), ALU.mult, ALU.add))
            own.done(dve.tensor_copy(R["start_i"], R["top"]))
            own.done(dve.tensor_scalar(R["expert_i"], R["start_i"], 9, None, ALU.arith_shift_right))

        class Further:

            def __init__(self, l):
                names = ("listed", "meta", "idx", "gath", "turn", "xe", "gu_in", "dn_in", "gu", "silu", "gated",
                         "gturn", "gt", "dn", "y", "scat", "sp", "dve", "pool", "pool_end", "pe", "act")
                self.s = {k: (lasting if k in ("gath", "scat") else sem)(f"more{l}_{k}") for k in names}
                self.l = l

            def count(self, eng):
                eng.wait_ge(self.s["listed"], 1)
                return eng.value_load(R["n_more_i"], min_val=0, max_val=MORE)

            def run(self, eng, count, body, tick, before=lambda: None):
                with eng.If(count > 0):
                    before()
                    with eng.Fori(0, count) as i:
                        body(i)
                        wait_alone(eng, self.s["scat"], 16 * i + 16, tick)

            def sp(self, sp, count, before):
                s = self.s
                gu, dn = pair[0]
                def body(i):
                    e = sp.value_load(R["expert_i"][:, bass.ds(i, 1)], min_val=0, max_val=NE - 1)
                    row = sp.value_load(R["start_i"][:, bass.ds(i, 1)], min_val=0, max_val=NE * TABLE - SLOTS)
                    for u in range(2):
                        sp.dma_start(meta1[u * SLOTS:(u + 1) * SLOTS, :], table[bass.ds(row, SLOTS), :])\
                          .then_inc(s["meta"], 16)
                    sp.dma_start(gu[:, :].rearrange("p (e k n) -> p e k n", e=1, k=KD),
                                 A["moe_w_gu"][self.l][bass.ds(e, 1)].rearrange("e (k p) n -> p e k n", p=P))\
                      .then_inc(s["gu_in"], 16)
                    sp.dma_start(dn[:, :].rearrange("p (e k n) -> p e k n", e=1, k=FF // P),
                                 A["moe_w_down"][self.l][bass.ds(e, 1)].rearrange("e (k p) n -> p e k n", p=P))\
                      .then_inc(s["dn_in"], 16)
                self.run(sp, count, body, s["sp"], before)

            def dve(self, dve, count, before):
                s = self.s
                def body(i):
                    dve.wait_ge(s["meta"], 32 * i + 32)
                    dve.scalar_tensor_tensor(take1[1], meta1[:, 0:1], 2.0, half_col[:, 0:1], ALU.mult, ALU.add)\
                       .then_inc(s["idx"], 1)
                    dve.scalar_tensor_tensor(put1[1], meta1[:, 1:2], 2.0, half_col[:, 0:1], ALU.mult, ALU.add)\
                       .then_inc(s["idx"], 1)
                    dve.wait_ge(s["silu"], i + 1)
                    times_up(dve, 1).then_inc(s["gated"], 1)
                    dve.wait_ge(s["gturn"], i + 1)
                    copy_gated(dve, 1).then_inc(s["gt"], 1)
                self.run(dve, count, body, s["dve"], before)

            def pool(self, pool, count):
                s = self.s
                def body(i):
                    wait_alone(pool, s["idx"], 2 * i + 2, s["pool"])
                    gather(pool, 1, take1[1], s["gath"])
                    wait_alone(pool, s["y"], i + 1, s["pool"])
                    scatter(pool, 1, put1[1], s["scat"])
                self.run(pool, count, body, s["pool_end"])

            def pe(self, pe, count):
                s = self.s
                def body(i):
                    pe.wait_ge(s["gath"], 16 * i + 16)
                    turn_gathered(pe, 1).then_inc(s["turn"], 1)
                    pe.wait_ge(s["xe"], i + 1)
                    pe.wait_ge(s["gu_in"], 16 * i + 16)
                    gate_up(pe, 1, gu_of[0], 0)
                    gate_up(pe, 1, gu_of[0], 1).then_inc(s["gu"], 1)
                    pe.wait_ge(s["gated"], i + 1)
                    turn_gated(pe, 1).then_inc(s["gturn"], 1)
                    pe.wait_ge(s["gt"], i + 1)
                    pe.wait_ge(s["dn_in"], 16 * i + 16)
                    down(pe, 1, dn_of[0]).then_inc(s["dn"], 1)
                self.run(pe, count, body, s["pe"])

            def act(self, act, count):
                s = self.s
                def body(i):
                    act.wait_ge(s["turn"], i + 1)
                    copy_gathered(act, 1).then_inc(s["xe"], 1)
                    act.wait_ge(s["gu"], i + 1)
                    silu(act, 1).then_inc(s["silu"], 1)
                    act.wait_ge(s["dn"], i + 1)
                    act.wait_ge(s["meta"], 32 * i + 32)
                    act.activation(ys[1], PS[:, 7, :], ACT.Copy, scale=meta1[:, 2:3]).then_inc(s["y"], 1)
                self.run(act, count, body, s["act"])

        def experts(l, then_load):
            n = f"moe{l}"
            PAIRS = NE // 2
            END = PAIRS - 2

            def expert(q, i):
                return {(0, END): NE - 1, (1, END): NE - 4, (0, END + 1): NE - 3, (1, END + 1): NE - 2}[q, i] \
                    if isinstance(i, int) and i >= END else 2 * i + q

            def area(q, i):
                if isinstance(i, int) and i >= END:
                    return {(0, END): (None, 0), (1, END): (0, END), (0, END + 1): (1, END),
                            (1, END + 1): (0, END + 1)}[q, i]
                return q, i

            def both(name, new=sem):
                return [new(f"{n}_{name}{q}") for q in range(2)]

            s_take, s_gath, s_turn, s_xe = both("take"), both("gath", lasting), both("turn"), both("xe")
            s_gu_half = both("gu_half")
            s_gu, s_silu, s_gated, s_gturn = both("gu"), both("silu"), both("gated"), both("gturn")
            sp_tick, pool_tick = sem(f"{n}_sp_tick"), sem(f"{n}_pool_tick")
            s_tab, s_place = lasting(f"{n}_tab"), sem(f"{n}_place")
            further, s_gates = Further(l), sem(f"{n}_gates")
            s_gt, s_dn, s_y, s_put, s_scat = both("gt"), both("dn"), both("y"), both("put"), both("scat", lasting)
            with nc.Block() as block:
                @block.sync
                def _(sp):
                    sp.wait_ge(s_gath[1], 16)
                    load_last_dn(sp, l)
                    more = further.count(sp)
                    with sp.Fori(1, END) as i:
                        for q in range(2):
                            wait_alone(sp, s_gu_half[q], i, sp_tick)
                            load_gu(sp, l, q, 2 * i + q, halves=(0,))
                            wait_alone(sp, s_gu[q], i, sp_tick)
                            load_gu(sp, l, q, 2 * i + q, halves=(1,))
                            wait_alone(sp, s_dn[q], i, sp_tick)
                            load_dn(sp, l, q, 2 * i + q)
                    for a, e, (q, i) in ((0, NE - 4, (0, END - 1)), (1, NE - 3, (1, END - 1)), (0, NE - 2, (1, END))):
                        sp.wait_ge(s_gu_half[q], i + 1)
                        load_gu(sp, l, a, e, halves=(0,))
                        sp.wait_ge(s_gu[q], i + 1)
                        load_gu(sp, l, a, e, halves=(1,))
                        sp.wait_ge(s_dn[q], i + 1)
                        load_dn(sp, l, a, e)
                    sp.wait_ge(s_gu[0], PAIRS)
                    sp.wait_ge(s_dn[0], PAIRS)
                    then_load(sp)

                    def areas_and_table():
                        sp.wait_ge(s_gu[1], PAIRS)
                        sp.wait_ge(s_dn[1], PAIRS)
                        sp.wait_ge(s_tab, 16 * 2 * T)
                    further.sp(sp, more, areas_and_table)

                @block.gpsimd
                def _(pool):
                    def take_rows(q, i, first=False):
                        if not first:
                            wait_alone(pool, s_turn[q], i, pool_tick)
                        pool.tensor_copy(take1[q], R["taken"][:, bass.ds(expert(q, i), 1)])\
                            .then_inc(s_take[q], 1)
                        wait_alone(pool, s_take[q], i + 1, pool_tick)
                        gather(pool, q, take1[q], s_gath[q])

                    def put_rows(q, i):
                        wait_alone(pool, s_y[q], i + 1, pool_tick)
                        pool.tensor_copy(put1[q], R["put"][:, bass.ds(expert(q, i), 1)]).then_inc(s_put[q], 1)
                        wait_alone(pool, s_put[q], i + 1, pool_tick)
                        scatter(pool, q, put1[q], s_scat[q])

                    take_rows(0, 0, first=True)
                    take_rows(1, 0, first=True)
                    pool.wait_ge(s_place, 1)
                    for c in range(2 * T):
                        pool.indirect_dma_start(
                            out=table, out_offset=bass.IndirectOffsetOnAxis(ap=R["place"][:, c:c + 1], axis=0),
                            in_=R["entry"][:, c, :], in_offset=None).then_inc(s_tab, 16)
                    more = further.count(pool)
                    with pool.Fori(0, END - 1) as i:
                        for q in range(2):
                            take_rows(q, i + 1)
                            put_rows(q, i)
                    for i in range(END - 1, PAIRS):
                        for q in range(2):
                            if i + 1 < PAIRS:
                                take_rows(q, i + 1)
                            put_rows(q, i)
                    pool.wait_ge(s_tab, 16 * 2 * T)
                    for q in range(2):
                        pool.wait_ge(s_scat[q], 16 * PAIRS)
                    further.pool(pool, more)

                @block.tensor
                def _(pe):
                    def one(q, i, first=False):
                        a, loads = area(q, i)
                        pe.wait_ge(s_gath[q], 16 * i + 16)
                        turn_gathered(pe, q).then_inc(s_turn[q], 1)
                        pe.wait_ge(s_xe[q], i + 1)
                        for half, done in enumerate((s_gu_half, s_gu)):
                            if a is None:
                                pe.wait_ge(last_in[0][l], 32)
                            else:
                                pe.wait_ge(gu_in[l][a][half], 16 * loads + 16)
                            gate_up(pe, q, last_gu if a is None else gu_of[a], half).then_inc(done[q], 1)
                        pe.wait_ge(s_gated[q], i + 1)
                        turn_gated(pe, q).then_inc(s_gturn[q], 1)
                        pe.wait_ge(s_gt[q], i + 1)
                        if a is None:
                            pe.wait_ge(last_in[1][l], 16)
                        else:
                            pe.wait_ge(dn_in[l][a], 16 * loads + 16)
                        if first:
                            pe.wait_ge(s_place, 1)
                        else:
                            pe.wait_ge(s_y[q], i)
                        down(pe, q, last_dn if a is None else dn_of[a]).then_inc(s_dn[q], 1)

                    for u in range(2 * T):
                        m = pe.matmul(GP, RS[:, u, :], GATES[:, u, :], start=(u == 0), stop=(u == 2 * T - 1))
                    m.then_inc(s_gates, 1)
                    one(0, 0, first=True)
                    one(1, 0, first=True)
                    more = further.count(pe)
                    with pe.Fori(1, END) as i:
                        one(0, i)
                        one(1, i)
                    for i in (END, END + 1):
                        one(0, i)
                        one(1, i)
                    further.pe(pe, more)

                @block.scalar
                def _(act):
                    def one(q, i, first=False):
                        act.wait_ge(s_turn[q], i + 1)
                        copy_gathered(act, q).then_inc(s_xe[q], 1)
                        act.wait_ge(s_gu[q], i + 1)
                        if q == 1:
                            act.wait_ge(s_gated[0], i + 1)
                        elif not first:
                            act.wait_ge(s_gated[1], i)
                        silu(act, q).then_inc(s_silu[q], 1)
                        act.wait_ge(s_dn[q], i + 1)
                        if first:
                            act.wait_ge(s_place, 1)
                        else:
                            act.wait_ge(s_scat[q], 16 * i)
                        act.activation(ys[q], PS[:, 6 + q, :], ACT.Copy,
                                       scale=R["gate_of"][:, bass.ds(expert(q, i), 1)]).then_inc(s_y[q], 1)

                    one(0, 0, first=True)
                    one(1, 0, first=True)
                    more = further.count(act)
                    with act.Fori(1, END) as i:
                        one(0, i)
                        one(1, i)
                    for i in (END, END + 1):
                        one(0, i)
                        one(1, i)
                    further.act(act, more)

                @block.vector
                def _(dve):
                    def one(q, i, first=False):
                        dve.wait_ge(s_silu[q], i + 1)
                        times_up(dve, q).then_inc(s_gated[q], 1)
                        dve.wait_ge(s_gturn[q], i + 1)
                        if q == 1:
                            dve.wait_ge(s_dn[0], i + 1)
                        elif not first:
                            dve.wait_ge(s_dn[1], i)
                        copy_gated(dve, q).then_inc(s_gt[q], 1)

                    list_further(dve, Own(dve, f"{n}_own"), s_gates, s_place)
                    dve.sem_inc(further.s["listed"], 1)
                    one(0, 0, first=True)
                    one(1, 0, first=True)
                    more = further.count(dve)
                    with dve.Fori(1, END) as i:
                        one(0, i)
                        one(1, i)
                    for i in (END, END + 1):
                        one(0, i)
                        one(1, i)
                    further.dve(dve, more, lambda: dve.wait_ge(s_scat[1], 16 * PAIRS))
            Stages.end()

        Y0, Y1 = three(w3[:, :], D), three(w4[:, :], D)
        PTOK = three(pair[1][1][:, 2 * D:2 * D + T * PLE], PLE)
        PTR = three(w1[:, 1024:2048], SEQ)
        sig = [w1[:, 2048 + b * NB:2048 + (b + 1) * NB] for b in range(4)]
        PWP = three(w2[:, :], NB)

        def load_injection(eng, l, s_wp):
            eng.dma_start(three(pair[1][1][:, 0:2 * D], D), rows(A["ple_w_proj"][l], D)).then_inc(s_wp, 16)
            eng.dma_start(PTOK, A["p"][l, 0].rearrange("(t p) c -> p t c", p=P)).then_inc(s_wp, 16)

        def injection(l, s_wg, s_wp, loads, after_tile, turn_after):
            n = f"inj{l}"
            wg, wp = three(pair[1][0][:, :], D), three(pair[1][1][:, 0:2 * D], D)
            s_y = [sem(f"{n}_y{t}") for t in range(T)]
            s_pt, s_ptc = sem(f"{n}_pt"), sem(f"{n}_ptc")
            s_pw, s_pwc = sem(f"{n}_pw"), sem(f"{n}_pwc")
            EARLY = 6
            s_unit, s_sig, s_done = sem(f"{n}_unit"), sem(f"{n}_sig"), sem(f"{n}_done")
            norm = Norm(f"{n}_norm")
            turn = Turn(f"{n}_turn", lambda t: 0)
            turn2 = Turn(f"{n}_turn2", lambda t: 0) if turn_after else None
            y_tok = y_rows.rearrange("(j t u) c -> j t (u c)", j=2, u=2)
            U = 2 * T
            with nc.Block() as block:
                @block.sync
                def _(sp):
                    for t in range(T):
                        for j, Y in enumerate((Y0, Y1)):
                            sp.dma_start(Y[:, t, :], y_tok[j, t * P:(t + 1) * P, :]).then_inc(s_y[t], 16)
                        if t in (1, 2):
                            cs = slice((t - 1) * NB, t * NB)
                            sp.dma_start(wg[:, :, cs], rows(A["ple_w_gate"][l, :, cs], NB)).then_inc(s_wg[t - 1], 16)
                    sp.wait_ge(s_pt, 1)
                    loads(sp, norm)
                    after_tile(sp, s_done)

                @block.tensor
                def _(pe):
                    def project(u):
                        if u >= 6:
                            pe.wait_ge(s_pwc, u - 5)
                        t, c = u // 2, u % 2
                        for k in range(2):
                            m = pe.matmul(PS[:, 2 + u % 6, :], PTR[:, k, t * P:(t + 1) * P],
                                          wp[:, k, c * NB:(c + 1) * NB], start=(k == 0), stop=(k == 1))
                        m.then_inc(s_pw, 1)

                    pe.wait_ge(s_wp, 32)
                    for k in range(2):
                        for t in range(T):
                            m = pe.transpose(PS[:, 2 + k, t * P:(t + 1) * P], PTOK[:, t, k * P:(k + 1) * P],
                                             ident[:, :])
                    m.then_inc(s_pt, 1)
                    pe.wait_ge(s_ptc, 2)
                    for u in range(EARLY):
                        project(u)
                    def gates(u):
                        if u < 6:
                            pe.wait_ge(s_pwc, min(u + 7, U))
                        else:
                            pe.wait_ge(s_sig, u - 5)
                        t, c = u // 2, u % 2
                        if t == 0:
                            pe.wait_ge(s_wg[c], 16)
                        for k in range(KD):
                            m = pe.matmul(PS[:, 2 + u % 6, :], XT[:, k, t * P:(t + 1) * P],
                                          wg[:, k, c * NB:(c + 1) * NB], start=(k == 0), stop=(k == KD - 1))
                        m.then_inc(s_unit, 1)

                    def turn_back(t):
                        if turn2:
                            turn.wait(pe, T - 1)
                            if t >= 1:
                                turn2.wait(pe, t - 1)
                            pe.wait_ge(s_done, 2 * t + 2)
                            turn2.pe(pe, t)

                    pe.wait_ge(norm.done, 1)
                    turn.pe(pe, 0)
                    for u in range(EARLY, U):
                        project(u)
                    for t in range(T):
                        turn.wait(pe, t)
                        gates(2 * t)
                        if t + 1 < T:
                            pe.wait_ge(norm.done, t + 2)
                            turn.pe(pe, t + 1)
                        else:
                            turn_back(1)
                        gates(2 * t + 1)
                        if t == T - 2:
                            turn_back(0)
                    turn_back(2)
                    turn_back(3)

                @block.scalar
                def _(act):
                    fetch_sqrt(act)

                    def keep(units):
                        for u in units:
                            act.wait_ge(s_pw, u + 1)
                            act.activation(PWP[:, u, :], PS[:, 2 + u % 6, :], ACT.Copy).then_inc(s_pwc, 1)

                    act.wait_ge(s_pt, 1)
                    act.activation(PTR[:, 0, :], PS[:, 2, :], ACT.Copy).then_inc(s_ptc, 1)
                    keep(range(3))
                    norm.act_tile(act, 0)
                    keep(range(3, EARLY))
                    turn.act(act, 0)
                    keep(range(EARLY, U))
                    norm.act_tile(act, 1)

                    def gate(u):
                        act.wait_ge(s_unit, u + 1)
                        if u >= 4:
                            act.wait_ge(s_done, u - 3)
                        act.activation(sig[u % 4], PS[:, 2 + u % 6, :], ACT.Sigmoid).then_inc(s_sig, 1)

                    for t in range(T):
                        if t + 1 < T:
                            turn.act(act, t + 1)
                        if t + 2 < T:
                            norm.act_tile(act, t + 2)
                        gate(2 * t)
                        if t == T - 1 and turn2:
                            turn2.act(act, 1)
                        gate(2 * t + 1)
                        if t == T - 2 and turn2:
                            turn2.act(act, 0)
                    if turn2:
                        turn2.act(act, 2)
                        turn2.act(act, 3)

                @block.vector
                def _(dve):
                    own = Own(dve, f"{n}_own")
                    dve.wait_ge(s_pt, 1)
                    dve.tensor_copy(PTR[:, 1, :], PS[:, 3, :]).then_inc(s_ptc, 1)
                    dve.wait_ge(s_ln, 64 * l + 64)
                    for t in range(T + 2):
                        if t < T:
                            dve.wait_ge(s_y[t], 32)
                            own.done(dve.scalar_tensor_tensor(X[:, t, :], X[:, t, :], ALPHA, Y0[:, t, :],
                                                              ALU.mult, ALU.add))
                            own.done(dve.tensor_tensor(X[:, t, :], X[:, t, :], Y1[:, t, :], ALU.add))
                            for c in range(2):
                                norm.dve_stats(dve, own, t, c)
                            norm.dve_tile(dve, own, t)
                        if t == 2:
                            dve.wait_ge(s_pwc, U)
                        if t >= 2:
                            for c in range(2):
                                u = 2 * (t - 2) + c
                                dve.wait_ge(s_sig, u + 1)
                                own.done(dve.tensor_tensor(sig[u % 4], sig[u % 4], PWP[:, u, :], ALU.mult))
                                xs = X[:, t - 2, c * NB:(c + 1) * NB]
                                dve.tensor_tensor(xs, xs, sig[u % 4], ALU.add).then_inc(s_done, 1)
            Stages.end()

        CW = three(wide[1][:, :], D)
        WKI = three(w4[:, 0:KD * (HD + IH)], HD + IH)
        WIT = w4[HD:HD + IH, 1088:1600]
        UQ, UK = three(slim[0][:, 0:2048], D), three(slim[0][:, 2048:4096], D)
        UV = three(slim[1][:, 2048:4096], D)
        CQ = three(w1[:, 0:2048], NB)
        CT = three(w1[:, 2048:4096], SEQ)
        QI = three(w2[:, 0:2048], SEQ)
        KI = three(w2[:, 2048:3072], SEQ)
        QH = wide[1][:, :].rearrange("p (u c s) -> p u c s", u=2, c=8)
        KH = three(w4[:, :], SEQ)
        VH = three(XT[:, :, :].rearrange("p k s -> p (k s)"), D)
        WI = three(w2[:, 3072:3104], IH)
        squares = w2[:, 3104:3360]
        sq = w2[:, 3360:3376]
        m8 = {1: w2[:, 3376:3384], 2: w2[:, 3384:3392], 3: w2[:, 3392:3400]}
        SEL = list(range(1, T))
        width = [(t + 1) * P for t in range(T)]
        at = {1: 0, 2: 256, 3: 640}
        IS = {t: w3[:, at[t]:at[t] + width[t]] for t in SEL}
        WK = {t: slim[1][:, at[t]:at[t] + width[t]] for t in SEL}
        relu = [slim[1][:, 1152:1664], w2[:, 3584:4096]]
        DIST = dist[:, :]
        s_cw, s_ki, s_up = lasting("s_cw"), lasting("s_ki"), lasting("s_up")
        s_uv, s_cwout = lasting("s_uv"), lasting("s_cwout")
        s_cgain, s_dist = lasting("s_cgain"), lasting("s_dist")

        def load_latent_weights(sp):
            sp.dma_start(CW, rows(A["c_w_in"][0, :, 0:D], D)).then_inc(s_cw, 16)
            sp.dma_start(UQ, rows(A["c_w_uq"][0], D)).then_inc(s_up, 16)
            sp.dma_start(UK, rows(A["c_w_uk"][0].rearrange("c h d -> c (h d)"), D)).then_inc(s_up, 16)
            sp.dma_start(UV, rows(A["c_w_uv"][0].rearrange("c h d -> c (h d)"), D)).then_inc(s_uv, 16)

        def load_indexer_weights(sp):
            sp.dma_start(WKI, rows(A["c_w_in"][0, :, D:D + HD + IH], HD + IH)).then_inc(s_ki, 16)
            sp.dma_start(gains[:, 8:10], A["c_q_norm"][0].rearrange("(k p) -> p k", p=P)).then_inc(s_cgain, 16)
            sp.dma_start(gains[:, 10:12], A["c_kv_norm"][0].rearrange("(k p) -> p k", p=P)).then_inc(s_cgain, 16)

        def latents():
            n = "lat"
            s_full, s_sq, s_rms, s_cq = sem(f"{n}_full"), sem(f"{n}_sq"), sem(f"{n}_rms"), sem(f"{n}_cq")
            s_key, s_keyc, s_wtc = sem(f"{n}_key"), sem(f"{n}_keyc"), sem(f"{n}_wtc")
            s_qi, s_qic = sem(f"{n}_qi"), sem(f"{n}_qic")
            s_ct, s_ctc = sem(f"{n}_ct"), sem(f"{n}_ctc")
            s_wi, s_wic = sem(f"{n}_wi"), sem(f"{n}_wic")
            s_is, s_relu, s_acc, s_mask = sem(f"{n}_is"), sem(f"{n}_relu"), sem(f"{n}_acc"), sem(f"{n}_mask")
            s_half, s_inv = sem(f"{n}_half"), sem(f"{n}_inv")
            up = Jobs(f"{n}_up", ["act"] * 24)
            units = [(t, h) for h in range(IH) for t in SEL]
            per_chunk = 2 * len(SEL)
            with nc.Block() as block:
                @block.sync
                def _(sp):
                    sp.dma_start(three(wide[0][:, :], D), rows(A["c_w_out"][0], D)).then_inc(s_cwout, 16)
                    sp.dma_start(DIST, A["c_dist"]).then_inc(s_dist, 16)

                @block.tensor
                def _(pe):
                    def queries(c):
                        for k in range(KD):
                            m = pe.matmul(PS[:, c, :], CW[:, k, NB + c * P:NB + (c + 1) * P], XT[:, k, :],
                                          start=(k == 0), stop=(k == KD - 1))
                        m.then_inc(s_qi, 1)

                    def scores(c):
                        pe.wait_ge(s_qic, c + 1)
                        for i in range(per_chunk * c, per_chunk * (c + 1)):
                            t, h = units[i]
                            if i >= 2:
                                pe.wait_ge(s_relu, i - 1)
                            pe.matmul(PS[:, 6 + i % 2, 0:width[t]], QI[:, h // 2, t * P:(t + 1) * P],
                                      KI[:, h % 2, 0:width[t]], start=True, stop=True).then_inc(s_is, 1)

                    pe.wait_ge(s_ki, 16)
                    for k in range(KD):
                        m = pe.matmul(PS[0:HD + IH, 4, :], WKI[:, k, :], XT[:, k, :], start=(k == 0),
                                      stop=(k == KD - 1))
                    m.then_inc(s_key, 1)
                    pe.wait_ge(s_cw, 16)
                    queries(0)
                    pe.wait_ge(s_wtc, 1)
                    for t in range(T):
                        m = pe.transpose(PS[:, 5, t * IH:(t + 1) * IH], WIT[:, t * P:(t + 1) * P],
                                         ident[HD:HD + IH, HD:HD + IH])
                    m.then_inc(s_wi, 1)
                    queries(1)
                    pe.wait_ge(s_keyc, 2)
                    pe.wait_ge(s_half, 2)
                    scores(0)
                    queries(2)
                    scores(1)
                    queries(3)
                    scores(2)
                    scores(3)
                    for t in range(T):
                        for k in range(KD):
                            m = pe.matmul(PS[:, t, :], XT[:, k, t * P:(t + 1) * P], CW[:, k, 0:NB],
                                          start=(k == 0), stop=(k == KD - 1))
                        m.then_inc(s_full, 1)
                    pe.wait_ge(s_wic, 1)
                    pe.wait_ge(s_relu, len(units))
                    for t in range(T):
                        pe.wait_ge(s_cq, 2 * t + 2)
                        for c in range(4):
                            m = pe.transpose(PS[:, 4 + c, t * P:(t + 1) * P], CQ[:, t, c * P:(c + 1) * P],
                                             ident[:, :])
                            if t == T - 1:
                                m.then_inc(s_ct, 1)
                    pe.wait_ge(s_ctc, 4)
                    pe.wait_ge(s_up, 32)
                    for j in range(24):
                        if j >= 8:
                            up.wait_emptied(pe, j - 8)
                        if j == 16:
                            pe.wait_ge(s_uv, 16)
                        for k in range(2):
                            if j < 8:
                                lhsT, rhs = UQ[:, k, j * P:(j + 1) * P], CT[:, k, :]
                            elif j < 16:
                                lhsT, rhs = UK[:, k, (j - 8) * P:(j - 7) * P], CT[:, 2 + k, :]
                            else:
                                t, c = (j - 16) // 2, j % 2
                                lhsT, rhs = CT[:, 2 + k, t * P:(t + 1) * P], UV[:, k, c * NB:(c + 1) * NB]
                            m = pe.matmul(PS[:, j % 8, :], lhsT, rhs, start=(k == 0), stop=(k == 1))
                        m.then_inc(up.full, 1)

                @block.scalar
                def _(act):
                    def copy_queries(c):
                        act.wait_ge(s_qi, c + 1)
                        act.activation(QI[:, c, :], PS[:, c, :], ACT.Copy).then_inc(s_qic, 1)

                    def rectify(c):
                        for i in range(per_chunk * c, per_chunk * (c + 1)):
                            t, h = units[i]
                            act.wait_ge(s_is, i + 1)
                            if i >= 2:
                                act.wait_ge(s_acc, i - 1)
                            act.activation(relu[i % 2][:, 0:width[t]], PS[:, 6 + i % 2, 0:width[t]], ACT.Relu)\
                               .then_inc(s_relu, 1)

                    act.wait_ge(s_key, 1)
                    for u in range(2):
                        act.activation(KI[u * HD:(u + 1) * HD, u, :], PS[0:HD, 4, :], ACT.Copy)\
                           .then_inc(s_keyc, 1)
                    act.activation(WIT, PS[HD:HD + IH, 4, :], ACT.Copy).then_inc(s_wtc, 1)
                    copy_queries(0)
                    act.wait_ge(s_wi, 1)
                    act.activation(WI, three(PS[:, 5, 0:T * IH], IH), ACT.Copy).then_inc(s_wic, 1)
                    copy_queries(1)
                    rectify(0)
                    copy_queries(2)
                    rectify(1)
                    copy_queries(3)
                    rectify(2)
                    rectify(3)
                    for t in range(T):
                        ts = slice(2 * t, 2 * t + 2)
                        inv = slice(8 + 2 * t, 10 + 2 * t)
                        act.wait_ge(s_full, t + 1)
                        for u in range(2):
                            i = 2 * t + u
                            if i >= 1:
                                act.wait_ge(s_sq, i)
                            act.activation(squares, PS[:, t, u * RANK:(u + 1) * RANK], ACT.Square,
                                           accum_out=sq[:, i:i + 1]).then_inc(s_sq, 1)
                        act.wait_ge(s_sq, 2 * t + 2)
                        act.activation(sq[:, inv], sq[:, ts], ACT.Sqrt, bias=eps[:, 1:2], scale=1.0 / RANK)\
                           .then_inc(s_rms, 1)
                        act.wait_ge(s_inv, t + 1)
                        for u in range(2):
                            act.activation(CQ[:, t, u * RANK:(u + 1) * RANK], PS[:, t, u * RANK:(u + 1) * RANK],
                                           ACT.Copy, scale=sq[:, 8 + 2 * t + u:9 + 2 * t + u]).then_inc(s_cq, 1)
                    act.wait_ge(s_cgain, 32)
                    for c in range(4):
                        act.wait_ge(s_ct, c + 1)
                        act.activation(CT[:, c, :], PS[:, 4 + c, :], ACT.Copy, scale=gains[:, 8 + c:9 + c])\
                           .then_inc(s_ctc, 1)
                    for j in range(24):
                        up.wait_full(act, j)
                        src = PS[:, j % 8, :]
                        if j < 8:
                            act.activation(QH[0:HD, 0, j, :], src[0:HD, :], ACT.Copy, scale=HD ** -0.5)
                            act.activation(QH[HD:P, 1, j, :], src[HD:P, :], ACT.Copy, scale=HD ** -0.5)\
                               .then_inc(up.sem_of(0), 1)
                        elif j < 16:
                            act.activation(KH[:, j - 8, :], src, ACT.Copy).then_inc(up.sem_of(0), 1)
                        else:
                            t, c = (j - 16) // 2, j % 2
                            act.activation(VH[:, t, c * NB:(c + 1) * NB], src, ACT.Copy).then_inc(up.sem_of(0), 1)

                @block.vector
                def _(dve):
                    own = Own(dve, f"{n}_own")
                    dve.wait_ge(s_wic, 1)
                    for i, (t, h) in enumerate(units):
                        dve.wait_ge(s_relu, i + 1)
                        r, w = relu[i % 2][:, 0:width[t]], WI[:, t, h:h + 1]
                        if h == 0:
                            dve.tensor_scalar(IS[t], r, w, None, ALU.mult).then_inc(s_acc, 1)
                        else:
                            dve.wait_ge(s_acc, i - len(SEL) + 1)
                            dve.scalar_tensor_tensor(IS[t], r, w, IS[t], ALU.mult, ALU.add).then_inc(s_acc, 1)
                    dve.wait_ge(s_dist, 16)
                    dve.wait_ge(s_mask, len(SEL))
                    inverse_after = [TOPK // 64 * (t + 1) for t in range(T)]
                    last = {}

                    def step(t, ins):
                        own.mark(ins)
                        last[t] = own.n

                    for r in range(TOPK // 8):
                        cur = IS if r == 0 else WK
                        for t in SEL:
                            if r > 0:
                                dve.wait_ge(own.sem, last[t])
                            step(t, dve.max(m8[t], cur[t]))
                        for t in SEL:
                            dve.wait_ge(own.sem, last[t])
                            step(t, dve.match_replace(WK[t], m8[t], cur[t], LOWEST))
                        if r in inverse_after:
                            t = inverse_after.index(r)
                            inv = sq[:, 8 + 2 * t:10 + 2 * t]
                            dve.wait_ge(s_rms, t + 1)
                            dve.reciprocal(inv, inv).then_inc(s_inv, 1)
                    for t in SEL:
                        dve.wait_ge(own.sem, last[t])
                        step(t, dve.tensor_tensor(IS[t], IS[t], WK[t], ALU.is_equal))
                    for t in SEL:
                        dve.wait_ge(own.sem, last[t])
                        own.mark(dve.scalar_tensor_tensor(IS[t], IS[t], BIG, DIST[:, SEQ - width[t]:SEQ],
                                                          ALU.mult, ALU.add))
                    own.wait()

                @block.gpsimd
                def _(pool):
                    pool.memset(KI[HD:P, 0, :], 0.0).then_inc(s_half, 1)
                    pool.wait_ge(s_half, 1)
                    pool.memset(KI[0:HD, 1, :], 0.0).then_inc(s_half, 1)
                    pool.wait_ge(s_half, 2)
                    for n_, t in enumerate(SEL):
                        pool.wait_ge(s_acc, len(units) - len(SEL) + n_ + 1)
                        d = IS[t][:, t * P:(t + 1) * P]
                        pool.affine_select(out=d, in_=d, compare_op=ALU.is_ge, fill=LOWEST, base=0,
                                           pattern=[[-1, P]], channel_multiplier=1).then_inc(s_mask, 1)
                        pool.wait_ge(s_mask, n_ + 1)
                    pool.wait_ge(s_full, T)
                    pool.memset(QH[HD:P, 0, :, :], 0.0).then_inc(s_half, 1)
                    pool.wait_ge(s_half, 3)
                    pool.memset(QH[0:HD, 1, :, :], 0.0).then_inc(s_half, 1)
                    pool.wait_ge(s_half, 4)
            Stages.end()

        DMASK = {t: IS[t] for t in SEL}
        DMASK[0] = DIST[:, SEQ - P:SEQ]
        LGS = 8
        LG = [w3[:, 1536 + b * NB:2048 + b * NB] for b in range(5)] + [w1[:, b * NB:(b + 1) * NB] for b in range(3)]
        PTS = [w2[:, b * NB:(b + 1) * NB] for b in range(4)]
        nmax = w2[:, 2048:2112]
        rsum = w2[:, 2112:2176]
        rden = w2[:, 2176:2240]
        MC = three(slim[1][:, :], SEQ)

        def attention():
            n = "att"
            units = [(t, h) for t in range(T) for h in range(AH)]
            N = len(units)
            LAG_R, LAG_T, LAG_V = 1, 4, 6
            s_s, s_l, s_max, s_p = sem(f"{n}_s"), sem(f"{n}_l"), sem(f"{n}_max"), sem(f"{n}_p")
            s_r, s_n = sem(f"{n}_r"), [sem(f"{n}_n_{e}") for e in ("pool", "dve")]
            s_pt, s_ptc, s_pv = sem(f"{n}_pt"), sem(f"{n}_ptc"), sem(f"{n}_pv")
            s_o = [sem(f"{n}_o_{e}") for e in ("act", "dve")]
            slope = [2.0 ** (-8.0 * (h + 1) / AH) for h in range(AH)]

            def finish(eng, copy, half, t):
                eng.wait_ge(s_pv, AH // 2 * (t + 1))
                copy(MC[:, 4 * half:4 * half + 4, t * P:(t + 1) * P], three(PS[:, 4 + 2 * (t % 2) + half, :], P))\
                    .then_inc(s_o[half], 1)

            with nc.Block() as block:
                @block.tensor
                def _(pe):
                    for i in range(0, N + LAG_V, 2):
                        for j in (i, i + 1):
                            if j < N:
                                t, h = units[j]
                                if j >= 2:
                                    pe.wait_ge(s_l, j - 1)
                                pe.matmul(PS[:, j % 2, 0:width[t]], QH[:, h % 2, h // 2, t * P:(t + 1) * P],
                                          KH[:, h // 2, 0:width[t]], start=True, stop=True).then_inc(s_s, 1)
                            j -= LAG_T
                            if 0 <= j < N:
                                t, h = units[j]
                                pe.wait_ge(s_n[j % 2], j // 2 + 1)
                                if j >= 2:
                                    pe.wait_ge(s_ptc, j - 1)
                                for kb in range(t + 1):
                                    m = pe.transpose(PS[:, 2 + j % 2, kb * P:(kb + 1) * P],
                                                     LG[j % LGS][:, kb * P:(kb + 1) * P], ident[:, :])
                                m.then_inc(s_pt, 1)
                        j = i - LAG_V
                        if j >= 0:
                            t, h = units[j]
                            pe.wait_ge(s_ptc, j + 2)
                            if t >= 2 and h == 0:
                                for s in s_o:
                                    pe.wait_ge(s, t - 1)
                            for kb in range(t + 1):
                                for u in range(2):
                                    m = pe.matmul(PS[u * HD:(u + 1) * HD, 4 + 2 * (t % 2) + h // 8,
                                                     (h // 2 % 4) * P:(h // 2 % 4 + 1) * P],
                                                  VH[:, kb, (h + u) * HD:(h + u + 1) * HD],
                                                  PTS[(j + u) % 4][:, kb * P:(kb + 1) * P],
                                                  start=(kb == 0), stop=(kb == t))
                            m.then_inc(s_pv, 1)

                @block.vector
                def _(dve):
                    def invert(i):
                        dve.wait_ge(s_p, i + 1)
                        dve.reciprocal(rden[:, i:i + 1], rsum[:, i:i + 1]).then_inc(s_r, 1)

                    def divide(i):
                        if i % 2 == 1:
                            dve.wait_ge(s_r, i + 1)
                            g = LG[i % LGS][:, 0:width[units[i][0]]]
                            dve.tensor_scalar(g, g, rden[:, i:i + 1], None, ALU.mult).then_inc(s_n[1], 1)

                    for i, (t, h) in enumerate(units):
                        dve.wait_ge(s_s, i + 1)
                        if i >= LGS:
                            dve.wait_ge(s_pt, i - LGS + 1)
                        g = LG[i % LGS][:, 0:width[t]]
                        dve.scalar_tensor_tensor(g, DMASK[t], -slope[h], PS[:, i % 2, 0:width[t]],
                                                 ALU.mult, ALU.add).then_inc(s_l, 1)
                        dve.wait_ge(s_l, i + 1)
                        dve.tensor_reduce(nmax[:, i:i + 1], g, AX.X, ALU.max, negate=True).then_inc(s_max, 1)
                        if i >= LAG_R:
                            invert(i - LAG_R)
                        if i > LAG_R:
                            divide(i - LAG_R - 1)
                        if h == 10 and t >= 1:
                            finish(dve, dve.tensor_copy, 1, t - 1)
                    for i in range(N - LAG_R, N):
                        divide(i - 1)
                        invert(i)
                    divide(N - 1)
                    finish(dve, dve.tensor_copy, 1, T - 1)

                @block.scalar
                def _(act):
                    for i in range(N + LAG_T):
                        if i < N:
                            t, h = units[i]
                            act.wait_ge(s_max, i + 1)
                            g = LG[i % LGS][:, 0:width[t]]
                            act.activation(g, g, ACT.Exp, bias=nmax[:, i:i + 1],
                                           accum_out=rsum[:, i:i + 1]).then_inc(s_p, 1)
                        j = i - LAG_T
                        if j >= 0:
                            t, h = units[j]
                            act.wait_ge(s_pt, j + 1)
                            if j >= 4:
                                act.wait_ge(s_pv, (j - 4) // 2 + 1)
                            act.activation(PTS[j % 4][:, 0:width[t]], PS[:, 2 + j % 2, 0:width[t]],
                                           ACT.Copy).then_inc(s_ptc, 1)
                            if h == 8 and t >= 1:
                                finish(act, lambda o, a: act.activation(o, a, ACT.Copy), 0, t - 1)
                    finish(act, lambda o, a: act.activation(o, a, ACT.Copy), 0, T - 1)

                @block.gpsimd
                def _(pool):
                    for i in range(0, N, 2):
                        pool.wait_ge(s_r, i + 1)
                        g = LG[i % LGS][:, 0:width[units[i][0]]]
                        pool.tensor_scalar(g, g, rden[:, i:i + 1], None, ALU.mult).then_inc(s_n[0], 1)
                        pool.wait_ge(s_n[0], i // 2 + 1)
            Stages.end()

        s_wg = [[lasting(f"s_wg{l}{c}") for c in range(2)] for l in range(2)]
        s_wp = [lasting(f"s_wp{l}") for l in range(2)]
        s_out = lasting("s_out")

        def before_out(l):
            def load_first(sp):
                if l == 1:
                    load_gu(sp, 1, 0, 0)
                    load_dn(sp, 1, 0, 0)
                load_last_gu(sp, l)
            return load_first

        def after_out(l):
            def then_load(sp, sums):
                sums.wait_full(sp, 7)
                load_gu(sp, l, 1, 1)
                load_dn(sp, l, 1, 1)
            return then_load

        def layer_end(l, loads, after_tile, turn_after):
            route(l)
            experts(l, lambda sp: load_injection(sp, l, s_wp[l]))
            injection(l, s_wg[l], s_wp[l], loads, after_tile, turn_after)

        def next_layer_loads(sp, norm):
            load_latent_weights(sp)
            sp.wait_ge(norm.done, T)
            load_indexer_weights(sp)
            load_ln(sp, A["ln1_g"][1], A["ln1_b"][1], s_ln)

        def store_tiles(sp, s_done):
            for t in range(T):
                sp.wait_ge(s_done, 2 * t + 2)
                sp.dma_start(out[0, t * P:(t + 1) * P, :], X[:, t, :]).then_inc(s_out, 16)
            sp.wait_ge(s_out, 16 * T)

        out_projection(0, MT, w_out0, s_wout, before_out(0), after_out(0))
        layer_end(0, next_layer_loads, lambda sp, s_done: None, True)
        latents()
        attention()
        WO = three(wide[0][:, :], D)
        out_projection(1, MC, [WO[:, :, 0:NB], WO[:, :, NB:D]], [s_cwout], before_out(1), after_out(1))
        layer_end(1, lambda sp, norm: None, store_tiles, False)


_INS = ['x', 'p', 'ab_w_in', 'ret_gn_g', 'pool_w', 'pool_scale', 'ab_w_out', 'c_w_in', 'c_q_norm', 'c_kv_norm',
        'c_w_uq', 'c_w_uk', 'c_w_uv', 'c_w_out', 'ln1_g', 'ln1_b', 'ln2_g', 'ln2_b', 'moe_w_group', 'moe_b_group',
        'moe_w_expert', 'moe_b_expert', 'moe_w_gu', 'moe_w_down', 'ple_w_gate', 'ple_w_proj']


def constants(np):
    f = np.float32
    p = np.arange(P)
    j = np.arange(SEQ)
    c = {"c_ident": np.eye(P), "c_tri": (p[:, None] < p[None, :]), "c_iota": np.tile(np.arange(NE), (P, 1)),
         "c_half": np.stack([p // SLOTS, p // SLOTS + 2 * NOWHERE], axis=1),
         "c_slot": np.tile(p % SLOTS, (P, 1)), "c_tok": np.arange(T)[None, :] * P + p[:, None],
         "c_eps": np.tile([LN_EPS, RMS_EPS], (P, 1))}
    diff = j[None, :] - p[:, None]
    gamma = 1.0 - 2.0 ** (-5.0 - np.arange(RH))
    c["c_decay"] = np.where(diff[None] >= 0, gamma[:, None, None] ** np.maximum(diff, 0)[None] * P ** -0.5, 0.0)
    c["c_edge"] = np.array([[w / min(t + 1, w) for t in range(WMAX)] for w in WINDOWS])
    c["c_empty"] = np.tile([NOWHERE, NOWHERE, 0.0, 0.0], (P, NB // 4))
    e, b = np.meshgrid(np.arange(NE), np.arange(1, 8), indexing="ij")
    c["c_more"] = np.stack([(NE * TABLE - (TABLE * e + SLOTS * b)).ravel(), (SLOTS * b).ravel()])
    dist = (SEQ - P) + p[:, None] - j[None, :]
    c["c_dist"] = np.where(dist >= 0, dist, BIG)
    return {k: np.ascontiguousarray(v.astype(f)) for k, v in c.items()}


def kernel(**inputs):
    import numpy as _np
    import concourse.bacc as _bacc
    from concourse import mybir as _mybir
    from concourse.bass_utils import run_bass_kernel_spmd as _run

    nc = _bacc.Bacc("TRN2", target_bir_lowering=False, num_devices=1)
    arrays, args = {}, {}
    given = {name: _np.ascontiguousarray(inputs[name]) for name in _INS}
    given.update(constants(_np))
    for name, a in given.items():
        arrays[f"in_{name}"] = a
        args[name] = nc.dram_tensor(f"in_{name}", a.shape, _mybir.dt.from_np(a.dtype), kind="ExternalInput").ap()
    out = nc.dram_tensor("out", (1, SEQ, D), _mybir.dt.float32, kind="ExternalOutput").ap()
    build(nc, args, out)
    r = _run(nc, [arrays], core_ids=[0])
    return r.results[0]["out"]
```
